# Optimizing a Trainium2 kernel written in Bass

```python
import math
import jax, jax.numpy as jnp
from jax import lax
import numpy as np

D_MODEL = 1024
BATCH = 1
SEQ = 256
DEPTH = 2

CTX_LEN = 256
GRID_W = 64
N_MIXERS = 2
N_LAYERS_A = (DEPTH + 1) // 2
N_LAYERS_B = DEPTH // 2
BRANCH_WIDTH = D_MODEL
DA_HEAD_DIM = 64
DA_HEADS = BRANCH_WIDTH // (2 * DA_HEAD_DIM)
DA_QK_WIDTH = DA_HEADS * 2 * DA_HEAD_DIM
DA_IN_WIDTH = 2 * DA_QK_WIDTH + 2 * BRANCH_WIDTH
GQ_HEAD_DIM = 128
GQ_HEADS = BRANCH_WIDTH // GQ_HEAD_DIM
GQ_KV_HEADS = 2
GQ_Q_WIDTH = GQ_HEADS * GQ_HEAD_DIM
GQ_KV_WIDTH = GQ_KV_HEADS * GQ_HEAD_DIM
GQ_IN_WIDTH = GQ_Q_WIDTH + 2 * GQ_KV_WIDTH + BRANCH_WIDTH
ROPE_THETA = 10000.0
Q_BLOCK = 128
NORM_EPS = 1e-6


def rms_norm(x, g):
    xf = x.astype(jnp.float32)
    y = xf * lax.rsqrt(jnp.mean(xf * xf, axis=-1, keepdims=True) + NORM_EPS)
    return (y * g.astype(jnp.float32)).astype(x.dtype)

def adaln(cvec, w, b):
    m = jax.nn.silu(cvec) @ w + b
    return jnp.split(m, 3, axis=-1)

def axial_rope_tables(rows, cols, head_dim):
    axis_dim = head_dim // 2
    freqs = ROPE_THETA ** (-jnp.arange(0, axis_dim, 2, dtype=jnp.float32) / axis_dim)
    ang = jnp.concatenate([rows.astype(jnp.float32)[:, None] * freqs,
                           cols.astype(jnp.float32)[:, None] * freqs], axis=-1)
    return jnp.cos(ang), jnp.sin(ang)

def apply_rope(x, cos, sin):
    S, half = cos.shape
    shp = (1, S) + (1,) * (x.ndim - 3) + (half,)
    cs = cos.reshape(shp).astype(x.dtype)
    sn = sin.reshape(shp).astype(x.dtype)
    x1, x2 = jnp.split(x, 2, axis=-1)
    return jnp.concatenate([x1 * cs - x2 * sn, x2 * cs + x1 * sn], axis=-1)

def sweep_attention(q, k, v):
    B, Sq, Hq, Dh = q.shape
    Hkv = k.shape[2]
    G = Hq // Hkv
    Dv = v.shape[-1]
    scale = Dh ** -0.5
    k32 = k.astype(jnp.float32)
    qb = q.reshape(B, Sq // Q_BLOCK, Q_BLOCK, Hkv, G, Dh).transpose(1, 0, 2, 3, 4, 5)

    def one_block(qblk):
        s = jnp.einsum('bqhgd,bkhd->bhgqk', qblk.astype(jnp.float32), k32) * scale
        p = jax.nn.softmax(s, axis=-1)
        return jnp.einsum('bhgqk,bkhd->bqhgd', p.astype(v.dtype), v)

    out = lax.map(one_block, qb)
    return out.transpose(1, 0, 2, 3, 4, 5).reshape(B, Sq, Hq, Dv)

def lambda_init_fn(layer_idx):
    return 0.8 - 0.6 * math.exp(-0.3 * layer_idx)

def diff_attention_mixer(h, hc, w_in, w_out, lam_p, subln_g, lam_init, cos, sin, with_ctx_out):
    B, S, _ = h.shape

    def project(t):
        L = t.shape[1]
        p = t @ w_in
        q, k, v, z = jnp.split(p, [DA_QK_WIDTH, 2 * DA_QK_WIDTH, 2 * DA_QK_WIDTH + BRANCH_WIDTH], axis=-1)
        q = q.reshape(B, L, DA_HEADS, 2, DA_HEAD_DIM)
        k = k.reshape(B, L, DA_HEADS, 2, DA_HEAD_DIM)
        v = v.reshape(B, L, DA_HEADS, 2 * DA_HEAD_DIM)
        return q, k, v, z

    q, k, v, z = project(h)
    qc, kc, vc, zc = project(hc)
    q = apply_rope(q, cos, sin)
    k = apply_rope(k, cos, sin)
    k_all = jnp.concatenate([k, kc], axis=1)
    v_all = jnp.concatenate([v, vc], axis=1)

    lp = lam_p.astype(jnp.float32)
    lam = jnp.exp(jnp.sum(lp[0] * lp[1])) - jnp.exp(jnp.sum(lp[2] * lp[3])) + lam_init

    def diff(qq, kk, vv, gate):
        o1 = sweep_attention(qq[..., 0, :], kk[..., 0, :], vv)
        o2 = sweep_attention(qq[..., 1, :], kk[..., 1, :], vv)
        o = o1 - lam.astype(o1.dtype) * o2
        o = rms_norm(o, subln_g) * (1.0 - lam_init)
        o = o.reshape(o.shape[0], o.shape[1], BRANCH_WIDTH)
        return (o * jax.nn.silu(gate)) @ w_out

    y = diff(q, k_all, v_all, z)
    yc = diff(qc, kc, vc, zc) if with_ctx_out else None
    return y, yc

def gqa_mixer(h, hc, w_in, w_out, qk_g, cos, sin, with_ctx_out):
    B, S, _ = h.shape

    def project(t):
        L = t.shape[1]
        p = t @ w_in
        q, k, v, z = jnp.split(p, [GQ_Q_WIDTH, GQ_Q_WIDTH + GQ_KV_WIDTH, GQ_Q_WIDTH + 2 * GQ_KV_WIDTH], axis=-1)
        q = rms_norm(q.reshape(B, L, GQ_HEADS, GQ_HEAD_DIM), qk_g[0])
        k = rms_norm(k.reshape(B, L, GQ_KV_HEADS, GQ_HEAD_DIM), qk_g[1])
        v = v.reshape(B, L, GQ_KV_HEADS, GQ_HEAD_DIM)
        return q, k, v, z

    q, k, v, z = project(h)
    qc, kc, vc, zc = project(hc)
    q = apply_rope(q, cos, sin)
    k = apply_rope(k, cos, sin)
    k_all = jnp.concatenate([k, kc], axis=1)
    v_all = jnp.concatenate([v, vc], axis=1)

    def attend(qq, kk, vv, gate):
        o = sweep_attention(qq, kk, vv)
        o = o.reshape(o.shape[0], o.shape[1], BRANCH_WIDTH)
        return (o * jax.nn.silu(gate)) @ w_out

    y = attend(q, k_all, v_all, z)
    yc = attend(qc, kc, vc, zc) if with_ctx_out else None
    return y, yc

def first_inputs(seed: int = 0) -> dict:
    key = jax.random.key(seed)
    ks = jax.random.split(key, 16)
    f32 = jnp.float32
    D = D_MODEL
    s_in = D ** -0.5
    return {
        "x": jax.random.normal(ks[0], (BATCH, SEQ, D), f32),
        "c": jax.random.normal(ks[1], (BATCH, D), f32),
        "ctx": jax.random.normal(ks[2], (BATCH, CTX_LEN, D), f32),
        "c_ctx": jax.random.normal(ks[3], (D,), f32),
        "ada_w": jax.random.normal(ks[4], (DEPTH, D, 3 * D), f32) * (0.5 * s_in),
        "ada_b": jax.random.normal(ks[5], (DEPTH, 3 * D), f32) * 0.01,
        "pre_g": 1.0 + 0.05 * jax.random.normal(ks[6], (DEPTH, D), f32),
        "post_g": 1.0 + 0.05 * jax.random.normal(ks[7], (DEPTH, D), f32),
        "w_out": jax.random.normal(ks[8], (DEPTH, BRANCH_WIDTH, D), f32) * (BRANCH_WIDTH ** -0.5),
        "a_w_in": jax.random.normal(ks[9], (N_LAYERS_A, D, DA_IN_WIDTH), f32) * s_in,
        "a_lambda": jax.random.normal(ks[10], (N_LAYERS_A, 4, DA_HEAD_DIM), f32) * 0.1,
        "a_subln_g": 1.0 + 0.05 * jax.random.normal(ks[11], (N_LAYERS_A, 2 * DA_HEAD_DIM), f32),
        "b_w_in": jax.random.normal(ks[12], (N_LAYERS_B, D, GQ_IN_WIDTH), f32) * s_in,
        "b_qk_g": 1.0 + 0.05 * jax.random.normal(ks[13], (N_LAYERS_B, 2, GQ_HEAD_DIM), f32),
    }

def first_block(x, c, ctx, c_ctx, ada_w, ada_b, pre_g, post_g, w_out, a_w_in, a_lambda, a_subln_g, b_w_in, b_qk_g):
    n_tokens = x.shape[1]
    n_rows = n_tokens // GRID_W
    rows = jnp.repeat(jnp.arange(n_rows, dtype=jnp.int32), GRID_W)
    cols = jnp.tile(jnp.arange(GRID_W, dtype=jnp.int32), n_rows)
    cos_a, sin_a = axial_rope_tables(rows, cols, DA_HEAD_DIM)
    cos_b, sin_b = axial_rope_tables(rows, cols, GQ_HEAD_DIM)

    xc = ctx
    for i in range(DEPTH):
        last = i == DEPTH - 1
        shift, scale, gate = adaln(c, ada_w[i], ada_b[i])
        shift, scale, gate = shift[:, None, :], scale[:, None, :], gate[:, None, :]
        cshift, cscale, cgate = adaln(c_ctx, ada_w[i], ada_b[i])
        h = rms_norm(x, pre_g[i]) * (1.0 + scale) + shift
        hc = rms_norm(xc, pre_g[i]) * (1.0 + cscale) + cshift
        j = i // N_MIXERS
        if i % N_MIXERS == 0:
            y, yc = diff_attention_mixer(h, hc, a_w_in[j], w_out[i], a_lambda[j], a_subln_g[j],
                                         lambda_init_fn(i), cos_a, sin_a, not last)
        else:
            y, yc = gqa_mixer(h, hc, b_w_in[j], w_out[i], b_qk_g[j], cos_b, sin_b, not last)
        x = x + gate * rms_norm(y, post_g[i])
        if not last:
            xc = xc + cgate * rms_norm(yc, post_g[i])
    return x


DEPTH_2 = 1

CHUNK = 64
HEAD_DIM = 64
MIX_WIDTH = D_MODEL
A_WIDTH = MIX_WIDTH // 2
B_WIDTH = MIX_WIDTH - A_WIDTH
A_HEADS = A_WIDTH // HEAD_DIM
B_HEADS = B_WIDTH // HEAD_DIM
KV_LATENT = 128
IDX_HEADS = 4
IDX_DIM = 32
TOPK_MAX = 256
NUM_BUCKETS = 32
MAX_DISTANCE = 128
ROPE_BASE = 10000.0
RMS_EPS = 1e-6
GN_EPS = 1e-5
FFN_HIDDEN = ((-(-(8 * D_MODEL) // 3) + 255) // 256) * 256

IN_SIZES = [A_WIDTH, KV_LATENT, IDX_HEADS * IDX_DIM, IDX_DIM, IDX_HEADS,
            B_WIDTH, B_WIDTH, B_WIDTH, B_WIDTH]
IN_WIDTH = sum(IN_SIZES)
IN_OFFSETS = [int(o) for o in np.cumsum(IN_SIZES)[:-1]]


def rmsnorm(x, w):
    xf = x.astype(jnp.float32)
    y = xf * lax.rsqrt(jnp.mean(xf * xf, axis=-1, keepdims=True) + RMS_EPS)
    return (y * w.astype(jnp.float32)).astype(x.dtype)

def t5_bucket(rel):
    half = NUM_BUCKETS // 2
    max_exact = half // 2
    ret = jnp.where(rel > 0, half, 0)
    n = jnp.abs(rel)
    nf = jnp.maximum(n, 1).astype(jnp.float32)
    large = max_exact + (jnp.log(nf / max_exact) / math.log(MAX_DISTANCE / max_exact)
                         * (half - max_exact)).astype(jnp.int32)
    large = jnp.minimum(large, half - 1)
    return ret + jnp.where(n < max_exact, n, large)

def rotary(x, pos):
    half = x.shape[-1] // 2
    inv = ROPE_BASE ** (-jnp.arange(half, dtype=jnp.float32) / half)
    ang = pos.astype(jnp.float32)[:, None] * inv[None, :]
    cos = jnp.cos(ang)[:, None, :]
    sin = jnp.sin(ang)[:, None, :]
    x1, x2 = x[..., :half], x[..., half:]
    return jnp.concatenate([x1 * cos - x2 * sin, x1 * sin + x2 * cos], axis=-1)

def indexed_sparse_attention(q, k, v, iq, ik, iw, rel_bias):
    b, s, h, dh = q.shape
    topk = min(TOPK_MAX, s // 4)
    n_blocks = s // Q_BLOCK
    key_pos = jnp.arange(s)
    idx_scale = IDX_DIM ** -0.5
    w_scale = IDX_HEADS ** -0.5

    def block(i):
        t0 = i * Q_BLOCK
        qb = lax.dynamic_slice_in_dim(q, t0, Q_BLOCK, axis=1)
        iqb = lax.dynamic_slice_in_dim(iq, t0, Q_BLOCK, axis=1)
        iwb = lax.dynamic_slice_in_dim(iw, t0, Q_BLOCK, axis=1)
        qpos = t0 + jnp.arange(Q_BLOCK)
        limit = (qpos // CHUNK + 1) * CHUNK
        admissible = key_pos[None, :] < limit[:, None]
        dots = jnp.einsum('bthd,bsd->bths', iqb, ik).astype(jnp.float32) * idx_scale
        score = jnp.einsum('bth,bths->bts', iwb.astype(jnp.float32) * w_scale,
                           jax.nn.relu(dots))
        score = jnp.where(admissible[None], score, -jnp.inf)
        _, idx = lax.top_k(score, topk)
        valid = idx < limit[None, :, None]
        kg = jax.vmap(lambda kb, ib: kb[ib])(k, idx)
        vg = jax.vmap(lambda vb, ib: vb[ib])(v, idx)
        logits = jnp.einsum('bthd,btkd->bhtk', qb, kg).astype(jnp.float32) * dh ** -0.5
        bias = rel_bias[t5_bucket(idx - qpos[None, :, None])]
        logits = logits + jnp.transpose(bias, (0, 3, 1, 2)).astype(jnp.float32)
        logits = jnp.where(valid[:, None], logits, -jnp.inf)
        p = jax.nn.softmax(logits, axis=-1)
        return jnp.einsum('bhtk,btkd->bthd', p.astype(v.dtype), vg)

    outs = lax.map(block, jnp.arange(n_blocks))
    return jnp.moveaxis(outs, 0, 1).reshape(b, s, h * dh)

def chunkwise_retention(q, k, v):
    b, s, h, dh = q.shape
    nc = s // CHUNK
    log_g = jnp.log1p(-(2.0 ** (-5.0 - jnp.arange(h, dtype=jnp.float32))))
    j = jnp.arange(CHUNK, dtype=jnp.float32)
    rel = j[:, None] - j[None, :]
    inner_decay = jnp.where(rel[None] >= 0,
                            jnp.exp(jnp.maximum(rel, 0.0)[None] * log_g[:, None, None]), 0.0)
    query_decay = jnp.exp((j + 1.0)[:, None] * log_g[None, :])[None, :, :, None]
    key_decay = jnp.exp((CHUNK - 1.0 - j)[:, None] * log_g[None, :])[None, :, :, None]
    chunk_decay = jnp.exp(CHUNK * log_g)[None, :, None, None]

    def to_chunks(t):
        return jnp.transpose(t.reshape(b, nc, CHUNK, h, dh), (1, 0, 2, 3, 4))

    def step(state, xs):
        qc, kc, vc = xs
        scores = jnp.einsum('bihd,bjhd->bhij', qc, kc) * inner_decay[None]
        inner = jnp.einsum('bhij,bjhd->bihd', scores, vc)
        cross = jnp.einsum('bihd,bhde->bihe', qc, state) * query_decay
        new_state = state * chunk_decay + jnp.einsum('bjhd,bjhe->bhde', kc * key_decay, vc)
        return new_state, inner + cross

    state0 = jnp.zeros((b, h, dh, dh), jnp.float32)
    _, ys = lax.scan(step, state0, (to_chunks(q), to_chunks(k), to_chunks(v)))
    return jnp.transpose(ys, (1, 0, 2, 3, 4)).reshape(b, s, h, dh)

def second_inputs(seed: int = 0) -> dict:
    key = jax.random.key(seed)
    ks = jax.random.split(key, 20)
    f32 = jnp.float32

    def nrm(k, shape, fan_in):
        return jax.random.normal(k, shape, f32) * fan_in ** -0.5

    def gain(k, shape):
        return 1.0 + 0.02 * jax.random.normal(k, shape, f32)

    return {
        "x": jax.random.normal(ks[0], (BATCH, SEQ, D_MODEL), f32),
        "norm1_w": gain(ks[1], (DEPTH_2, D_MODEL)),
        "w_in": nrm(ks[2], (DEPTH_2, D_MODEL, IN_WIDTH), D_MODEL),
        "q_norm_w": gain(ks[3], (DEPTH_2, HEAD_DIM)),
        "k_norm_w": gain(ks[4], (DEPTH_2, HEAD_DIM)),
        "kv_norm_w": gain(ks[5], (DEPTH_2, KV_LATENT)),
        "w_uk": nrm(ks[6], (DEPTH_2, KV_LATENT, HEAD_DIM), KV_LATENT),
        "w_uv": nrm(ks[7], (DEPTH_2, KV_LATENT, HEAD_DIM), KV_LATENT),
        "rel_bias": 0.1 * jax.random.normal(ks[8], (NUM_BUCKETS, A_HEADS), f32),
        "ret_gn_w": gain(ks[9], (DEPTH_2, B_WIDTH)),
        "ret_gn_b": 0.02 * jax.random.normal(ks[10], (DEPTH_2, B_WIDTH), f32),
        "w_out": nrm(ks[11], (DEPTH_2, MIX_WIDTH, D_MODEL), MIX_WIDTH),
        "norm2_w": gain(ks[12], (DEPTH_2, D_MODEL)),
        "w_gate": nrm(ks[13], (DEPTH_2, D_MODEL, FFN_HIDDEN), D_MODEL),
        "w_up": nrm(ks[14], (DEPTH_2, D_MODEL, FFN_HIDDEN), D_MODEL),
        "w_down": nrm(ks[15], (DEPTH_2, FFN_HIDDEN, D_MODEL), FFN_HIDDEN),
    }

def second_block(x, norm1_w, w_in, q_norm_w, k_norm_w, kv_norm_w, w_uk, w_uv, rel_bias,
              ret_gn_w, ret_gn_b, w_out, norm2_w, w_gate, w_up, w_down):
    b, s, _ = x.shape
    pos = jnp.arange(s)
    for l in range(DEPTH_2):
        h = rmsnorm(x, norm1_w[l])
        z = h @ w_in[l]
        qa, c_kv, iq, ik, iw, qb, kb, vb, gb = jnp.split(z, IN_OFFSETS, axis=-1)

        qa = rmsnorm(qa.reshape(b, s, A_HEADS, HEAD_DIM), q_norm_w[l])
        c = rmsnorm(c_kv, kv_norm_w[l])
        ka = rmsnorm(c @ w_uk[l], k_norm_w[l])
        va = c @ w_uv[l]
        out_a = indexed_sparse_attention(qa, ka, va,
                                         iq.reshape(b, s, IDX_HEADS, IDX_DIM), ik, iw, rel_bias)

        qr = rotary(qb.reshape(b, s, B_HEADS, HEAD_DIM).astype(jnp.float32), pos)
        kr = rotary(kb.reshape(b, s, B_HEADS, HEAD_DIM).astype(jnp.float32), pos) * HEAD_DIM ** -0.5
        vr = vb.reshape(b, s, B_HEADS, HEAD_DIM).astype(jnp.float32)
        y = chunkwise_retention(qr, kr, vr)
        mu = jnp.mean(y, axis=-1, keepdims=True)
        var = jnp.mean(jnp.square(y - mu), axis=-1, keepdims=True)
        y = ((y - mu) * lax.rsqrt(var + GN_EPS)).reshape(b, s, B_WIDTH)
        y = y * ret_gn_w[l].astype(jnp.float32) + ret_gn_b[l].astype(jnp.float32)
        out_b = (jax.nn.silu(gb.astype(jnp.float32)) * y).astype(x.dtype)

        x = x + jnp.concatenate([out_a, out_b], axis=-1) @ w_out[l]

        h2 = rmsnorm(x, norm2_w[l])
        x = x + (jax.nn.silu(h2 @ w_gate[l]) * (h2 @ w_up[l])) @ w_down[l]
    return x


def setup_inputs(seed=0):
    out = dict(first_inputs(seed))
    for name, value in second_inputs(seed + 1).items():
        if name != "x":
            out[name + "_2"] = value
    return out


def reference(
    x, c, ctx, c_ctx, ada_w, ada_b, pre_g, post_g, w_out, a_w_in, a_lambda, a_subln_g, b_w_in,
    b_qk_g, norm1_w_2, w_in_2, q_norm_w_2, k_norm_w_2, kv_norm_w_2, w_uk_2, w_uv_2, rel_bias_2,
    ret_gn_w_2, ret_gn_b_2, w_out_2, norm2_w_2, w_gate_2, w_up_2, w_down_2,
):
    x = first_block(
        x, c, ctx, c_ctx, ada_w, ada_b, pre_g, post_g, w_out, a_w_in, a_lambda, a_subln_g,
        b_w_in, b_qk_g,
    )
    return second_block(
        x, norm1_w_2, w_in_2, q_norm_w_2, k_norm_w_2, kv_norm_w_2, w_uk_2, w_uv_2, rel_bias_2,
        ret_gn_w_2, ret_gn_b_2, w_out_2, norm2_w_2, w_gate_2, w_up_2, w_down_2,
    )


_drawn_inputs = setup_inputs


def setup_inputs(seed=0):
    import zlib

    import numpy as np

    out = dict(_drawn_inputs(seed))
    spreads = {}
    factors = {'b_qk_g': 3.729,
     'q_norm_w_2': 8.0,
     'k_norm_w_2': 8.0,
     'kv_norm_w_2': 8.0,
     'rel_bias_2': 14.674,
     'ret_gn_w_2': 103.063,
     'ret_gn_b_2': 93.225,
     'norm2_w_2': 13.773}
    for name, (base, spread) in spreads.items():
        noise = np.random.default_rng([zlib.crc32(name.encode()), seed]).standard_normal(out[name].shape)
        drawn = base * np.exp(spread * noise) if base else spread * noise
        out[name] = __import__('jax').numpy.asarray(drawn.astype(out[name].dtype))
    for name, factor in factors.items():
        out[name] = (out[name] * factor).astype(out[name].dtype)
    return out
```

```python
import math
from contextlib import ExitStack

import concourse.bass as bass
from concourse import mybir

F32 = mybir.dt.float32
F32R = mybir.dt.float32r
ALU = mybir.AluOpType
ACTF = mybir.ActivationFunctionType
AX_X = mybir.AxisListType.X

P = 128
D = 1024
KT = D // P
XT = 2
NT = 4
COLS = 512
HALF_KT = 4
RING = 3
HEADS = 8
FFN = 2816
FFN_COLS = 256
FFN_STEPS = FFN // FFN_COLS
EPS = 1e-6
GN_EPS = 1e-5
LAMBDA_INIT = 0.8 - 0.6 * math.exp(-0.3 * 0)
IN2 = [(0, 512), (512, 292), (804, 512), (1316, 512), (1828, 512), (2340, 512)]
LOWEST = -3.4e38
INADMISSIBLE = -3.0e38

C_SILU, C_PRE, C_N1, C_N2, C_ADAB, C_KV, N_COLS = 0, 16, 32, 40, 48, 96, 97


class Sequence:

    def __init__(self, moved):
        self.moved, self.count, self.last = moved, {}, None

    def note(self, ins, sem):
        self.count[sem.name] = self.count.get(sem.name, 0) + 1
        self.last = (sem, self.count[sem.name])

    def freed(self, ins, name):
        self.last = self.moved(name)


def halves_plan():
    plan = []
    for stage, chunks in (("ada0", 4), ("in0", 8), ("ada0g", 2), ("ada1", 6), ("out0", 2), ("in1", 5), ("out1", 2),
                          ("in2", 6), ("out2", 2)):
        plan += [(stage, c, h) for c in range(chunks) for h in range(2)]
    for j in range(FFN_STEPS):
        plan += [("gu", j, 0), ("gu", j, 1)]
        if j > 0:
            plan.append(("down", j - 1, 0))
    plan.append(("down", FFN_STEPS - 1, 0))
    return plan


GEMM_CHUNKS = {"ada0": 4, "in0": 8, "ada0g": 2, "ada1": 6, "out0": 2, "in1": 5, "out1": 2, "in2": 6, "out2": 2}


def gemm_tiles(stage, chunk):
    if stage.startswith("ada"):
        return [0]
    if stage in ("in0", "out0") or (stage, chunk) == ("in1", 2):
        return [0, 1, 2, 3]
    return [0, 1]


BESIDE_ATTENTION0 = ([("in0", c, t, part) for c in (6, 7) for t in range(NT) for part in range(2)]
                     + [("ada0g", c, 0, part) for c in range(2) for part in range(2)]
                     + [("ada1", c, 0, part) for c in range(6) for part in range(2)])
SUB_AT = [18, 20, 26]
SPLITS_BESIDE0 = [7, 9] + list(range(15, NT * HEADS))


def banks_plan():
    order = {b: [] for b in range(8)}
    place = {}

    def put(name, bank):
        place[name] = (bank, len(order[bank]))
        order[bank].append(name)

    turn = [0]

    def gemm_unit(stage, c, t):
        put((stage, c, t), turn[0] % 2)
        turn[0] += 1

    def units(stage, chunks):
        for c in chunks:
            for t in gemm_tiles(stage, c):
                gemm_unit(stage, c, t)

    def norm(stage):
        for k in range(KT):
            put((stage, k), 2 + k % 4)

    def to_feature(stage, tiles):
        for t in range(tiles):
            for h in range(2):
                put((stage, t, h), 2 + (2 * t + h) % 4)

    put(("cols",), 7)
    units("ada0", range(4))
    put(("mod0",), 2)
    norm("norm0")
    units("in0", range(6))
    for c in range(4):
        for t in range(NT):
            put(("turn0", c, t), 2 + t)
    for p in range(NT * HEADS):
        put(("s0", p, 0), 2 + 2 * (p % 2))
        put(("s0", p, 1), 3 + 2 * (p % 2))
        put(("t0", p), 6)
        put(("pv0", p), 7)
    for stage, c, t, part in BESIDE_ATTENTION0:
        if part:
            gemm_unit(stage, c, t)
    put(("mod1",), 6)
    put(("gate1", 0, 0), 7)
    put(("gate1", 0, 1), 6)
    to_feature("turn_o0", NT)
    units("out0", range(1))
    for c in range(2):
        for s in range(2):
            put(("gate0", s, c), 6 + s)
    units("out0", range(1, 2))
    norm("norm1")
    units("in1", range(3))
    for c in range(3):
        for t in gemm_tiles("in1", c):
            put(("turn1", c, t), 2 + t)
    for p in range(XT * HEADS):
        put(("s1", p), 2 + p % 2)
        put(("t1", p), 6)
        put(("pv1", p), 7)
    units("in1", range(3, 5))
    to_feature("turn_o1", XT)
    units("out1", range(2))
    norm("norm2")
    units("in2", range(6))
    for t in range(XT):
        put(("turn_qa", t), 2 + t)
        put(("turn_c", t), 4 + t)
        put(("latent", t), 6 + t)
        put(("turn_ka", t), 6 + t)
        put(("turn_qb", t), 2 + t)
    put(("bias",), 5)
    for t in range(XT):
        put(("turn_kb", t), 4 + t)
    for t in range(XT):
        for i in range(4):
            put(("idx", t, i), 2 + i)
    for h in range(HEADS):
        put(("ret_s", h), 2 + h % 2)
    for t in range(XT):
        put(("ret_y", t), 6 + t)
    for p in range(8):
        put(("s2", p, 0), 2 + 2 * (p % 2))
        put(("s2", p, 1), 3 + 2 * (p % 2))
        put(("t2", p), 6)
        put(("pv2", p), 7)
    to_feature("turn_o2", XT)
    units("out2", range(2))
    norm("norm3")
    for t in range(XT):
        for c in range(2):
            put(("down", t, c), 2 * t + c)
    for j in range(FFN_STEPS):
        for t in range(XT):
            put(("gu", j, t), 4 + t)
            put(("turn_h", j, t), 6 + t)
    return place


def block_kernel(nc, a, out):
    halves = halves_plan()
    half_no = {key: g for g, key in enumerate(halves)}
    place = banks_plan()

    ctx = ExitStack()
    with ctx:
        def sb(name, shape, dt=F32):
            return ctx.enter_context(nc.sbuf_tensor(name, shape, dt))

        def sem(name):
            return ctx.enter_context(nc.semaphore(name))

        xs = sb("xs", [P, NT, D])
        with ExitStack() as parts:
            act_hi = parts.enter_context(nc.sbuf_tensor("act_hi", [P, KT, NT * P], F32R))
            act_lo = parts.enter_context(nc.sbuf_tensor("act_lo", [P, KT, NT * P], F32R))
        squares0 = sb("act_hi_as_f32", [P, NT, HEADS, P])
        act_lo_f32 = sb("act_lo_as_f32", [P, NT * D])
        raw = sb("raw", [P, RING, 2048])
        w_hi = sb("w_hi", [P, RING, 2048], F32R)
        w_lo = sb("w_lo", [P, RING, 2048], F32R)
        qT = sb("qT", [P, HEADS, NT * P])
        kT = sb("kT", [P, HEADS, NT * P])
        vbuf = sb("vbuf", [P, NT, D])
        zbuf = sb("zbuf", [P, NT, D])
        gate0 = sb("gate0", [P, 2, D])
        sc = sb("sc", [P, 8, COLS])
        ident = sb("ident", [P, P])
        vecs = sb("vecs", [P, P])
        cols = sb("cols", [P, P])
        silu_t = sc[0:16, 7, 0:256].rearrange("p (a n) -> p a n", a=2)
        c_hi = sb("c_hi", [P, 16], F32R)
        c_lo = sb("c_lo", [P, 16])
        cstat = sb("cstat", [P, KT, P], F32R)
        sel = sb("sel", [P, 2, P])
        mod = sb("mod", [P, 2, 2, KT, 2])
        zero = sb("zero", [P, 1])
        rope_a = sb("rope_a", [P, 2, XT, 32])
        rope_b = sb("rope_b", [P, 2, XT, 64])
        rope_c = sb("rope_c", [P, 2, XT, 32])
        lamb = sb("lamb", [P, 4, 64])
        lam_s = sb("lam_s", [P, 8])
        subln = sb("subln", [P, P])
        qk_g = sb("qk_g", [P, 2, P])
        qkn2 = sb("qkn2", [P, 2, 64])
        w_ukv = sb("w_ukv", [P, 2, 64])
        relb = sb("relb", [32, HEADS])
        ss = sb("ss", [P, 256])
        ms = sb("ms", [P, 128])
        rstd = sb("rstd", [P, 128])
        half_neg = sb("half_neg", [P, 16])
        nmax = sb("nmax", [P, 2, 2])
        rsum = sb("rsum", [P, 2, 2])
        rinv = sb("rinv", [P, 2, 4])

        gate1 = kT[:].rearrange("p h n -> p (h n)")[:, 3 * D:4 * D]
        mrow = qT[:].rearrange("p h n -> p (h n)")[:, 0:3 * D]
        xn = zbuf
        y_tok = vbuf
        q_flat = qT[:].rearrange("p h n -> p (h n)")
        qaT = q_flat[:, 0:1024].rearrange("p (b n) -> p b n", b=4)
        qbT = q_flat[:, 1024:2048].rearrange("p (b n) -> p b n", b=4)
        kbT = q_flat[:, 2048:3072].rearrange("p (b n) -> p b n", b=4)
        kaT = q_flat[:, 3072:3328]
        iqT = q_flat[:, 3328:3584]
        ikT = q_flat[:, 3584:3840]
        cT = q_flat[:, 3840:4096]
        biasm = kT[:].rearrange("p h n -> p (h n)").rearrange("p (h t k) -> p t h k", h=HEADS, t=XT)
        v_flat = vbuf[:].rearrange("p t n -> p (t n)")
        y2 = v_flat[:, 0:2048].rearrange("p (t n) -> p t n", t=XT)
        decay = v_flat[:, 0:2048].rearrange("p (h i) -> p h i", h=HEADS)
        gn_wb = v_flat[:, 2048:3072].rearrange("p (w n) -> p w n", w=2)
        onehot = v_flat[0:32, 3072:3584]
        toep = v_flat[0:HEADS, 3584:4096]
        z_flat = zbuf[:].rearrange("p t n -> p (t n)")
        mix = z_flat[:, 0:2048].rearrange("p (t n) -> p t n", t=XT)
        gb = z_flat[:, 2048:3072].rearrange("p (t n) -> p t n", t=XT)
        vb = z_flat[:, 3072:4096].rearrange("p (t n) -> p t n", t=XT)
        score = sc[:, 6, :].rearrange("p (t k) -> p t k", t=XT)
        small = gate0[:, 0, :]
        va = small[:, 0:128].rearrange("p (t d) -> p t d", t=XT)
        iw = small[:, 128:136].rearrange("p (t h) -> p t h", t=XT)
        best = small[:, 136:144]
        lat = small[:, 144:400].rearrange("p (t n) -> p t n", t=XT)
        iq = small[:, 400:656].rearrange("p (t n) -> p t n", t=XT)
        ik4 = small[:, 656:912].rearrange("p (t n) -> p t n", t=XT)
        ka2 = lat

        psum = ctx.enter_context(nc.psum_tensor("psum", [P, 8, COLS], F32))
        toep_dram = nc.dram_tensor("toep_scratch", (HEADS, COLS), F32, kind="Internal").ap()

        landed = [sem(f"raw_landed{i}") for i in range(RING)]
        s_whi, s_wlo, s_wused = sem("w_hi_ready"), sem("w_lo_ready"), sem("w_first_half_used")
        full = [sem(f"bank{b}_full") for b in range(8)]
        free = [sem(f"bank{b}_free") for b in range(8)]
        s_v, s_a, s_g = sem("vector_seq"), sem("scalar_seq"), sem("pool_seq")
        s_cin, s_xin, s_par, s_par1, s_par2 = sem("consts_in"), sem("x_in"), sem("params_in"), sem("ada1_params_in"), sem("block2_in")
        s_cst = sem("cstat_ready")
        s_mod = sem("mod_rows_ready")
        s_silu = sem("silu_exp")
        s_silu_v = sem("silu_cols")
        s_xn, s_h, s_act = sem("xn_ready"), sem("act_hi_ready"), sem("act_ready")
        s_rot, s_attn = sem("rot_ready"), sem("attn_in_ready")
        s_mx, s_ex, s_comb, s_pt = sem("max_ready"), sem("exp_ready"), sem("probs_ready"), sem("probsT_ready")
        s_tanh, s_sq = sem("tanh_ready"), sem("square_sum_ready")
        s_powin, s_powout = sem("mean_ready"), sem("rstd_ready")
        s_tok = sem("gated_ready")
        s_rinv = sem("rinv_ready")
        s_lamin, s_lamout = sem("lambda_sums"), sem("lambda_exps")
        s_toep, s_toepw, s_toepr, s_idx = sem("toep_ready"), sem("toep_written"), sem("toep_read"), sem("idx_relu_ready")
        s_store = sem("stored")
        s_outr = sem("out_ready")
        s_yc = sem("centred")
        s_half = sem("minus_half")
        s_zg, s_og = sem("gate_branch_weighted"), sem("head_outputs_normed")
        s_res, s_yret = sem("residual_ready"), sem("retention_head_done")
        N_CIN = 8
        N_PAR = 13
        mrow1 = act_lo_f32[:, 0:3 * D]
        mrow0g = gate0[:, 0, :]
        k_flat = kT[:].rearrange("p h n -> p (h n)")
        ss_norm = {("norm0", t): t for t in range(NT)}
        ss_norm.update({("norm1", t): 4 + t for t in range(NT)})
        ss_norm.update({("norm2", t): 8 + t for t in range(XT)})
        ss_norm.update({("norm3", t): 10 + t for t in range(XT)})
        ss_post = {("out0", t): 12 + 2 * t for t in range(NT)}
        ss_post.update({("out1", t): 20 + 2 * t for t in range(XT)})
        ss_lat, ss_ka = 24, 26

        def half_src(stage, c, h):
            rows = slice(h * HALF_KT * P, (h + 1) * HALF_KT * P)

            def cut(w, lo, n):
                return w[rows, lo:lo + n].rearrange("(k p) n -> p k n", p=P)

            if stage == "ada0g":
                return [cut(a["ada_w"][0], (4 + c) * COLS, COLS)]
            if stage in ("ada0", "ada1"):
                return [cut(a["ada_w"][int(stage[3])], c * COLS, COLS)]
            if stage == "in0":
                return [cut(a["a_w_in"][0], c * COLS, COLS)]
            if stage in ("out0", "out1"):
                return [cut(a["w_out"][int(stage[3])], c * COLS, COLS)]
            if stage == "in1":
                return [cut(a["b_w_in"][0], c * COLS, COLS)]
            if stage == "in2":
                return [cut(a["w_in_2"][0], *IN2[c])]
            if stage == "out2":
                return [cut(a["w_out_2"][0], c * COLS, COLS)]
            if stage == "gu":
                return [cut(a["w_gate_2"][0], c * FFN_COLS, FFN_COLS), cut(a["w_up_2"][0], c * FFN_COLS, FFN_COLS)]
            return [a["w_down_2"][0][c * FFN_COLS:(c + 1) * FFN_COLS, :].rearrange("(k p) n -> p k n", p=P)]

        def half_size(g):
            stage, c, _ = halves[g]
            return HALF_KT * IN2[c][1] if stage == "in2" else 2048

        def half_width(g):
            stage, c, _ = halves[g]
            return IN2[c][1] if stage == "in2" else D if stage == "down" else COLS

        def w_view(buf, g):
            n = half_width(g)
            return buf[:, g % RING, 0:half_size(g)].rearrange("p (k n) -> p k n", n=n)

        released, firsts = {}, 0
        for g, (stage, c, h) in enumerate(halves):
            if stage == "down":
                firsts += 1
                released[g] = (s_wused, firsts)
            elif h == 0:
                firsts += 1
                released[g] = (s_wused, firsts)
            else:
                key = (stage, c, 1) if stage == "gu" else (stage, c, gemm_tiles(stage, c)[-1])
                b, n = place[key]
                released[g] = (full[b], n + 1)

        landed_at, n_landed = {}, [0] * RING
        for g, (stage, c, h) in enumerate(halves):
            n_landed[g % RING] += 32 if stage == "gu" else 16
            landed_at[g] = n_landed[g % RING]

        act_base, n = {}, 0
        for stage, count in (("norm0", 8), ("turn_o0", 8), ("norm1", 8), ("turn_o1", 4), ("norm2", 8),
                             ("turn_o2", 4), ("norm3", 8), ("hidden", 2 * FFN_STEPS)):
            act_base[stage] = n
            n += count
        xn_base = {"norm0": 0, "norm1": 4, "norm2": 8, "norm3": 10}
        norm_tiles = {"norm0": NT, "norm1": NT, "norm2": XT, "norm3": XT}
        pows, pow_at, n = [], {}, 0
        for key, width in ([(("norm0", t), 1) for t in range(NT)]
                           + [(("sub", t), 8) for t in range(NT)]
                           + [(("post0", t), 1) for t in range(NT)] + [(("norm1", t), 1) for t in range(NT)]
                           + [(("qk1", c, t), 4 if c < 2 else 2) for c in range(3) for t in gemm_tiles("in1", c)]
                           + [(("post1", t), 1) for t in range(XT)] + [(("norm2", t), 1) for t in range(XT)]
                           + [(("qa", t), 8) for t in range(XT)] + [(("lat", t), 1) for t in range(XT)]
                           + [(("ka", t), 1) for t in range(XT)]
                           + [(("gn", t), 8) for t in range(XT)] + [(("norm3", t), 1) for t in range(XT)]):
            pow_at[key] = (len(pows), n, width)
            pows.append((n, width))
            n += width
        assert n <= 128

        def bank(name, n=COLS):
            return psum[:, place[name][0], 0:n]

        block = ctx.enter_context(nc.Block())

        @block.sync
        def _(sp):
            

            def load(dst, src, s):
                sp.dma_start(dst, src).then_inc(s, 16)

            def stream(g):
                if g >= RING:
                    sp.wait_ge(s_wlo, g - RING + 1)
                n = half_width(g)
                dst = w_view(raw, g)
                parts = half_src(*halves[g])
                if len(parts) == 1:
                    sp.dma_start(dst, parts[0]).then_inc(landed[g % RING], 16)
                else:
                    for i, part in enumerate(parts):
                        sp.dma_start(dst[:, :, i * FFN_COLS:(i + 1) * FFN_COLS], part).then_inc(landed[g % RING], 16)

            load(silu_t[0:8, 0, :], a["c"].rearrange("a (k p) -> (a k) p", p=P), s_cin)
            load(silu_t[8:16, 0, :], a["c_ctx"].rearrange("(k p) -> k p", p=P), s_cin)
            load(vecs[16:32, :], a["pre_g"].rearrange("l (k p) -> (l k) p", p=P), s_cin)
            load(vecs[32:40, :], a["norm1_w_2"].rearrange("l (k p) -> (l k) p", p=P), s_cin)
            load(vecs[40:48, :], a["norm2_w_2"].rearrange("l (k p) -> (l k) p", p=P), s_cin)
            load(vecs[48:96, :], a["ada_b"].rearrange("l (k p) -> (l k) p", p=P), s_cin)
            load(vecs[96:97, :], a["kv_norm_w_2"], s_cin)
            load(ident[:], a["k_ident"], s_cin)
            for g in range(RING):
                stream(g)
            for g in range(RING, len(halves)):
                if halves[g] == ("out0", 1, 0):
                    b, n = place[("s0", NT * HEADS - 1, 1)]
                    sp.wait_ge(full[b], n + 1)
                    load(k_flat[:, 0:D], a["ada_b"][1, 2 * D:3 * D].partition_broadcast(P), s_par1)
                    load(k_flat[:, D:2 * D], a["post_g"][1].partition_broadcast(P), s_par1)
                    load(k_flat[:, 2 * D:3 * D], a["ada_b"][0, 2 * D:3 * D].partition_broadcast(P), s_par1)
                if halves[g] == ("in2", 2, 0):
                    sp.wait_ge(s_xn, xn_base["norm2"] + XT)
                    load(decay, a["k_decay"], s_par2)
                    load(gn_wb[:, 0, :], a["ret_gn_w_2"][0].partition_broadcast(P), s_par2)
                    load(gn_wb[:, 1, :], a["ret_gn_b_2"][0].partition_broadcast(P), s_par2)
                    load(onehot, a["k_onehot"], s_par2)
                if halves[g] == ("out2", 0, 0):
                    sp.wait_ge(s_toep, 1)
                    sp.dma_start(toep_dram, toep).then_inc(s_toepw, 16)
                    sp.wait_ge(s_toepw, 16)
                    for t in range(XT):
                        band = bass.AP(toep_dram.tensor, t * P, [[1, P], [COLS, HEADS], [1, 256]])
                        load(biasm[:, t], band, s_toepr)
                stream(g)
            for t in range(XT):
                sp.wait_ge(s_outr, 2 * (t + 1))
                sp.dma_start(out[0, t * P:(t + 1) * P, :], xs[:, t, :]).then_inc(s_store, 16)
            sp.wait_ge(s_store, 16 * XT)


        def bank_full(name):
            return full[place[name][0]]

        def bank_free(name):
            return free[place[name][0]]

        def finished(name):
            b, n = place[name]
            return full[b], n + 1

        def moved(name):
            b, n = place[name]
            return free[b], n + 1

        def tile_cols(t, n=1):
            return slice(t * P, (t + n) * P)

        def last_unit(stage):
            c = GEMM_CHUNKS[stage] - 1
            return (stage, c, gemm_tiles(stage, c)[-1])

        NORM_COLS = {"norm2": C_N1, "norm3": C_N2}
        h_base, n = {}, 0
        for stage, count in (("norm0", 8), ("turn_o0", 8), ("norm1", 8), ("turn_o1", 4), ("norm2", 8),
                             ("turn_o2", 4), ("norm3", 8), ("hidden", 2 * FFN_STEPS)):
            h_base[stage] = n
            n += count
        act_base = {"norm0": 0, "norm1": 8, "norm2": 16, "norm3": 24}
        act_of = {"in0": "norm0", "out0": "turn_o0", "in1": "norm1", "out1": "turn_o1", "in2": "norm2",
                  "out2": "turn_o2", "gu": "norm3"}
        tok_base = {"turn_o0": 0, "turn_o1": NT, "turn_o2": NT + XT}
        before_act = {"norm0": None, "turn_o0": "in0", "norm1": "out0", "turn_o1": "in1", "norm2": "out1",
                      "turn_o2": "in2", "norm3": "out2"}
        rot_units = ([("turn0", c, t) for c in range(4) for t in range(NT)]
                     + [("turn1", c, t) for c in range(3) for t in gemm_tiles("in1", c)]
                     + [("turn_qa", t) for t in range(XT)] + [("turn_qb", t) for t in range(XT)]
                     + [("turn_kb", t) for t in range(XT)])
        rot_no = {name: n for n, name in enumerate(rot_units)}

        def rot_buf(name):
            return sc[:, rot_no[name] % 3, :]

        z_first0, z_first1 = half_no[("in0", 6, 0)], half_no[("in1", 3, 0)]
        sq_order = ([("norm0", t) for t in range(NT)] + [("sub", t) for t in range(NT)]
                    + [("norm1", t) for t in range(NT)]
                    + [("qk1", c, t) for c in range(3) for t in gemm_tiles("in1", c)]
                    + [("norm2", t) for t in range(XT)] + [("qa", t) for t in range(XT)]
                    + [("lat", t) for t in range(XT)] + [("ka", t) for t in range(XT)]
                    + [("gn", t) for t in range(XT)] + [("norm3", t) for t in range(XT)])
        sq_no = {name: n for n, name in enumerate(sq_order)}

        @block.tensor
        def _(pe):
            

            def begin(name):
                b, n = place[name]
                if n:
                    pe.wait_ge(free[b], n)
                return psum[:, b, :]

            def act_ready(stage, c, t, k):
                src = act_of[stage]
                if c:
                    return
                if src in act_base:
                    if t == 0:
                        pe.wait_ge(s_act, act_base[src] + k + 1)
                elif k % HALF_KT == 0:
                    pe.wait_ge(*moved((src, t, k // HALF_KT)))

            def gemm_unit(stage, c, t, parts=(0, 1)):
                name = (stage, c, t)
                o = begin(name) if parts[0] == 0 else psum[:, place[name][0], :]
                g0 = half_no[(stage, c, 0)]
                n = half_width(g0)
                for h in parts:
                    pe.wait_ge(s_wlo, g0 + h + 1)
                    hi, lo = w_view(w_hi, g0 + h), w_view(w_lo, g0 + h)
                    for kk in range(HALF_KT):
                        k = h * HALF_KT + kk
                        act_ready(stage, c, t, k)
                        x_hi, x_lo = act_hi[:, k, tile_cols(t)], act_lo[:, k, tile_cols(t)]
                        pe.matmul(o[:, 0:n], x_hi, hi[:, kk, :], start=(k == 0), stop=False)
                        pe.matmul(o[:, 0:n], x_hi, lo[:, kk, :], start=False, stop=False)
                        mm = pe.matmul(o[:, 0:n], x_lo, hi[:, kk, :], start=False, stop=(k == KT - 1))
                    if h == 0 and t == (gemm_tiles(stage, c)[-1] if stage != "gu" else XT - 1):
                        mm.then_inc(s_wused, 1)
                if parts[-1] == 1:
                    mm.then_inc(bank_full(name), 1)

            def ada_half(stage, c, h):
                name = (stage, c, 0)
                o = psum[:, place[name][0], :] if h else begin(name)
                g = half_no[(stage, c, h)]
                pe.wait_ge(s_wlo, g + 1)
                hi, lo = w_view(w_hi, g), w_view(w_lo, g)
                for kk in range(HALF_KT):
                    k = h * HALF_KT + kk
                    pe.matmul(o, cstat[:, k, :], hi[:, kk, :], start=(k == 0), stop=False)
                    mm = pe.matmul(o, cstat[:, k, :], lo[:, kk, :], start=False, stop=(k == KT - 1))
                if h == 0:
                    mm.then_inc(s_wused, 1)
                else:
                    mm.then_inc(bank_full(name), 1)

            def mod_columns(l):
                rows = mrow if l == 0 else mrow1
                for c in range(4):
                    pe.wait_ge(*moved((f"ada{l}", c, 0)))
                o = begin((f"mod{l}",))
                for blk in range(2 * KT):
                    mm = pe.matmul(o[:, 2 * blk:2 * blk + 2], rows[:, blk * P:(blk + 1) * P], sel[:, :, 0],
                                   start=True, stop=True)
                mm.then_inc(bank_full((f"mod{l}",)), 1)

            def gate_row(l, s, c):
                rows = mrow1[:, 2 * D:3 * D] if l else mrow0g
                pe.wait_ge(*moved(("ada1", 4 + c, 0) if l else ("ada0g", c, 0)))
                name = (f"gate{l}", s, c)
                o = begin(name)
                pe.matmul(o, sel[:, s, :], rows[:, c * COLS:(c + 1) * COLS],
                          start=True, stop=True).then_inc(bank_full(name), 1)

            def norm(stage):
                for t in range(norm_tiles[stage]):
                    pe.wait_ge(s_xn, xn_base[stage] + t + 1)
                for k in range(KT):
                    o = begin((stage, k))
                    for t in range(norm_tiles[stage]):
                        mm = pe.transpose(o[:, tile_cols(t)], xn[:, t, k * P:(k + 1) * P], ident[:])
                    mm.then_inc(bank_full((stage, k)), 1)

            def to_feature(stage, tiles, src):
                for t in (range(tiles) if isinstance(tiles, int) else tiles):
                    pe.wait_ge(s_tok, tok_base[stage] + t + 1)
                    for h in range(2):
                        o = begin((stage, t, h))
                        for i in range(HALF_KT):
                            k = h * HALF_KT + i
                            mm = pe.transpose(o[:, tile_cols(i)], src[:, t, k * P:(k + 1) * P], ident[:])
                        mm.then_inc(bank_full((stage, t, h)), 1)

            def turn(name, blocks=4):
                pe.wait_ge(s_rot, rot_no[name] + 1)
                o = begin(name)
                for i in range(blocks):
                    mm = pe.transpose(o[:, tile_cols(i)], rot_buf(name)[:, tile_cols(i)], ident[:])
                mm.then_inc(bank_full(name), 1)

            def turn_probs(name, src, blocks):
                o = begin(name)
                for i in range(blocks):
                    mm = pe.transpose(o[:, tile_cols(i)], src[:, tile_cols(i)], ident[:])
                mm.then_inc(bank_full(name), 1)

            pe.wait_ge(s_cin, 16 * N_CIN)
            pe.wait_ge(s_silu_v, 1)
            o = begin(("cols",))
            pe.transpose(o[:, 0:N_COLS], vecs[0:N_COLS, :], ident[0:N_COLS, 0:N_COLS]).then_inc(bank_full(("cols",)), 1)
            pe.wait_ge(s_cst, 1)
            for c in range(4):
                for h in range(2):
                    ada_half("ada0", c, h)
            pe.wait_ge(s_par, 16 * N_PAR)
            mod_columns(0)

            norm("norm0")
            units = [(c, t) for c in range(6) for t in range(NT)]
            for n, (c, t) in enumerate(units):
                gemm_unit("in0", c, t)
                if 2 <= n < 2 + 4 * NT:
                    turn(("turn0", *units[n - 2]))
            for c in range(4):
                for t in range(NT):
                    pe.wait_ge(*moved(("turn0", c, t)))

            def scores0(p):
                t, h = divmod(p, HEADS)
                keys = slice(0, NT * P) if t < XT else slice(XT * P, NT * P)
                n = keys.stop - keys.start
                for s in range(2):
                    rows = slice(64 * s, 64 * s + 64)
                    o = begin(("s0", p, s))
                    pe.matmul(o[:, 0:n], qT[rows, h, tile_cols(t)], kT[rows, h, keys], start=True, stop=True).then_inc(bank_full(("s0", p, s)), 1)

            def values0(p):
                t, h = divmod(p, HEADS)
                blocks = NT if t < XT else XT
                pe.wait_ge(*moved(("t0", p)))
                o = begin(("pv0", p))
                probs = sc[:, 6 + p % 2, :]
                for i in range(blocks):
                    mm = pe.matmul(o[:, 0:P], probs[:, tile_cols(i)], vbuf[:, NT - blocks + i, tile_cols(h)],
                                   start=(i == 0), stop=(i == blocks - 1))
                mm.then_inc(bank_full(("pv0", p)), 1)

            for c in (4, 5):
                for t in range(NT):
                    pe.wait_ge(*moved(("in0", c, t)))
            scores0(0)
            scores0(1)
            for p in range(NT * HEADS):
                pe.wait_ge(s_comb, p + 1)
                turn_probs(("t0", p), sc[:, 4 + p % 2, :], NT if p < XT * HEADS else XT)
                stage, c, t, part = BESIDE_ATTENTION0[p]
                if stage == "in0":
                    gemm_unit(stage, c, t, parts=(part,))
                else:
                    ada_half(stage, c, part)
                if p + 2 < NT * HEADS:
                    scores0(p + 2)
                values0(p)

            mod_columns(1)
            gate_row(1, 0, 0)
            gate_row(1, 0, 1)
            to_feature("turn_o0", range(NT - 1), zbuf)
            for t in range(NT):
                if t == NT - 1:
                    to_feature("turn_o0", range(NT - 1, NT), zbuf)
                gemm_unit("out0", 0, t)
            for c in range(2):
                for s in range(2):
                    gate_row(0, s, c)
            for t in range(NT):
                gemm_unit("out0", 1, t)

            norm("norm1")
            units = [(c, t) for c in range(3) for t in gemm_tiles("in1", c)]
            for n in range(len(units) + 2):
                if n < len(units):
                    gemm_unit("in1", *units[n])
                if n >= 2:
                    turn(("turn1", *units[n - 2]), 4 if units[n - 2][0] < 2 else 2)
            for c, t in units:
                pe.wait_ge(*moved(("turn1", c, t)))

            def scores1(p):
                t, h = divmod(p, HEADS)
                o = begin(("s1", p))
                pe.matmul(o, qT[:, h, tile_cols(t)], kT[:, h // 4, :], start=True, stop=True).then_inc(bank_full(("s1", p)), 1)

            def values1(p):
                t, h = divmod(p, HEADS)
                pe.wait_ge(*moved(("t1", p)))
                o = begin(("pv1", p))
                probs = sc[:, 6 + p % 2, :]
                for i in range(NT):
                    mm = pe.matmul(o[:, 0:P], probs[:, tile_cols(i)], vbuf[:, i, tile_cols(h // 4)],
                                   start=(i == 0), stop=(i == NT - 1))
                mm.then_inc(bank_full(("pv1", p)), 1)

            z_units1 = [(c, t) for c in (3, 4) for t in range(XT)]
            scores1(0)
            scores1(1)
            for p in range(XT * HEADS):
                pe.wait_ge(*moved(("s1", p)))
                turn_probs(("t1", p), sc[:, p % 2, :], NT)
                if p % 2 == 0:
                    gemm_unit("in1", *z_units1[p // 4], parts=((p // 2) % 2,))
                if p + 2 < XT * HEADS:
                    scores1(p + 2)
                values1(p)
            to_feature("turn_o1", XT, zbuf)
            for c in range(2):
                for t in range(XT):
                    gemm_unit("out1", c, t)

            norm("norm2")

            def in2(c):
                for t in range(XT):
                    gemm_unit("in2", c, t)

            in2(0)
            in2(1)
            for t in range(XT):
                turn(("turn_qa", t))
            in2(2)
            for t in range(XT):
                pe.wait_ge(*moved(("in2", 1, t)))
                o = begin(("turn_c", t))
                for i, src in enumerate((lat, iq, ik4)):
                    mm = pe.transpose(o[:, tile_cols(i)], src[:, t, :], ident[:])
                mm.then_inc(bank_full(("turn_c", t)), 1)
            pe.wait_ge(s_par2, 16 * 4)
            o = begin(("bias",))
            pe.matmul(o[0:HEADS, :], relb[:], onehot, start=True, stop=True).then_inc(bank_full(("bias",)), 1)
            in2(3)
            for t in range(XT):
                pe.wait_ge(*moved(("turn_c", t)))
                o = begin(("latent", t))
                pe.matmul(o[:, 0:P], cT[:, tile_cols(t)], w_ukv[:].rearrange("p a d -> p (a d)"),
                              start=True, stop=True).then_inc(bank_full(("latent", t)), 1)
                turn(("turn_qb", t))
            in2(4)
            for t in range(XT):
                pe.wait_ge(*moved(("latent", t)))
                o = begin(("turn_ka", t))
                pe.transpose(o[:, 0:P], ka2[:, t, :], ident[:]).then_inc(bank_full(("turn_ka", t)), 1)
                turn(("turn_kb", t))
            in2(5)
            for t in range(XT):
                for i in range(4):
                    rows = slice(32 * i, 32 * i + 32)
                    o = begin(("idx", t, i))
                    pe.matmul(o[:, 0:256], iqT[rows, tile_cols(t)], ikT[rows, :], start=True, stop=True).then_inc(bank_full(("idx", t, i)), 1)
            for t in range(XT):
                pe.wait_ge(*moved(("turn_qb", t)))
                pe.wait_ge(*moved(("turn_kb", t)))
                pe.wait_ge(*moved(("in2", 4, t)))

            def ret_scores(h):
                rows = slice(64 * (h % 2), 64 * (h % 2) + 64)
                o = begin(("ret_s", h))
                pe.matmul(o[:, 0:256], kbT[rows, h // 2, 0:P], qbT[rows, h // 2, 0:256], start=True, stop=True)
                pe.matmul(o[:, 256:384], kbT[rows, h // 2, P:256], qbT[rows, h // 2, P:256],
                              start=True, stop=True).then_inc(bank_full(("ret_s", h)), 1)

            y_out = [begin(("ret_y", t)) for t in range(XT)]
            ret_scores(0)
            for h in range(HEADS):
                if h + 1 < HEADS:
                    ret_scores(h + 1)
                pe.wait_ge(*moved(("ret_s", h)))
                m = sc[:, 4 + h % 2, :]
                d = slice(64 * h, 64 * h + 64)
                mm = pe.matmul(y_out[0][:, d], m[:, 0:P], vb[:, 0, d], start=True, stop=True)
                if h == HEADS - 1:
                    mm.then_inc(bank_full(("ret_y", 0)), 1)
                pe.matmul(y_out[1][:, d], m[:, P:256], vb[:, 0, d], start=True, stop=False)
                mm = pe.matmul(y_out[1][:, d], m[:, 256:384], vb[:, 1, d], start=False, stop=True)
                if h == HEADS - 1:
                    mm.then_inc(bank_full(("ret_y", 1)), 1)
                else:
                    mm.then_inc(s_yret, 1)

            def scores2(p):
                t, hp = divmod(p, 4)
                for e in range(2):
                    rows = slice(64 * e, 64 * e + 64)
                    o = begin(("s2", p, e))
                    pe.matmul(o[:, 0:256], qaT[rows, hp, tile_cols(t)], kaT[rows, :], start=True, stop=True).then_inc(bank_full(("s2", p, e)), 1)

            scores2(0)
            for p in range(8):
                if p + 1 < 8:
                    scores2(p + 1)
                pe.wait_ge(s_ex, p + 1)
                turn_probs(("t2", p), sc[:, p % 2, :], 4)
                pe.wait_ge(*moved(("t2", p)))
                o = begin(("pv2", p))
                probs = sc[:, 2 + p % 2, :]
                for e in range(2):
                    for i in range(2):
                        mm = pe.matmul(o[:, 64 * e:64 * e + 64], probs[:, tile_cols(2 * e + i)], va[:, i, :],
                                       start=(i == 0), stop=(i == 1))
                mm.then_inc(bank_full(("pv2", p)), 1)
            to_feature("turn_o2", XT, mix)
            for c in range(2):
                for t in range(XT):
                    gemm_unit("out2", c, t)

            norm("norm3")
            down_out = {(t, c): begin(("down", t, c)) for t in range(XT) for c in range(2)}

            def turn_hidden(j):
                for t in range(XT):
                    pe.wait_ge(*moved(("gu", j, t)))
                    o = begin(("turn_h", j, t))
                    for i in range(2):
                        mm = pe.transpose(o[:, tile_cols(i)], sc[:, 4 + 2 * (j % 2) + t, tile_cols(i)], ident[:])
                    mm.then_inc(bank_full(("turn_h", j, t)), 1)

            def down(j):
                g = half_no[("down", j, 0)]
                pe.wait_ge(s_wlo, g + 1)
                hi, lo = w_view(w_hi, g), w_view(w_lo, g)
                for t in range(XT):
                    pe.wait_ge(*moved(("turn_h", j, t)))
                    for i in range(2):
                        k = 2 * (j % 2) + i
                        x_hi, x_lo = act_hi[:, k, tile_cols(XT + t)], act_lo[:, k, tile_cols(XT + t)]
                        for c in range(2):
                            w = slice(c * COLS, (c + 1) * COLS)
                            o = down_out[(t, c)]
                            last = j == FFN_STEPS - 1 and i == 1
                            pe.matmul(o, x_hi, hi[:, i, w], start=(j == 0 and i == 0), stop=False)
                            pe.matmul(o, x_hi, lo[:, i, w], start=False, stop=False)
                            mm = pe.matmul(o, x_lo, hi[:, i, w], start=False, stop=last)
                            if last:
                                mm.then_inc(bank_full(("down", t, c)), 1)
                if not last:
                    mm.then_inc(s_wused, 1)

            for j in range(FFN_STEPS):
                gemm_unit("gu", j, 0)
                if j:
                    turn_hidden(j - 1)
                gemm_unit("gu", j, 1)
                if j:
                    down(j - 1)
            turn_hidden(FFN_STEPS - 1)
            down(FFN_STEPS - 1)

        @block.scalar
        def _(act):
            seq = Sequence(moved)
            done_halves = [0]

            def split_through(g):
                while done_halves[0] <= min(g, len(halves) - 1):
                    n = done_halves[0]
                    act.wait_ge(landed[n % RING], landed_at[n])
                    if n >= RING:
                        act.wait_ge(*released[n - RING])
                    seq.note(act.activation(w_hi[:, n % RING, 0:half_size(n)], raw[:, n % RING, 0:half_size(n)],
                                             ACTF.Copy).then_inc(s_whi, 1), s_whi)
                    done_halves[0] += 1

            def run_chunk(stage, c, unit):
                g0 = half_no[(stage, c, 0)]
                tiles = gemm_tiles(stage, c)
                for t in tiles:
                    if t == tiles[-1]:
                        split_through(g0 + 3)
                    unit(c, t)
                split_through(g0 + 4)

            def square_sum(name, src, dst_junk, accum=None):
                act.wait_ge(*seq.last)
                if accum is None:
                    ins = act.activation(dst_junk, src, ACTF.Square)
                else:
                    ins = act.activation(dst_junk, src, ACTF.Square, accum_out=accum)
                assert seq.count.get(s_sq.name, 0) == sq_no[name], name
                seq.note(ins.then_inc(s_sq, 1), s_sq)

            def norm(stage, l=None):
                tiles = norm_tiles[stage]
                for k in range(KT):
                    act.wait_ge(*finished((stage, k)))
                    buf = sc[:, 5 + k % 2, :]
                    if k >= 2:
                        act.wait_ge(s_act, act_base[stage] + k - 1)
                    ps = psum[:, place[(stage, k)][0], :]
                    for s in range(tiles // XT):
                        r = slice(s * XT * P, (s + 1) * XT * P)
                        if l is None:
                            c0 = NORM_COLS[stage]
                            ins = act.activation(buf[:, r], ps[:, r], ACTF.Identity, scale=cols[:, c0 + k:c0 + k + 1],
                                                 bias=zero[:])
                        else:
                            ins = act.activation(buf[:, r], ps[:, r], ACTF.Identity, scale=mod[:, l, 0, k, s:s + 1],
                                                 bias=mod[:, l, 1, k, s:s + 1])
                        if s == tiles // XT - 1:
                            seq.freed(ins.then_inc(bank_free((stage, k)), 1), (stage, k))
                        else:
                            seq.note(ins.then_inc(s_a, 1), s_a)
                    act.wait_ge(*seq.last)
                    if k == 0 and before_act[stage]:
                        act.wait_ge(*finished(last_unit(before_act[stage])))
                    seq.note(act.activation(act_hi[:, k, 0:tiles * P], buf[:, 0:tiles * P], ACTF.Copy).then_inc(s_h, 1), s_h)

            def to_feature(stage, tiles):
                act.wait_ge(*finished(last_unit(before_act[stage])))
                for t in (range(tiles) if isinstance(tiles, int) else tiles):
                    for h in range(2):
                        act.wait_ge(*finished((stage, t, h)))
                        ps = psum[:, place[(stage, t, h)][0], :].rearrange("p (k n) -> p k n", k=HALF_KT)
                        seq.note(act.activation(act_hi[:, h * HALF_KT:(h + 1) * HALF_KT, tile_cols(t)], ps,
                                                 ACTF.Copy).then_inc(s_h, 1), s_h)

            def move(dst, name, n=COLS, scale=1.0, wait_for=None):
                act.wait_ge(*finished(name))
                if wait_for:
                    act.wait_ge(*finished(wait_for))
                src = psum[:, place[name][0], 0:n]
                if len(dst.shape) == 3:
                    src = src.rearrange("p (k n) -> p k n", k=dst.shape[1])
                seq.freed(act.activation(dst, src, ACTF.Copy, scale=scale).then_inc(bank_free(name), 1), name)

            def tanh_half(dst, name, n=COLS):
                act.wait_ge(*finished(name))
                seq.note(act.activation(dst, psum[:, place[name][0], 0:n], ACTF.Tanh, scale=0.5).then_inc(s_tanh, 1), s_tanh)

            act.wait_ge(s_cin, 16 * N_CIN)
            seq.note(act.activation(silu_t[:, 1, :], silu_t[:, 0, :], ACTF.Tanh, scale=0.5).then_inc(s_silu, 1), s_silu)
            for t in range(XT):
                act.dma_start(xs[:, t, :], a["x"][0, t * P:(t + 1) * P, :]).then_inc(s_xin, 16)
                act.dma_start(xs[:, XT + t, :], a["ctx"][0, t * P:(t + 1) * P, :]).then_inc(s_xin, 16)
            split_through(2)
            act.wait_ge(s_xin, 16 * NT)
            for t in range(NT):
                square_sum(("norm0", t), xs[:, t, :], sc[:, 2 * (t % 2):2 * (t % 2) + 2, :].rearrange("p a n -> p (a n)"),
                           ss[:, t:t + 1])

            for c in range(4):
                run_chunk("ada0", c, lambda c, t: move(mrow[:, c * COLS:(c + 1) * COLS], ("ada0", c, 0)))
            act.wait_ge(s_lamin, 1)
            seq.note(act.activation(lam_s[:, 2:4], lam_s[:, 0:2], ACTF.Exp).then_inc(s_lamout, 1), s_lamout)
            act.wait_ge(s_mod, 1)
            norm("norm0", 0)

            turned = [("turn0", c, t) for c in range(4) for t in range(NT)]

            def move_turned(name):
                _, c, t = name
                dst = (qT if c < 2 else kT)[:, 4 * (c % 2):4 * (c % 2) + 4, tile_cols(t)]
                move(dst, name, scale=0.125 if c < 2 else 1.0)

            def unit0(c, t):
                n = c * NT + t
                if 2 <= n < 2 + len(turned):
                    move_turned(turned[n - 2])
                if c in (4, 5):
                    move(vbuf[:, t, (c - 4) * COLS:(c - 3) * COLS], ("in0", c, t))

            for c in range(6):
                run_chunk("in0", c, unit0)

            def exp0(p):
                t = p // HEADS
                n = NT * P if t < XT else XT * P
                act.wait_ge(s_mx, p + 1)
                if p >= 2:
                    act.wait_ge(s_comb, p - 1)
                for s in range(2):
                    b = place[("s0", p, s)][0]
                    seq.freed(act.activation(sc[:, 2 * (p % 2) + s, 0:n], psum[:, b, 0:n], ACTF.Exp,
                                                 bias=nmax[:, p % 2, s:s + 1], accum_out=rsum[:, p % 2, s:s + 1]).then_inc(bank_free(("s0", p, s)), 1), ("s0", p, s))

            def out0(p):
                t, h = divmod(p, HEADS)
                move(qT[:, h, tile_cols(t)], ("pv0", p), n=P, scale=rinv[:, p % 2, 0:1])

            def beside0(p):
                stage, c, t, part = BESIDE_ATTENTION0[p]
                if part == 0:
                    return
                if stage == "in0":
                    tanh_half(zbuf[:, t, (c - 6) * COLS:(c - 5) * COLS], (stage, c, t))
                elif stage == "ada0g":
                    move(mrow0g[:, c * COLS:(c + 1) * COLS], (stage, c, t))
                else:
                    move(mrow1[:, c * COLS:(c + 1) * COLS], (stage, c, t))

            def sub_squares(t):
                square_sum(("sub", t), qT[:, :, tile_cols(t)], squares0[:, t] if t < NT - 1 else
                           sc[:, 0:2, :].rearrange("p a (h d) -> p (a h) d", d=P))

            exp0(0)
            for p in range(NT * HEADS):
                if p:
                    out0(p - 1)
                if p + 1 < NT * HEADS:
                    exp0(p + 1)
                n = NT * P if p < XT * HEADS else XT * P
                move(sc[:, 6 + p % 2, 0:n], ("t0", p), n=n, wait_for=("pv0", p - 2) if p >= 2 else None)
                if p:
                    beside0(p - 1)
                if p in SPLITS_BESIDE0:
                    split_through(done_halves[0])
                if p in SUB_AT:
                    sub_squares(SUB_AT.index(p))
            out0(NT * HEADS - 1)
            beside0(NT * HEADS - 1)
            sub_squares(NT - 1)
            act.wait_ge(s_powin, pow_at[("sub", NT - 2)][0] + 1)
            to_feature("turn_o0", range(NT - 1))

            def out_unit(stage, c, t):
                name = (stage, c, t)
                act.wait_ge(*finished(name))
                ps = psum[:, place[name][0], :]
                seq.note(act.activation(y_tok[:, t, c * COLS:(c + 1) * COLS], ps, ACTF.Copy).then_inc(s_a, 1), s_a)
                act.wait_ge(*seq.last)
                n0 = ss_post[(stage, t)]
                seq.freed(act.activation(sc[:, 7, :], ps, ACTF.Square, accum_out=ss[:, n0 + c:n0 + c + 1]).then_inc(bank_free(name), 1), name)

            def unit_out0(c, t):
                out_unit("out0", c, t)
                if c == 0 and t == NT - 2:
                    to_feature("turn_o0", range(NT - 1, NT))

            for c in range(2):
                run_chunk("out0", c, unit_out0)

            def norm_squares(stage, tiles, base):
                for t in range(tiles):
                    act.wait_ge(s_res, base + t + 1)
                    square_sum((stage, t), xs[:, t, :],
                               sc[:, 2 * (t % 2):2 * (t % 2) + 2, :].rearrange("p a n -> p (a n)"),
                               ss[:, ss_norm[(stage, t)]:ss_norm[(stage, t)] + 1])

            norm_squares("norm1", NT, 0)
            act.wait_ge(s_mod, 2)
            norm("norm1", 1)

            units1 = [(c, t) for c in range(3) for t in gemm_tiles("in1", c)]
            unit_no = {u: n for n, u in enumerate(units1)}

            def move_turned1(name):
                _, c, t = name
                if c < 2:
                    move(qT[:, 4 * c:4 * c + 4, tile_cols(t)], name, scale=float(P) ** -0.5)
                else:
                    move(kT[:, 0:2, tile_cols(t)], name, n=256)

            def unit1(c, t):
                n = unit_no[(c, t)]
                if n >= 2:
                    move_turned1(("turn1", *units1[n - 2]))
                name = ("in1", c, t)
                act.wait_ge(*finished(name))
                ps = psum[:, place[name][0], :]
                if n >= 2:
                    act.wait_ge(s_powin, pow_at[("qk1", *units1[n - 2])][0] + 1)
                if c == 2:
                    seq.note(act.activation(vbuf[:, t, 0:256], ps[:, 256:512], ACTF.Copy).then_inc(s_a, 1), s_a)
                w = 4 if c < 2 else 2
                square_sum(("qk1", c, t), ps[:, 0:w * P], sc[:, 5 + n % 2, 0:w * P])

            for c in range(3):
                run_chunk("in1", c, unit1)
            for u in units1[-2:]:
                move_turned1(("turn1", *u))

            def exp1(p):
                act.wait_ge(s_mx, NT * HEADS + p + 1)
                if p >= 2:
                    act.wait_ge(*finished(("t1", p - 2)))
                b = place[("s1", p)][0]
                seq.freed(act.activation(sc[:, p % 2, :], psum[:, b, :], ACTF.Exp, bias=nmax[:, p % 2, 0:1],
                                             accum_out=rsum[:, p % 2, 0:1]).then_inc(bank_free(("s1", p)), 1), ("s1", p))

            exp1(0)
            z_units1 = [(c, t) for c in (3, 4) for t in range(XT)]
            for p in range(XT * HEADS):
                if p + 1 < XT * HEADS:
                    if p >= 1:
                        act.wait_ge(s_rinv, p)
                    exp1(p + 1)
                move(sc[:, 6 + p % 2, :], ("t1", p), wait_for=("pv1", p - 2) if p >= 2 else None)
                if p % 4 == 3:
                    c, t = z_units1[p // 4]
                    tanh_half(zbuf[:, t, (c - 3) * COLS:(c - 2) * COLS], ("in1", c, t))
                if p == 6:
                    split_through(z_first1 + 3)
                if p == 8:
                    split_through(z_first1 + 4)
            split_through(half_no[("out1", 0, 0)] + 2)
            to_feature("turn_o1", XT)
            for c in range(2):
                run_chunk("out1", c, lambda c, t: out_unit("out1", c, t))
            norm_squares("norm2", XT, NT)
            norm("norm2")

            def unit2(c, t):
                name = ("in2", c, t)
                ps = psum[:, place[name][0], :]
                if c == 0:
                    act.wait_ge(*finished(name))
                    square_sum(("qa", t), ps, sc[:, 5 + t, :])
                elif c == 1:
                    act.wait_ge(*finished(name))
                    seq.note(act.activation(iq[:, t, :], ps[:, 128:256], ACTF.Copy).then_inc(s_a, 1), s_a)
                    seq.note(act.activation(ik4[:, t, :].rearrange("p (r d) -> p r d", r=4),
                                             ps[:, 256:288].unsqueeze(1).broadcast_to((P, 4, 32)), ACTF.Copy).then_inc(s_a, 1), s_a)
                    seq.note(act.activation(iw[:, t, :], ps[:, 288:292], ACTF.Copy, scale=0.5).then_inc(s_a, 1), s_a)
                    square_sum(("lat", t), ps[:, 0:P], z_flat[:, 0:P], ss[:, ss_lat + t:ss_lat + t + 1])
                elif c == 2:
                    move(qaT[:, :, tile_cols(t)], ("turn_qa", t), scale=0.125)
                elif c == 3:
                    for u in range(XT if t == 0 else 0):
                        nm = ("turn_c", u)
                        act.wait_ge(*finished(nm))
                        tp = psum[:, place[nm][0], :]
                        seq.note(act.activation(cT[:, tile_cols(u)], tp[:, 0:P], ACTF.Copy,
                                                 scale=cols[:, C_KV:C_KV + 1]).then_inc(s_a, 1), s_a)
                        seq.note(act.activation(iqT[:, tile_cols(u)], tp[:, P:2 * P], ACTF.Copy).then_inc(s_a, 1), s_a)
                        seq.freed(act.activation(ikT[:, tile_cols(u)], tp[:, 2 * P:3 * P], ACTF.Copy).then_inc(bank_free(nm), 1), nm)
                elif c == 4:
                    nm = ("latent", t)
                    act.wait_ge(*finished(nm))
                    square_sum(("ka", t), psum[:, place[nm][0], 0:64], z_flat[:, 0:64], ss[:, ss_ka + t:ss_ka + t + 1])
                    move(qbT[:, :, tile_cols(t)], ("turn_qb", t))
                    move(vb[:, t, :], name)
                else:
                    move(kaT[:, tile_cols(t)], ("turn_ka", t), n=P)
                    move(kbT[:, :, tile_cols(t)], ("turn_kb", t), scale=0.125)
                    tanh_half(gb[:, t, :], name)

            for c in range(6):
                run_chunk("in2", c, unit2)
            for t in range(XT):
                for i in range(4):
                    nm = ("idx", t, i)
                    act.wait_ge(*finished(nm))
                    seq.freed(act.activation(sc[:, 2 * t + i // 2, (i % 2) * 256:(i % 2) * 256 + 256],
                                                 psum[:, place[nm][0], 0:256], ACTF.Relu, scale=32.0 ** -0.5).then_inc(bank_free(nm), 1), nm)
            for t in range(XT):
                act.wait_ge(s_yc, t + 1)
                square_sum(("gn", t), sc[:, 4 + t, :], sc[:, 2 + t, :])
            for p in range(8):
                act.wait_ge(s_mx, (NT + XT) * HEADS + p + 1)
                for e in range(2):
                    v = sc[:, p % 2, 256 * e:256 * e + 256]
                    seq.note(act.activation(v, v, ACTF.Exp, bias=nmax[:, p % 2, e:e + 1],
                                             accum_out=rsum[:, p % 2, e:e + 1]).then_inc(s_ex if e else s_a, 1), s_ex if e else s_a)
                move(sc[:, 2 + p % 2, :], ("t2", p), wait_for=("pv2", p - 2) if p >= 2 else None)
            to_feature("turn_o2", XT)
            for c in range(2):
                run_chunk("out2", c, lambda c, t: None)
            for t in range(XT):
                act.wait_ge(*moved(("out2", 0, t)))
                act.wait_ge(*moved(("out2", 1, t)))
                square_sum(("norm3", t), xs[:, t, :],
                           sc[:, 2 * (t % 2):2 * (t % 2) + 2, :].rearrange("p a n -> p (a n)"),
                           ss[:, ss_norm[("norm3", t)]:ss_norm[("norm3", t)] + 1])
            norm("norm3")
            n_tanh = [0]

            def gate_tanh(j, t):
                act.wait_ge(*finished(("gu", j, t)))
                if j:
                    act.wait_ge(*moved(("gu", j - 1, t)))
                seq.note(act.activation(sc[:, t, 0:256], psum[:, 4 + t, 0:256], ACTF.Tanh, scale=0.5).then_inc(s_tanh, 1), s_tanh)

            def hidden_hi(j):
                for t in range(XT):
                    act.wait_ge(*finished(("turn_h", j, t)))
                    if j >= 2:
                        act.wait_ge(*released[half_no[("down", j - 2, 0)]])
                    ps = psum[:, 6 + t, 0:256].rearrange("p (k n) -> p k n", k=2)
                    k = 2 * (j % 2)
                    seq.note(act.activation(act_hi[:, k:k + 2, tile_cols(XT + t)], ps, ACTF.Copy).then_inc(s_h, 1), s_h)

            for j in range(FFN_STEPS):
                gate_tanh(j, 0)
                if j:
                    hidden_hi(j - 1)
                split_through(half_no.get(("gu", j + 1, 0), 0))
                gate_tanh(j, 1)
                split_through(half_no.get(("gu", j + 1, 1), 0))
                split_through(half_no[("down", j, 0)])
            hidden_hi(FFN_STEPS - 1)

        @block.gpsimd
        def _(pool):
            seq = Sequence(moved)
            seq.note(pool.memset(half_neg[:], -0.5).then_inc(s_g, 1), s_g)
            pool.memset(zero[:], 0.0).then_inc(s_half, 1)
            for dst, src in ((sel[:], a["k_sel"]), (rope_a[:], a["k_rope_a"]),
                             (lamb[:], a["a_lambda"][0].partition_broadcast(P)),
                             (gate0[:, 1, :], a["post_g"][0].partition_broadcast(P)),
                             (subln[:], a["a_subln_g"][0].partition_broadcast(P)),
                             (rope_b[:], a["k_rope_b"]), (rope_c[:], a["k_rope_c"]),
                             (qk_g[:], a["b_qk_g"][0].partition_broadcast(P)),
                             (qkn2[:, 0, :], a["q_norm_w_2"][0].partition_broadcast(P)),
                             (qkn2[:, 1, :], a["k_norm_w_2"][0].partition_broadcast(P)),
                             (w_ukv[:, 0, :], a["w_uk_2"][0]), (w_ukv[:, 1, :], a["w_uv_2"][0]),
                             (relb[:], a["rel_bias_2"])):
                pool.dma_start(dst, src).then_inc(s_par, 16)
            pool.wait_ge(s_half, 1)
            n_pows = [0]

            def powers_through(key):
                while n_pows[0] <= pow_at[key][0]:
                    n, w = pows[n_pows[0]]
                    pool.wait_ge(s_powin, n_pows[0] + 1)
                    seq.note(pool.tensor_tensor(rstd[:, n:n + w], ms[:, n:n + w], half_neg[:, 0:w], ALU.pow).then_inc(s_powout, 1), s_powout)
                    n_pows[0] += 1

            powers_through(("norm0", NT - 1))
            for t in range(NT):
                pool.wait_ge(*moved(("in0", 6, t)))
                pool.wait_ge(*moved(("in0", 7, t)))
                z = zbuf[:, t, :].rearrange("p (h d) -> p h d", d=P)
                seq.note(pool.tensor_tensor(z, z, subln[:].unsqueeze(1).broadcast_to((P, HEADS, P)), ALU.mult).then_inc(s_zg, 1), s_zg)
            for t in range(NT):
                powers_through(("sub", t))
                n = pow_at[("sub", t)][1]
                o = qT[:, :, tile_cols(t)]
                pool.wait_ge(*seq.last)
                seq.note(pool.tensor_tensor(o, o, rstd[:, n:n + HEADS].unsqueeze(2).broadcast_to((P, HEADS, P)), ALU.mult).then_inc(s_og, 1), s_og)
            powers_through(("norm3", XT - 1))

        @block.vector
        def _(dve):
            seq = Sequence(moved)
            done_halves = [0]

            def split_through(g):
                while done_halves[0] <= min(g, len(halves) - 1):
                    n = done_halves[0]
                    r = slice(0, half_size(n))
                    dve.wait_ge(s_whi, n + 1)
                    seq.note(dve.tensor_tensor(w_lo[:, n % RING, r], raw[:, n % RING, r],
                                                w_hi[:, n % RING, r].bitcast(F32), ALU.subtract).then_inc(s_wlo, 1), s_wlo)
                    done_halves[0] += 1

            def run_chunk(stage, c, unit):
                g0 = half_no[(stage, c, 0)]
                tiles = gemm_tiles(stage, c)
                for t in tiles:
                    if t == tiles[-1]:
                        split_through(g0 + 3)
                    unit(c, t)
                split_through(g0 + 4)

            def free_bank(name):
                dve.wait_ge(*seq.last)
                seq.freed(dve.tensor_copy(ss[0:1, 255:256], psum[0:1, place[name][0], 0:1]).then_inc(bank_free(name), 1), name)

            def mean_power(key, sums, width, scale, eps=EPS):
                i, n, w = pow_at[key]
                assert i == seq.count.get(s_powin.name, 0) and w == width, key
                seq.note(dve.tensor_scalar(ms[:, n:n + w], sums, scale, eps, ALU.mult, ALU.add).then_inc(s_powin, 1), s_powin)

            def rs(key):
                i, n, w = pow_at[key]
                dve.wait_ge(s_powout, i + 1)
                return rstd[:, n:n + w]

            def squares(name):
                dve.wait_ge(s_sq, sq_no[name] + 1)

            def norm_in(stage):
                tiles = norm_tiles[stage]
                for t in range(tiles):
                    squares((stage, t))
                    n0 = ss_norm[(stage, t)]
                    mean_power((stage, t), ss[:, n0:n0 + 1], 1, 1.0 / D)
                for t in range(tiles):
                    assert seq.count.get(s_xn.name, 0) == xn_base[stage] + t
                    seq.note(dve.tensor_scalar(xn[:, t, :], xs[:, t, :], rs((stage, t)), None, ALU.mult).then_inc(s_xn, 1), s_xn)

            def norm_lo(stage):
                tiles = norm_tiles[stage]
                if before_act[stage]:
                    dve.wait_ge(*finished(last_unit(before_act[stage])))
                for k in range(KT):
                    dve.wait_ge(s_h, h_base[stage] + k + 1)
                    r = slice(0, tiles * P)
                    seq.note(dve.tensor_tensor(act_lo[:, k, r], sc[:, 5 + k % 2, r], act_hi[:, k, r].bitcast(F32),
                                                ALU.subtract).then_inc(s_act, 1), s_act)

            def to_feature(stage, tiles):
                dve.wait_ge(*finished(last_unit(before_act[stage])))
                for t in (range(tiles) if isinstance(tiles, int) else tiles):
                    for h in range(2):
                        name = (stage, t, h)
                        dve.wait_ge(s_h, h_base[stage] + 2 * t + h + 1)
                        ps = psum[:, place[name][0], :].rearrange("p (k n) -> p k n", k=HALF_KT)
                        r = slice(h * HALF_KT, (h + 1) * HALF_KT)
                        seq.freed(dve.tensor_tensor(act_lo[:, r, tile_cols(t)], ps,
                                                        act_hi[:, r, tile_cols(t)].bitcast(F32), ALU.subtract).then_inc(bank_free(name), 1), name)

            def rope(src, table, heads, half, dst, src_name=None, on_done=None):
                def v(ap):
                    return ap[:, 0:heads * 2 * half].rearrange("p (h s d) -> p h s d", h=heads, s=2)
                cos, sin = table
                full_cos = cos.unsqueeze(1).unsqueeze(1).broadcast_to((P, heads, 2, half))
                one_sin = sin.unsqueeze(1).broadcast_to((P, heads, half))
                x, ta, tb, o = v(src), v(sc[:, 3, :]), v(sc[:, 4, :]), v(dst)
                dve.wait_ge(*seq.last)
                seq.note(dve.tensor_tensor(ta, x, full_cos, ALU.mult).then_inc(s_v, 1), s_v)
                seq.note(dve.tensor_tensor(tb[:, :, 0, :], x[:, :, 1, :], one_sin, ALU.mult).then_inc(s_v, 1), s_v)
                ins = dve.tensor_tensor(tb[:, :, 1, :], x[:, :, 0, :], one_sin, ALU.mult)
                if src_name:
                    seq.freed(ins.then_inc(bank_free(src_name), 1), src_name)
                else:
                    seq.note(ins.then_inc(s_v, 1), s_v)
                dve.wait_ge(*seq.last)
                seq.note(dve.tensor_tensor(o[:, :, 0, :], ta[:, :, 0, :], tb[:, :, 0, :], ALU.subtract).then_inc(s_v, 1), s_v)
                seq.note(dve.tensor_tensor(o[:, :, 1, :], ta[:, :, 1, :], tb[:, :, 1, :], ALU.add).then_inc(s_rot, 1), s_rot)

            def rot_free(name):
                n = rot_no[name]
                assert seq.count.get(s_rot.name, 0) == n, name
                if n >= 3:
                    dve.wait_ge(*finished(rot_units[n - 3]))

            dve.wait_ge(s_silu, 1)
            seq.note(dve.scalar_tensor_tensor(out=silu_t[:, 1, :], in0=silu_t[:, 1, :], scalar=1.0,
                                               in1=silu_t[:, 0, :], op0=ALU.add, op1=ALU.mult).then_inc(s_v, 1), s_v)
            dve.wait_ge(*seq.last)
            seq.note(dve.tensor_scalar(vecs[0:16, :], silu_t[:, 1, :], 0.5, None, ALU.mult).then_inc(s_silu_v, 1), s_silu_v)
            dve.wait_ge(*finished(("cols",)))
            seq.freed(dve.tensor_copy(cols[:, 0:N_COLS], psum[:, place[("cols",)][0], 0:N_COLS]).then_inc(bank_free(("cols",)), 1), ("cols",))
            dve.wait_ge(*seq.last)
            seq.note(dve.tensor_copy(c_hi[:], cols[:, 0:16]).then_inc(s_v, 1), s_v)
            dve.wait_ge(*seq.last)
            seq.note(dve.tensor_tensor(c_lo[:], cols[:, 0:16], c_hi[:].bitcast(F32), ALU.subtract).then_inc(s_v, 1), s_v)
            dve.wait_ge(*seq.last)
            for g in range(4):
                src = (c_hi[:].bitcast(F32) if g < 2 else c_lo[:])[:, 8 * (g % 2):8 * (g % 2) + 8]
                seq.note(dve.tensor_copy(cstat[:, :, 32 * g:32 * g + 32], src.unsqueeze(2).broadcast_to((P, KT, 32))).then_inc(s_cst if g == 3 else s_v, 1), s_cst if g == 3 else s_v)
            split_through(2)
            norm_in("norm0")
            dve.wait_ge(s_par, 16 * N_PAR)
            pairs = lamb[:].rearrange("p (a b) d -> p a b d", a=2)
            prod = sc[:, 7, 0:128].rearrange("p (a d) -> p a d", a=2)
            seq.note(dve.tensor_tensor(prod, pairs[:, :, 0, :], pairs[:, :, 1, :], ALU.mult).then_inc(s_v, 1), s_v)
            dve.wait_ge(*seq.last)
            seq.note(dve.tensor_reduce(lam_s[:, 0:2], prod, AX_X, ALU.add).then_inc(s_lamin, 1), s_lamin)

            def mod_sums(l):
                nm = (f"mod{l}",)
                dve.wait_ge(*finished(nm))
                ps = psum[:, place[nm][0], 0:32].rearrange("p (w k s) -> p w k s", w=2, k=KT)
                b = cols[:, C_ADAB + 24 * l:C_ADAB + 24 * l + 16].rearrange("p (w k) -> p w k", w=2)
                for w in range(2):
                    ins = dve.tensor_tensor(mod[:, l, 1 - w], ps[:, w], b[:, w].unsqueeze(2).broadcast_to((P, KT, 2)), ALU.add)
                    if w:
                        seq.freed(ins.then_inc(bank_free(nm), 1), nm)
                    else:
                        seq.note(ins.then_inc(s_v, 1), s_v)
                dve.wait_ge(*seq.last)
                g = cols[:, C_PRE + 8 * l:C_PRE + 8 * l + 8].unsqueeze(2).broadcast_to((P, KT, 2))
                seq.note(dve.scalar_tensor_tensor(out=mod[:, l, 0], in0=mod[:, l, 0], scalar=1.0, in1=g,
                                                   op0=ALU.add, op1=ALU.mult).then_inc(s_mod, 1), s_mod)

            for c in range(4):
                run_chunk("ada0", c, lambda c, t: None)
            mod_sums(0)
            dve.wait_ge(s_lamout, 1)
            neg_lambda = lam_s[:, 4:5]
            seq.note(dve.tensor_scalar(neg_lambda, lam_s[:, 3:4], LAMBDA_INIT, lam_s[:, 2:3], ALU.subtract,
                                        ALU.subtract).then_inc(s_v, 1), s_v)
            norm_lo("norm0")

            def unit0(c, t):
                name = ("in0", c, t)
                if c < 4:
                    dve.wait_ge(*finished(name))
                    ps = psum[:, place[name][0], :]
                    rot_free(("turn0", c, t))
                    if t < XT:
                        rope(ps, (rope_a[:, 0, t, :], rope_a[:, 1, t, :]), 8, 32, rot_buf(("turn0", c, t)), name)
                    else:
                        seq.note(dve.tensor_copy(rot_buf(("turn0", c, t)), ps).then_inc(s_rot, 1), s_rot)
                        free_bank(name)

            for c in range(6):
                run_chunk("in0", c, unit0)

            def max0(p):
                n = NT * P if p < XT * HEADS else XT * P
                dve.wait_ge(*finished(("s0", p, 0)))
                dve.wait_ge(*finished(("s0", p, 1)))
                b = place[("s0", p, 0)][0]
                seq.note(dve.tensor_reduce(nmax[:, p % 2, :], psum[:, b:b + 2, 0:n], AX_X, ALU.max, negate=True).then_inc(s_mx, 1), s_mx)

            def comb0(p):
                n = NT * P if p < XT * HEADS else XT * P
                dve.wait_ge(*moved(("s0", p, 0)))
                dve.wait_ge(*moved(("s0", p, 1)))
                r = rinv[:, p % 2, :]
                if p >= 2:
                    dve.wait_ge(*moved(("pv0", p - 2)))
                seq.note(dve.reciprocal(r[:, 0:2], rsum[:, p % 2, :]).then_inc(s_v, 1), s_v)
                dve.wait_ge(*seq.last)
                seq.note(dve.scalar_tensor_tensor(out=r[:, 2:3], in0=r[:, 1:2], scalar=neg_lambda,
                                                   in1=rsum[:, p % 2, 0:1], op0=ALU.mult, op1=ALU.mult).then_inc(s_v, 1), s_v)
                dve.wait_ge(*seq.last)
                if p >= 2:
                    dve.wait_ge(*finished(("t0", p - 2)))
                seq.note(dve.scalar_tensor_tensor(out=sc[:, 4 + p % 2, 0:n], in0=sc[:, 2 * (p % 2) + 1, 0:n],
                                                   scalar=r[:, 2:3], in1=sc[:, 2 * (p % 2), 0:n],
                                                   op0=ALU.mult, op1=ALU.add).then_inc(s_comb, 1), s_comb)

            def gate_z(dst, name):
                dve.wait_ge(s_tanh, n_tanh[0] + 1)
                n_tanh[0] += 1
                seq.freed(dve.scalar_tensor_tensor(out=dst, in0=dst, scalar=1.0, in1=psum[:, place[name][0], :],
                                                       op0=ALU.add, op1=ALU.mult).then_inc(bank_free(name), 1), name)

            n_tanh = [0]
            def sub_mean(t):
                squares(("sub", t))
                n0 = 32 + 8 * t
                src = squares0[:, t] if t < NT - 1 else sc[:, 0:2, :].rearrange("p a (h d) -> p (a h) d", d=P)
                seq.note(dve.tensor_reduce(ss[:, n0:n0 + 8], src, AX_X, ALU.add).then_inc(s_v, 1), s_v)
                dve.wait_ge(*seq.last)
                mean_power(("sub", t), ss[:, n0:n0 + 8], 8, 1.0 / P)

            def gated0(t):
                dve.wait_ge(s_zg, t + 1)
                dve.wait_ge(s_og, t + 1)
                z = zbuf[:, t, :].rearrange("p (h d) -> p h d", d=P)
                seq.note(dve.scalar_tensor_tensor(out=z, in0=qT[:, :, tile_cols(t)], scalar=0.5 * (1.0 - LAMBDA_INIT), in1=z,
                                                   op0=ALU.mult, op1=ALU.mult).then_inc(s_tok, 1), s_tok)

            max0(0)
            for p in range(NT * HEADS):
                comb0(p)
                if p + 1 < NT * HEADS:
                    max0(p + 1)
                if p >= 2:
                    stage, c, t, part = BESIDE_ATTENTION0[p - 2]
                    if stage == "in0" and part == 1:
                        gate_z(zbuf[:, t, (c - 6) * COLS:(c - 5) * COLS], (stage, c, t))
                if p - 1 in SPLITS_BESIDE0:
                    split_through(done_halves[0])
                if p - 1 in SUB_AT:
                    sub_mean(SUB_AT.index(p - 1))
                if p - 4 in SUB_AT:
                    gated0(SUB_AT.index(p - 4))
            split_through(done_halves[0])
            sub_mean(NT - 1)
            mod_sums(1)
            dve.wait_ge(*finished(("gate1", 0, 1)))
            to_feature("turn_o0", range(NT - 1))
            gated0(NT - 1)
            dve.wait_ge(s_par1, 48)
            for c in range(2):
                nm = ("gate1", 0, c)
                r = slice(c * COLS, (c + 1) * COLS)
                seq.freed(dve.tensor_tensor(gate1[:, r], psum[:, place[nm][0], :], k_flat[:, r], ALU.add).then_inc(bank_free(nm), 1), nm)
                dve.wait_ge(*seq.last)
                seq.note(dve.tensor_tensor(gate1[:, r], gate1[:, r], k_flat[:, D + c * COLS:D + (c + 1) * COLS], ALU.mult).then_inc(s_v, 1), s_v)

            def gates0():
                for c in range(2):
                    r = slice(c * COLS, (c + 1) * COLS)
                    dve.wait_ge(*finished(("gate0", 0, c)))
                    dve.wait_ge(*finished(("gate0", 1, c)))
                    for s in range(2):
                        nm = ("gate0", s, c)
                        seq.freed(dve.tensor_tensor(sc[:, 2 * c + s, :], psum[:, place[nm][0], :], k_flat[:, 2 * D + c * COLS:2 * D + (c + 1) * COLS],
                                                    ALU.add).then_inc(bank_free(nm), 1), nm)
                    for s in range(2):
                        dve.wait_ge(*seq.last)
                        seq.note(dve.tensor_tensor(gate0[:, s, r], sc[:, 2 * c + s, :], gate0[:, 1, r], ALU.mult).then_inc(s_v, 1), s_v)

            def post(l, tiles):
                stage = f"out{l}"
                for t in range(tiles):
                    dve.wait_ge(*moved((stage, 0, t)))
                    dve.wait_ge(*moved((stage, 1, t)))
                    n0 = ss_post[(stage, t)]
                    seq.note(dve.tensor_tensor(ss[:, n0:n0 + 1], ss[:, n0:n0 + 1], ss[:, n0 + 1:n0 + 2], ALU.add).then_inc(s_v, 1), s_v)
                    dve.wait_ge(*seq.last)
                    mean_power((f"post{l}", t), ss[:, n0:n0 + 1], 1, 1.0 / D)
                for t in range(tiles):
                    seq.note(dve.scalar_tensor_tensor(out=y_tok[:, t, :], in0=y_tok[:, t, :], scalar=rs((f"post{l}", t)),
                                                       in1=gate1 if l else gate0[:, t // XT, :], op0=ALU.mult, op1=ALU.mult).then_inc(s_v, 1), s_v)
                    dve.wait_ge(*seq.last)
                    seq.note(dve.tensor_tensor(xs[:, t, :], xs[:, t, :], y_tok[:, t, :], ALU.add).then_inc(s_res, 1), s_res)

            def unit_out0(c, t):
                if c == 0 and t == NT - 2:
                    to_feature("turn_o0", range(NT - 1, NT))
                if c == 1 and t == 0:
                    gates0()

            for c in range(2):
                run_chunk("out0", c, unit_out0)
            post(0, NT)
            norm_in("norm1")
            norm_lo("norm1")

            units1 = [(c, t) for c in range(3) for t in gemm_tiles("in1", c)]
            unit_no = {u: n for n, u in enumerate(units1)}

            def unit1(c, t):
                n, w = unit_no[(c, t)], 4 if c < 2 else 2
                name = ("in1", c, t)
                key = ("qk1", c, t)
                squares(key)
                n0 = 80 + 4 * n
                dve.wait_ge(*seq.last)
                seq.note(dve.tensor_reduce(ss[:, n0:n0 + w], sc[:, 5 + n % 2, 0:w * P].rearrange("p (h d) -> p h d", d=P),
                                            AX_X, ALU.add).then_inc(s_v, 1), s_v)
                dve.wait_ge(*seq.last)
                mean_power(key, ss[:, n0:n0 + w], w, 1.0 / P)
                ps = psum[:, place[name][0], 0:w * P].rearrange("p (h d) -> p h d", d=P)
                buf = sc[:, 7, 0:w * P].rearrange("p (h d) -> p h d", d=P)
                seq.freed(dve.tensor_tensor(buf, ps, rs(key).unsqueeze(2).broadcast_to((P, w, P)), ALU.mult).then_inc(bank_free(name), 1), name)
                dve.wait_ge(*seq.last)
                g = qk_g[:, 0 if c < 2 else 1, :].unsqueeze(1).broadcast_to((P, w, P))
                nm = ("turn1", c, t)
                rot_free(nm)
                if t < XT:
                    seq.note(dve.tensor_tensor(buf, buf, g, ALU.mult).then_inc(s_v, 1), s_v)
                    rope(sc[:, 7, :], (rope_b[:, 0, t, :], rope_b[:, 1, t, :]), w, 64, rot_buf(nm))
                else:
                    dst = rot_buf(nm)[:, 0:w * P].rearrange("p (h d) -> p h d", d=P)
                    seq.note(dve.tensor_tensor(dst, buf, g, ALU.mult).then_inc(s_rot, 1), s_rot)

            for c in range(3):
                run_chunk("in1", c, unit1)

            def max1(p):
                dve.wait_ge(*finished(("s1", p)))
                b = place[("s1", p)][0]
                if p >= 2:
                    dve.wait_ge(*moved(("s1", p - 2)))
                seq.note(dve.tensor_reduce(nmax[:, p % 2, 0:1], psum[:, b, :], AX_X, ALU.max, negate=True).then_inc(s_mx, 1), s_mx)

            def out1(p):
                t, h = divmod(p, HEADS)
                dve.wait_ge(*finished(("pv1", p)))
                seq.freed(dve.tensor_scalar(qT[:, h, tile_cols(t)], psum[:, 7, 0:P], rinv[:, p % 2, 0:1], None,
                                                ALU.mult).then_inc(bank_free(("pv1", p)), 1), ("pv1", p))

            z_units1 = [(c, t) for c in (3, 4) for t in range(XT)]
            dve.wait_ge(*seq.last)
            max1(0)
            for p in range(XT * HEADS):
                if p + 1 < XT * HEADS:
                    max1(p + 1)
                dve.wait_ge(*moved(("s1", p)))
                dve.wait_ge(*seq.last)
                seq.note(dve.reciprocal(rinv[:, p % 2, 0:1], rsum[:, p % 2, 0:1]).then_inc(s_rinv, 1), s_rinv)
                if p:
                    out1(p - 1)
                if p % 4 == 3:
                    c, t = z_units1[p // 4]
                    gate_z(zbuf[:, t, (c - 3) * COLS:(c - 2) * COLS], ("in1", c, t))
                if p == 6:
                    split_through(z_first1 + 3)
                if p == 8:
                    split_through(z_first1 + 4)
            out1(XT * HEADS - 1)
            dve.wait_ge(*seq.last)
            for t in range(XT):
                z = zbuf[:, t, :].rearrange("p (h d) -> p h d", d=P)
                seq.note(dve.scalar_tensor_tensor(out=z, in0=qT[:, :, tile_cols(t)], scalar=0.5, in1=z,
                                                   op0=ALU.mult, op1=ALU.mult).then_inc(s_tok, 1), s_tok)
            split_through(half_no[("out1", 0, 0)] + 2)
            to_feature("turn_o1", XT)
            for c in range(2):
                run_chunk("out1", c, lambda c, t: None)
            post(1, XT)
            norm_in("norm2")
            norm_lo("norm2")

            def unit2(c, t):
                name = ("in2", c, t)
                ps = psum[:, place[name][0], :]
                if c == 0:
                    squares(("qa", t))
                    n0 = 120 + 8 * t
                    seq.note(dve.tensor_reduce(ss[:, n0:n0 + 8], sc[:, 5 + t, :].rearrange("p (h d) -> p h d", d=64),
                                                AX_X, ALU.add).then_inc(s_v, 1), s_v)
                    dve.wait_ge(*seq.last)
                    mean_power(("qa", t), ss[:, n0:n0 + 8], 8, 1.0 / 64)
                    buf = sc[:, 7, :].rearrange("p (h d) -> p h d", d=64)
                    v = ps.rearrange("p (h d) -> p h d", d=64)
                    dve.wait_ge(*seq.last)
                    seq.freed(dve.tensor_tensor(buf, v, rs(("qa", t)).unsqueeze(2).broadcast_to((P, 8, 64)), ALU.mult).then_inc(bank_free(name), 1), name)
                    dve.wait_ge(*seq.last)
                    nm = ("turn_qa", t)
                    rot_free(nm)
                    seq.note(dve.tensor_tensor(rot_buf(nm).rearrange("p (h d) -> p h d", d=64), buf,
                                                qkn2[:, 0, :].unsqueeze(1).broadcast_to((P, 8, 64)), ALU.mult).then_inc(s_rot, 1), s_rot)
                elif c == 1:
                    squares(("lat", t))
                    mean_power(("lat", t), ss[:, ss_lat + t:ss_lat + t + 1], 1, 1.0 / P)
                    seq.freed(dve.tensor_scalar(lat[:, t, :], ps[:, 0:P], rs(("lat", t)), None, ALU.mult).then_inc(bank_free(name), 1), name)
                elif c in (2, 3):
                    dve.wait_ge(*finished(name))
                    nm = ("turn_qb" if c == 2 else "turn_kb", t)
                    rot_free(nm)
                    rope(ps, (rope_c[:, 0, t, :], rope_c[:, 1, t, :]), 8, 32, rot_buf(nm), name)
                    if c == 3 and t == 0:
                        dve.wait_ge(*finished(("bias",)))
                        seq.note(dve.tensor_copy(toep, psum[0:HEADS, place[("bias",)][0], :]).then_inc(s_toep, 1), s_toep)
                        free_bank(("bias",))
                elif c == 4:
                    squares(("ka", t))
                    nm = ("latent", t)
                    lp = psum[:, place[nm][0], :]
                    mean_power(("ka", t), ss[:, ss_ka + t:ss_ka + t + 1], 1, 1.0 / 64)
                    dve.wait_ge(*finished(("turn_c", XT - 1)))
                    for e in range(2):
                        seq.note(dve.scalar_tensor_tensor(out=ka2[:, t, 64 * e:64 * e + 64], in0=lp[:, 0:64],
                                                           scalar=rs(("ka", t)), in1=qkn2[:, 1, :],
                                                           op0=ALU.mult, op1=ALU.mult).then_inc(s_v, 1), s_v)
                    dve.wait_ge(*seq.last)
                    seq.freed(dve.tensor_copy(va[:, t, :], lp[:, 64:128]).then_inc(bank_free(nm), 1), nm)
                else:
                    gate_z(gb[:, t, :], name)

            for c in range(6):
                run_chunk("in2", c, unit2)

            for t in range(XT):
                acc = score[:, t, :]
                for i in range(4):
                    dve.wait_ge(*moved(("idx", t, i)))
                    r = sc[:, 2 * t + i // 2, (i % 2) * 256:(i % 2) * 256 + 256]
                    if i:
                        dve.wait_ge(*seq.last)
                        seq.note(dve.scalar_tensor_tensor(out=acc, in0=r, scalar=iw[:, t, i:i + 1], in1=acc,
                                                           op0=ALU.mult, op1=ALU.add).then_inc(s_v, 1), s_v)
                    else:
                        seq.note(dve.tensor_scalar(acc, r, iw[:, t, 0:1], None, ALU.mult).then_inc(s_v, 1), s_v)
                dve.wait_ge(*seq.last)
                for half in range(2):
                    limit = t * P + 64 * (half + 1)
                    if limit < 256:
                        seq.note(dve.memset(score[64 * half:64 * half + 64, t, limit:256], INADMISSIBLE).then_inc(s_v, 1), s_v)
                dve.wait_ge(*seq.last)
                for _ in range(8):
                    seq.note(dve.max(best, acc).then_inc(s_v, 1), s_v)
                    dve.wait_ge(*seq.last)
                    seq.note(dve.match_replace(acc, best, acc, LOWEST).then_inc(s_v, 1), s_v)
                    dve.wait_ge(*seq.last)
                seq.note(dve.tensor_scalar(sc[:, 7, 256 * t:256 * t + 256], acc, -3.2e38, INADMISSIBLE,
                                            ALU.is_gt, ALU.mult).then_inc(s_v, 1), s_v)
            dve.wait_ge(s_par2, 16 * 4)
            for h in range(HEADS):
                nm = ("ret_s", h)
                dve.wait_ge(*finished(nm))
                if h >= 2:
                    dve.wait_ge(s_yret, h - 1)
                ps = psum[:, place[nm][0], :]
                m = sc[:, 4 + h % 2, :]
                seq.note(dve.tensor_tensor(m[:, 0:256], ps[:, 0:256], decay[:, h, :], ALU.mult).then_inc(s_v, 1), s_v)
                seq.freed(dve.tensor_tensor(m[:, 256:384], ps[:, 256:384], decay[:, h, 0:P], ALU.mult).then_inc(bank_free(nm), 1), nm)
            for t in range(XT):
                nm = ("ret_y", t)
                dve.wait_ge(*finished(("ret_y", 1)))
                y = psum[:, place[nm][0], :].rearrange("p (h d) -> p h d", d=64)
                yc = sc[:, 4 + t, :].rearrange("p (h d) -> p h d", d=64)
                n0 = 140 + 16 * t
                seq.note(dve.tensor_reduce(ss[:, n0:n0 + 8], y, AX_X, ALU.add).then_inc(s_v, 1), s_v)
                dve.wait_ge(*seq.last)
                seq.note(dve.tensor_scalar(ss[:, n0:n0 + 8], ss[:, n0:n0 + 8], 1.0 / 64, None, ALU.mult).then_inc(s_v, 1), s_v)
                dve.wait_ge(*seq.last)
                seq.note(dve.tensor_tensor(yc, y, ss[:, n0:n0 + 8].unsqueeze(2).broadcast_to((P, 8, 64)), ALU.subtract).then_inc(s_yc, 1), s_yc)
                free_bank(nm)
            for t in range(XT):
                squares(("gn", t))
                n0 = 140 + 16 * t + 8
                seq.note(dve.tensor_reduce(ss[:, n0:n0 + 8], sc[:, 2 + t, :].rearrange("p (h d) -> p h d", d=64), AX_X, ALU.add).then_inc(s_v, 1), s_v)
                dve.wait_ge(*seq.last)
                mean_power(("gn", t), ss[:, n0:n0 + 8], 8, 1.0 / 64, GN_EPS)
            for t in range(XT):
                yc = sc[:, 4 + t, :].rearrange("p (h d) -> p h d", d=64)
                flat = sc[:, 4 + t, :]
                seq.note(dve.tensor_tensor(yc, yc, rs(("gn", t)).unsqueeze(2).broadcast_to((P, 8, 64)), ALU.mult).then_inc(s_v, 1), s_v)
                dve.wait_ge(*seq.last)
                seq.note(dve.tensor_tensor(flat, flat, gn_wb[:, 0, :], ALU.mult).then_inc(s_v, 1), s_v)
                dve.wait_ge(*seq.last)
                seq.note(dve.tensor_tensor(flat, flat, gn_wb[:, 1, :], ALU.add).then_inc(s_v, 1), s_v)
                dve.wait_ge(*seq.last)
                seq.note(dve.scalar_tensor_tensor(out=mix[:, t, 512:1024], in0=flat, scalar=0.5, in1=gb[:, t, :],
                                                   op0=ALU.mult, op1=ALU.mult).then_inc(s_v, 1), s_v)
            dve.wait_ge(s_toepr, 32)

            def max2(p):
                t, hp = divmod(p, 4)
                buf = sc[:, p % 2, :]
                if p >= 2:
                    dve.wait_ge(*finished(("t2", p - 2)))
                for e in range(2):
                    nm = ("s2", p, e)
                    dve.wait_ge(*finished(nm))
                    rev = biasm[:, t, 2 * hp + e, ::-1]
                    seq.freed(dve.tensor_tensor(buf[:, 256 * e:256 * e + 256], psum[:, place[nm][0], 0:256], rev,
                                                    ALU.add).then_inc(bank_free(nm), 1), nm)
                dve.wait_ge(*seq.last)
                v = buf.rearrange("p (e k) -> p e k", e=2)
                seq.note(dve.tensor_tensor(v, v, sc[:, 7, 256 * t:256 * t + 256].unsqueeze(1).broadcast_to((P, 2, 256)),
                                            ALU.add).then_inc(s_v, 1), s_v)
                dve.wait_ge(*seq.last)
                seq.note(dve.tensor_reduce(nmax[:, p % 2, :], v, AX_X, ALU.max, negate=True).then_inc(s_mx, 1), s_mx)

            def out2(p):
                t, hp = divmod(p, 4)
                dve.wait_ge(s_ex, p + 1)
                seq.note(dve.reciprocal(rinv[:, p % 2, 0:2], rsum[:, p % 2, :]).then_inc(s_v, 1), s_v)
                dve.wait_ge(*seq.last)
                dve.wait_ge(*finished(("pv2", p)))
                ps = psum[:, 7, 0:P].rearrange("p (e d) -> p e d", e=2)
                dst = mix[:, t, hp * P:(hp + 1) * P].rearrange("p (e d) -> p e d", e=2)
                ins = dve.tensor_tensor(dst, ps, rinv[:, p % 2, 0:2].unsqueeze(2).broadcast_to((P, 2, 64)), ALU.mult)
                if hp == 3:
                    seq.note(ins.then_inc(s_tok, 1), s_tok)
                    free_bank(("pv2", p))
                else:
                    seq.freed(ins.then_inc(bank_free(("pv2", p)), 1), ("pv2", p))

            max2(0)
            for p in range(8):
                if p + 1 < 8:
                    max2(p + 1)
                out2(p)
            to_feature("turn_o2", XT)

            def add_out(c, t):
                nm = ("out2", c, t)
                dve.wait_ge(*finished(nm))
                v = xs[:, t, c * COLS:(c + 1) * COLS]
                seq.freed(dve.tensor_tensor(v, v, psum[:, place[nm][0], :], ALU.add).then_inc(bank_free(nm), 1), nm)

            for c in range(2):
                run_chunk("out2", c, add_out)
            norm_in("norm3")
            norm_lo("norm3")

            def gate_up(j, t):
                nm = ("gu", j, t)
                dve.wait_ge(s_tanh, n_tanh[0] + 1)
                n_tanh[0] += 1
                th, hid = sc[:, t, 0:256], sc[:, 4 + 2 * (j % 2) + t, 0:256]
                seq.note(dve.scalar_tensor_tensor(out=sc[:, 2 + t, 0:256], in0=th, scalar=1.0, in1=psum[:, 4 + t, 0:256],
                                                   op0=ALU.add, op1=ALU.mult).then_inc(s_v, 1), s_v)
                dve.wait_ge(*seq.last)
                if j >= 2:
                    dve.wait_ge(*finished(("turn_h", j - 2, t)))
                seq.freed(dve.scalar_tensor_tensor(out=hid, in0=sc[:, 2 + t, 0:256], scalar=0.5,
                                                       in1=psum[:, 4 + t, 256:512], op0=ALU.mult, op1=ALU.mult).then_inc(bank_free(nm), 1), nm)

            def hidden_lo(j):
                for t in range(XT):
                    dve.wait_ge(s_h, h_base["hidden"] + 2 * j + t + 1)
                    ps = psum[:, 6 + t, 0:256].rearrange("p (k n) -> p k n", k=2)
                    k = 2 * (j % 2)
                    hi = act_hi[:, k:k + 2, tile_cols(XT + t)].bitcast(F32)
                    seq.freed(dve.tensor_tensor(act_lo[:, k:k + 2, tile_cols(XT + t)], ps, hi, ALU.subtract).then_inc(bank_free(("turn_h", j, t)), 1), ("turn_h", j, t))

            for j in range(FFN_STEPS):
                gate_up(j, 0)
                if j:
                    hidden_lo(j - 1)
                split_through(half_no.get(("gu", j + 1, 0), 0))
                gate_up(j, 1)
                split_through(half_no.get(("gu", j + 1, 1), 0))
                split_through(half_no[("down", j, 0)])
            hidden_lo(FFN_STEPS - 1)
            for t in range(XT):
                for c in range(2):
                    nm = ("down", t, c)
                    dve.wait_ge(*finished(nm))
                    v = xs[:, t, c * COLS:(c + 1) * COLS]
                    seq.note(dve.tensor_tensor(v, v, psum[:, place[nm][0], :], ALU.add).then_inc(s_outr, 1), s_outr)


def _constants():
    import numpy as np

    f = np.float32
    k = {"k_ident": np.eye(P, dtype=f)}
    sel = np.zeros((P, 2, P), f)
    for s in range(2):
        sel[32 * s, s, :] = 1.0
        sel[64 + 32 * s, s, :] = 1.0
    k["k_sel"] = sel
    tok = np.arange(XT * P)
    rows, cols = tok // 64, tok % 64

    def axial(head_dim):
        ax = head_dim // 2
        fr = (f(10000.0) ** (-np.arange(0, ax, 2, dtype=f) / f(ax))).astype(f)
        ang = np.concatenate([rows.astype(f)[:, None] * fr, cols.astype(f)[:, None] * fr], axis=-1).astype(f)
        return ang

    half = 32
    inv = (f(10000.0) ** (-np.arange(half, dtype=f) / f(half))).astype(f)
    for name, ang in (("k_rope_a", axial(64)), ("k_rope_b", axial(128)), ("k_rope_c", tok.astype(f)[:, None] * inv)):
        t = np.stack([np.cos(ang), np.sin(ang)]).astype(f)
        k[name] = np.ascontiguousarray(t.reshape(2, XT, P, -1).transpose(2, 0, 1, 3))
    j = np.arange(P)[:, None, None].astype(np.float64)
    i = np.arange(2 * P)[None, None, :].astype(np.float64)
    g = 1.0 - 2.0 ** (-5.0 - np.arange(HEADS))[None, :, None]
    k["k_decay"] = np.where(i >= j, g ** np.maximum(i - j, 0.0), 0.0).astype(f)
    rel = 255 - np.arange(COLS)
    n = np.abs(rel)
    large = 8 + (np.log(np.maximum(n, 1).astype(f) / f(8)) / f(math.log(16.0)) * f(8)).astype(np.int32)
    bucket = np.where(rel > 0, 16, 0) + np.where(n < 8, n, np.minimum(large, 15))
    onehot = np.zeros((32, COLS), f)
    onehot[bucket, np.arange(COLS)] = 1.0
    k["k_onehot"] = onehot
    return k


_INS = ["x", "c", "ctx", "c_ctx", "ada_w", "ada_b", "pre_g", "post_g", "w_out", "a_w_in", "a_lambda", "a_subln_g",
        "b_w_in", "b_qk_g", "norm1_w_2", "w_in_2", "q_norm_w_2", "k_norm_w_2", "kv_norm_w_2", "w_uk_2", "w_uv_2",
        "rel_bias_2", "ret_gn_w_2", "ret_gn_b_2", "w_out_2", "norm2_w_2", "w_gate_2", "w_up_2", "w_down_2"]


def kernel(**inputs):
    import numpy as _np
    import concourse.bacc as _bacc
    from concourse.bass_utils import run_bass_kernel_spmd as _run

    nc = _bacc.Bacc("TRN2", target_bir_lowering=False, num_devices=1, dynamic_dma_scratch_size=1024)
    arrays, args = {}, {}
    for name in _INS:
        arrays[f"in_{name}"] = _np.ascontiguousarray(inputs[name])
    for name, v in _constants().items():
        arrays[f"in_{name}"] = v
    for key, v in arrays.items():
        args[key[3:]] = nc.dram_tensor(key, v.shape, mybir.dt.from_np(v.dtype), kind="ExternalInput").ap()
    out = nc.dram_tensor("out_0", (1, XT * P, D), F32, kind="ExternalOutput").ap()
    block_kernel(nc, args, out)
    r = _run(nc, [arrays], core_ids=[0])
    return r.results[0]["out_0"]
```

```python
import math
from contextlib import ExitStack

import concourse.bass as bass
from concourse import mybir

F32 = mybir.dt.float32
F32R = mybir.dt.float32r
ALU = mybir.AluOpType
ACTF = mybir.ActivationFunctionType
AX_X = mybir.AxisListType.X

P = 128
D = 1024
KT = D // P
XT = 2
NT = 4
COLS = 512
HALF_KT = 4
RING = 3
HEADS = 8
FFN = 2816
FFN_COLS = 256
FFN_STEPS = FFN // FFN_COLS
EPS = 1e-6
GN_EPS = 1e-5
LAMBDA_INIT = 0.8 - 0.6 * math.exp(-0.3 * 0)
IN2 = [(512, 292), (0, 512), (804, 512), (1316, 512), (1828, 512), (2340, 512)]
LOWEST = -3.4e38
INADMISSIBLE = -3.0e38

C_SILU, C_PRE, C_N1, C_N2, C_ADAB, C_KV, N_COLS = 0, 16, 32, 40, 48, 96, 97


class Sequence:

    def __init__(self, moved):
        self.moved, self.count, self.last = moved, {}, None

    def note(self, ins, sem):
        self.count[sem.name] = self.count.get(sem.name, 0) + 1
        self.last = (sem, self.count[sem.name])

    def freed(self, ins, name):
        self.last = self.moved(name)


def halves_plan():
    plan = []
    for stage, chunks in (("ada0", 4), ("in0", 8), ("ada0g", 2), ("ada1", 6), ("out0", 2), ("in1", 5), ("out1", 2),
                          ("in2", 6), ("out2", 2)):
        plan += [(stage, c, h) for c in range(chunks) for h in range(2)]
    for j in range(FFN_STEPS):
        plan += [("gu", j, 0), ("gu", j, 1)]
        if j > 0:
            plan.append(("down", j - 1, 0))
    plan.append(("down", FFN_STEPS - 1, 0))
    return plan


GEMM_CHUNKS = {"ada0": 4, "in0": 8, "ada0g": 2, "ada1": 6, "out0": 2, "in1": 5, "out1": 2, "in2": 6, "out2": 2}


def gemm_tiles(stage, chunk):
    if stage.startswith("ada"):
        return [0]
    if stage in ("in0", "out0") or (stage, chunk) == ("in1", 2):
        return [0, 1, 2, 3]
    return [0, 1]


BESIDE_ATTENTION0 = ([("in0", c, t, part) for c in (6, 7) for t in range(NT) for part in range(2)]
                     + [("ada0g", c, 0, part) for c in range(2) for part in range(2)]
                     + [("ada1", c, 0, part) for c in range(6) for part in range(2)])
SUB_AT = [18, 20, 26]
SPLITS_BESIDE0 = [7, 9] + list(range(15, NT * HEADS))


def banks_plan():
    order = {b: [] for b in range(8)}
    place = {}

    def put(name, bank):
        place[name] = (bank, len(order[bank]))
        order[bank].append(name)

    turn = [0]

    def gemm_unit(stage, c, t):
        put((stage, c, t), turn[0] % 2)
        turn[0] += 1

    def units(stage, chunks):
        for c in chunks:
            for t in gemm_tiles(stage, c):
                gemm_unit(stage, c, t)

    def norm(stage):
        for k in range(KT):
            put((stage, k), 2 + k % 4)

    def to_feature(stage, tiles):
        for t in range(tiles):
            for h in range(2):
                put((stage, t, h), 2 + (2 * t + h) % 4)

    put(("cols",), 7)
    units("ada0", range(4))
    put(("mod0",), 2)
    norm("norm0")
    units("in0", range(6))
    for c in range(4):
        for t in range(NT):
            put(("turn0", c, t), 2 + t)
    for p in range(NT * HEADS):
        put(("s0", p, 0), 2 + 2 * (p % 2))
        put(("s0", p, 1), 3 + 2 * (p % 2))
        put(("t0", p), 6)
        put(("pv0", p), 7)
    for stage, c, t, part in BESIDE_ATTENTION0:
        if part:
            gemm_unit(stage, c, t)
    put(("mod1",), 6)
    put(("gate1", 0, 0), 7)
    put(("gate1", 0, 1), 6)
    for c in range(2):
        for s in range(2):
            put(("gate0", s, c), 6 + s)
    to_feature("turn_o0", NT)
    units("out0", range(2))
    norm("norm1")
    units("in1", range(3))
    for c in range(3):
        for t in gemm_tiles("in1", c):
            put(("turn1", c, t), 2 + t)
    for p in range(XT * HEADS):
        put(("s1", p), 2 + p % 2)
        put(("t1", p), 6)
        put(("pv1", p), 7)
    units("in1", range(3, 5))
    to_feature("turn_o1", XT)
    units("out1", range(2))
    norm("norm2")
    units("in2", range(6))
    for t in range(XT):
        put(("turn_c", t), 4 + t)
    for t in range(XT):
        for i in range(4):
            put(("idx", t, i), 2 + i)
    for t in range(XT):
        put(("latent", t), 6 + t)
        put(("turn_qa", t), 2 + t)
    put(("bias",), 5)
    for t in range(XT):
        put(("turn_ka", t), 6 + t)
        put(("turn_qb", t), 2 + t)
        put(("turn_kb", t), 4 + t)
    for t in range(XT):
        put(("ret_y", t), t)
    for h in range(HEADS):
        put(("ret_s", h), 4 + h % 2)
    for p in range(8):
        put(("s2", p, 0), 2)
        put(("s2", p, 1), 3)
        put(("t2", p), 6)
        put(("pv2", p), 7)
    to_feature("turn_o2", XT)
    units("out2", range(2))
    norm("norm3")
    for t in range(XT):
        for c in range(2):
            put(("down", t, c), 2 * t + c)
    for j in range(FFN_STEPS):
        for t in range(XT):
            put(("gu", j, t), 4 + t)
            put(("turn_h", j, t), 6 + t)
    return place


def block_kernel(nc, a, out):
    halves = halves_plan()
    half_no = {key: g for g, key in enumerate(halves)}
    place = banks_plan()

    ctx = ExitStack()
    with ctx:
        def sb(name, shape, dt=F32):
            return ctx.enter_context(nc.sbuf_tensor(name, shape, dt))

        def sem(name):
            return ctx.enter_context(nc.semaphore(name))

        xs = sb("xs", [P, NT, D])
        with ExitStack() as parts:
            act_hi = parts.enter_context(nc.sbuf_tensor("act_hi", [P, KT, NT * P], F32R))
            act_lo = parts.enter_context(nc.sbuf_tensor("act_lo", [P, KT, NT * P], F32R))
        squares0 = sb("act_hi_as_f32", [P, NT, HEADS, P])
        act_lo_f32 = sb("act_lo_as_f32", [P, NT * D])
        raw = sb("raw", [P, RING, 2048])
        w_hi = sb("w_hi", [P, RING, 2048], F32R)
        w_lo = sb("w_lo", [P, RING, 2048], F32R)
        qT = sb("qT", [P, HEADS, NT * P])
        kT = sb("kT", [P, HEADS, NT * P])
        vbuf = sb("vbuf", [P, NT, D])
        zbuf = sb("zbuf", [P, NT, D])
        gate0 = sb("gate0", [P, 2, D])
        sc = sb("sc", [P, 8, COLS])
        ident = sb("ident", [P, P])
        vecs = sb("vecs", [P, P])
        cols = sb("cols", [P, P])
        silu_t = sc[0:16, 7, 0:256].rearrange("p (a n) -> p a n", a=2)
        c_hi = sb("c_hi", [P, 16], F32R)
        c_lo = sb("c_lo", [P, 16])
        cstat = sb("cstat", [P, KT, P], F32R)
        sel = sb("sel", [P, 2, P])
        mod = sb("mod", [P, 2, 2, KT, 2])
        zero = sb("zero", [P, 1])
        rope_a = sb("rope_a", [P, 2, XT, 32])
        rope_b = sb("rope_b", [P, 2, XT, 64])
        rope_c = sb("rope_c", [P, 2, XT, 32])
        lamb = sb("lamb", [P, 4, 64])
        lam_s = sb("lam_s", [P, 8])
        subln = sb("subln", [P, P])
        qk_g = sb("qk_g", [P, 2, P])
        qkn2 = sb("qkn2", [P, 2, 64])
        w_ukv = sb("w_ukv", [P, 2, 64])
        relb = sb("relb", [32, HEADS])
        ss = sb("ss", [P, 256])
        ms = sb("ms", [P, 128])
        rstd = sb("rstd", [P, 128])
        half_neg = sb("half_neg", [P, 16])
        nmax = sb("nmax", [P, 2, 2])
        rsum = sb("rsum", [P, 2, 2])
        rinv = sb("rinv", [P, 2, 4])

        gate1 = kT[:].rearrange("p h n -> p (h n)")[:, 3 * D:4 * D]
        mrow = qT[:].rearrange("p h n -> p (h n)")[:, 0:3 * D]
        xn = zbuf
        y_tok = vbuf
        q_flat = qT[:].rearrange("p h n -> p (h n)")
        qaT = q_flat[:, 0:1024].rearrange("p (b n) -> p b n", b=4)
        qbT = q_flat[:, 1024:2048].rearrange("p (b n) -> p b n", b=4)
        kbT = q_flat[:, 2048:3072].rearrange("p (b n) -> p b n", b=4)
        kaT = q_flat[:, 3072:3328]
        iqT = q_flat[:, 3328:3584]
        ikT = q_flat[:, 3584:3840]
        cT = q_flat[:, 3840:4096]
        biasm = kT[:].rearrange("p h n -> p (h n)").rearrange("p (h t k) -> p t h k", h=HEADS, t=XT)
        v_flat = vbuf[:].rearrange("p t n -> p (t n)")
        y2 = v_flat[:, 0:2048].rearrange("p (t n) -> p t n", t=XT)
        decay = v_flat[:, 0:2048].rearrange("p (h i) -> p h i", h=HEADS)
        gn_wb = v_flat[:, 2048:3072].rearrange("p (w n) -> p w n", w=2)
        onehot = v_flat[0:32, 3072:3584]
        toep = v_flat[0:HEADS, 3584:4096]
        z_flat = zbuf[:].rearrange("p t n -> p (t n)")
        mix = z_flat[:, 0:2048].rearrange("p (t n) -> p t n", t=XT)
        gb = z_flat[:, 2048:3072].rearrange("p (t n) -> p t n", t=XT)
        vb = z_flat[:, 3072:4096].rearrange("p (t n) -> p t n", t=XT)
        score = gate0[:, 1, 0:COLS].rearrange("p (t k) -> p t k", t=XT)
        taken = gate0[:, 1, COLS:D].rearrange("p (t k) -> p t k", t=XT)
        relus = z_flat[:, 0:2048].rearrange("p (t i k) -> p t i k", t=XT, i=4)
        small = gate0[:, 0, :]
        va = small[:, 0:128].rearrange("p (t d) -> p t d", t=XT)
        iw = small[:, 128:136].rearrange("p (t h) -> p t h", t=XT)
        best = small[:, 136:144]
        lat = small[:, 144:400].rearrange("p (t n) -> p t n", t=XT)
        iq = small[:, 400:656].rearrange("p (t n) -> p t n", t=XT)
        ik4 = small[:, 656:912].rearrange("p (t n) -> p t n", t=XT)
        ka2 = lat

        psum = ctx.enter_context(nc.psum_tensor("psum", [P, 8, COLS], F32))
        toep_dram = nc.dram_tensor("toep_scratch", (HEADS, COLS), F32, kind="Internal").ap()

        landed = [sem(f"raw_landed{i}") for i in range(RING)]
        s_whi, s_wlo, s_wused = sem("w_hi_ready"), sem("w_lo_ready"), sem("w_first_half_used")
        full = [sem(f"bank{b}_full") for b in range(8)]
        free = [sem(f"bank{b}_free") for b in range(8)]
        s_v, s_a, s_g = sem("vector_seq"), sem("scalar_seq"), sem("pool_seq")
        s_cin, s_xin, s_par, s_par1, s_par2 = sem("consts_in"), sem("x_in"), sem("params_in"), sem("ada1_params_in"), sem("block2_in")
        s_cst = sem("cstat_ready")
        s_mod = sem("mod_rows_ready")
        s_silu = sem("silu_exp")
        s_silu_v = sem("silu_cols")
        s_xn, s_h, s_act = sem("xn_ready"), sem("act_hi_ready"), sem("act_ready")
        s_rot, s_attn = sem("rot_ready"), sem("attn_in_ready")
        s_mx, s_ex, s_comb, s_pt = sem("max_ready"), sem("exp_ready"), sem("probs_ready"), sem("probsT_ready")
        s_tanh, s_sq = sem("tanh_ready"), sem("square_sum_ready")
        s_powin, s_powout = sem("mean_ready"), sem("rstd_ready")
        s_tok = sem("gated_ready")
        s_rinv = sem("rinv_ready")
        s_lamin, s_lamout = sem("lambda_sums"), sem("lambda_exps")
        s_toep, s_toepw, s_toepr, s_idx = sem("toep_ready"), sem("toep_written"), sem("toep_read"), sem("idx_relu_ready")
        s_store = sem("stored")
        s_outr = sem("out_ready")
        s_yc = sem("centred")
        s_half = sem("minus_half")
        s_modx, s_psq = sem("x_modulated"), sem("product_square_sum_ready")
        s_mark, s_masked = sem("taken_ready"), sem("bias_masked")
        s_late, s_sub, s_ka = sem("late_params_in"), sem("subln_scaled"), sem("keys_normed")
        s_zg, s_og = sem("gate_branch_weighted"), sem("head_outputs_normed")
        s_res, s_yret = sem("residual_ready"), sem("retention_head_done")
        N_CIN = 8
        N_PAR, N_LATE = 3, 10
        mrow1 = act_lo_f32[:, 0:3 * D]
        mrow0g = gate0[:, 0, :]
        k_flat = kT[:].rearrange("p h n -> p (h n)")
        ss_norm = {("norm0", t): t for t in range(NT)}
        ss_norm.update({("norm1", t): 4 + t for t in range(NT)})
        ss_norm.update({("norm2", t): 8 + t for t in range(XT)})
        ss_norm.update({("norm3", t): 10 + t for t in range(XT)})
        ss_post = {("out0", t): 12 + 2 * t for t in range(NT)}
        ss_post.update({("out1", t): 20 + 2 * t for t in range(XT)})
        ss_lat, ss_ka = 24, 26

        def half_src(stage, c, h):
            rows = slice(h * HALF_KT * P, (h + 1) * HALF_KT * P)

            def cut(w, lo, n):
                return w[rows, lo:lo + n].rearrange("(k p) n -> p k n", p=P)

            if stage == "ada0g":
                return [cut(a["ada_w"][0], (4 + c) * COLS, COLS)]
            if stage in ("ada0", "ada1"):
                return [cut(a["ada_w"][int(stage[3])], c * COLS, COLS)]
            if stage == "in0":
                return [cut(a["a_w_in"][0], c * COLS, COLS)]
            if stage in ("out0", "out1"):
                return [cut(a["w_out"][int(stage[3])], c * COLS, COLS)]
            if stage == "in1":
                return [cut(a["b_w_in"][0], c * COLS, COLS)]
            if stage == "in2":
                return [cut(a["w_in_2"][0], *IN2[c])]
            if stage == "out2":
                return [cut(a["w_out_2"][0], c * COLS, COLS)]
            if stage == "gu":
                return [cut(a["w_gate_2"][0], c * FFN_COLS, FFN_COLS), cut(a["w_up_2"][0], c * FFN_COLS, FFN_COLS)]
            return [a["w_down_2"][0][c * FFN_COLS:(c + 1) * FFN_COLS, :].rearrange("(k p) n -> p k n", p=P)]

        def half_size(g):
            stage, c, _ = halves[g]
            return HALF_KT * IN2[c][1] if stage == "in2" else 2048

        def half_width(g):
            stage, c, _ = halves[g]
            return IN2[c][1] if stage == "in2" else D if stage == "down" else COLS

        def w_view(buf, g):
            n = half_width(g)
            return buf[:, g % RING, 0:half_size(g)].rearrange("p (k n) -> p k n", n=n)

        released, firsts = {}, 0
        for g, (stage, c, h) in enumerate(halves):
            if stage == "down":
                firsts += 1
                released[g] = (s_wused, firsts)
            elif h == 0:
                firsts += 1
                released[g] = (s_wused, firsts)
            else:
                key = (stage, c, 1) if stage == "gu" else (stage, c, gemm_tiles(stage, c)[-1])
                b, n = place[key]
                released[g] = (full[b], n + 1)

        landed_at, n_landed = {}, [0] * RING
        for g, (stage, c, h) in enumerate(halves):
            n_landed[g % RING] += 32 if stage == "gu" else 16
            landed_at[g] = n_landed[g % RING]

        act_base, n = {}, 0
        for stage, count in (("norm0", 8), ("turn_o0", 8), ("norm1", 8), ("turn_o1", 4), ("norm2", 8),
                             ("turn_o2", 4), ("norm3", 8), ("hidden", 2 * FFN_STEPS)):
            act_base[stage] = n
            n += count
        xn_base = {"norm0": 0, "norm1": 4, "norm2": 8, "norm3": 10}
        norm_tiles = {"norm0": NT, "norm1": NT, "norm2": XT, "norm3": XT}
        def residual_pows(l, tiles):
            order = []
            for t in range(tiles + 2):
                if t >= 2:
                    order.append(((f"norm{l + 1}", t - 2), 1))
                if t < tiles:
                    order.append(((f"post{l}", t), 1))
            return order

        pows, pow_at, n = [], {}, 0
        for key, width in ([(("norm0", t), 1) for t in range(NT)]
                           + [(("sub", t), 8) for t in range(NT)]
                           + residual_pows(0, NT)
                           + [(("qk1", c, t), 4 if c < 2 else 2) for c in range(3) for t in gemm_tiles("in1", c)]
                           + residual_pows(1, XT)
                           + [(("lat", t), 1) for t in range(XT)] + [(("qa", t), 8) for t in range(XT)]
                           + [(("ka", t), 1) for t in range(XT)]
                           + [(("gn", t), 8) for t in range(XT)] + [(("norm3", t), 1) for t in range(XT)]):
            pow_at[key] = (len(pows), n, width)
            pows.append((n, width))
            n += width
        assert n <= 128

        def bank(name, n=COLS):
            return psum[:, place[name][0], 0:n]

        block = ctx.enter_context(nc.Block())

        @block.sync
        def _(sp):
            

            def load(dst, src, s):
                sp.dma_start(dst, src).then_inc(s, 16)

            def stream(g):
                if g >= RING:
                    sp.wait_ge(s_wlo, g - RING + 1)
                n = half_width(g)
                dst = w_view(raw, g)
                parts = half_src(*halves[g])
                if len(parts) == 1:
                    sp.dma_start(dst, parts[0]).then_inc(landed[g % RING], 16)
                else:
                    for i, part in enumerate(parts):
                        sp.dma_start(dst[:, :, i * FFN_COLS:(i + 1) * FFN_COLS], part).then_inc(landed[g % RING], 16)

            load(silu_t[0:8, 0, :], a["c"].rearrange("a (k p) -> (a k) p", p=P), s_cin)
            load(silu_t[8:16, 0, :], a["c_ctx"].rearrange("(k p) -> k p", p=P), s_cin)
            load(vecs[16:32, :], a["pre_g"].rearrange("l (k p) -> (l k) p", p=P), s_cin)
            load(vecs[32:40, :], a["norm1_w_2"].rearrange("l (k p) -> (l k) p", p=P), s_cin)
            load(vecs[40:48, :], a["norm2_w_2"].rearrange("l (k p) -> (l k) p", p=P), s_cin)
            load(vecs[48:96, :], a["ada_b"].rearrange("l (k p) -> (l k) p", p=P), s_cin)
            load(vecs[96:97, :], a["kv_norm_w_2"], s_cin)
            load(ident[:], a["k_ident"], s_cin)
            for g in range(RING):
                stream(g)
            for g in range(RING, len(halves)):
                if halves[g] == ("out0", 1, 0):
                    b, n = place[("s0", NT * HEADS - 1, 1)]
                    sp.wait_ge(full[b], n + 1)
                    load(k_flat[:, 0:D], a["ada_b"][1, 2 * D:3 * D].partition_broadcast(P), s_par1)
                    load(k_flat[:, D:2 * D], a["post_g"][1].partition_broadcast(P), s_par1)
                    load(k_flat[:, 2 * D:3 * D], a["ada_b"][0, 2 * D:3 * D].partition_broadcast(P), s_par1)
                if halves[g] == ("in2", 2, 0):
                    sp.wait_ge(s_xn, xn_base["norm2"] + XT)
                    load(decay, a["k_decay"], s_par2)
                    load(gn_wb[:, 0, :], a["ret_gn_w_2"][0].partition_broadcast(P), s_par2)
                    load(gn_wb[:, 1, :], a["ret_gn_b_2"][0].partition_broadcast(P), s_par2)
                    load(onehot, a["k_onehot"], s_par2)
                if halves[g] == ("out2", 0, 0):
                    sp.wait_ge(s_toep, 1)
                    sp.dma_start(toep_dram, toep).then_inc(s_toepw, 16)
                    sp.wait_ge(s_toepw, 16)
                    for t in range(XT):
                        band = bass.AP(toep_dram.tensor, t * P, [[1, P], [COLS, HEADS], [1, 256]])
                        load(biasm[:, t], band, s_toepr)
                stream(g)
            for t in range(XT):
                sp.wait_ge(s_outr, 2 * (t + 1))
                sp.dma_start(out[0, t * P:(t + 1) * P, :], xs[:, t, :]).then_inc(s_store, 16)
            sp.wait_ge(s_store, 16 * XT)


        def bank_full(name):
            return full[place[name][0]]

        def bank_free(name):
            return free[place[name][0]]

        def finished(name):
            b, n = place[name]
            return full[b], n + 1

        def moved(name):
            b, n = place[name]
            return free[b], n + 1

        def tile_cols(t, n=1):
            return slice(t * P, (t + n) * P)

        def last_unit(stage):
            c = GEMM_CHUNKS[stage] - 1
            return (stage, c, gemm_tiles(stage, c)[-1])

        NORM_COLS = {"norm2": C_N1, "norm3": C_N2}
        h_base, n = {}, 0
        for stage, count in (("norm0", 8), ("turn_o0", 8), ("norm1", 8), ("turn_o1", 4), ("norm2", 8),
                             ("turn_o2", 4), ("norm3", 8), ("hidden", 2 * FFN_STEPS)):
            h_base[stage] = n
            n += count
        act_base = {"norm0": 0, "norm1": 8}
        act_of = {"in0": "norm0", "out0": "turn_o0", "in1": "norm1", "out1": "turn_o1", "in2": "norm2",
                  "out2": "turn_o2", "gu": "norm3"}
        tok_base = {"turn_o0": 0, "turn_o1": NT, "turn_o2": NT + XT}
        before_act = {"norm0": None, "turn_o0": "in0", "norm1": "out0", "turn_o1": "in1", "norm2": "out1",
                      "turn_o2": "in2", "norm3": "out2"}
        rot_units = ([("turn0", c, t) for c in range(4) for t in range(NT)]
                     + [("turn1", c, t) for c in range(3) for t in gemm_tiles("in1", c)]
                     + [("turn_qa", t) for t in range(XT)] + [("turn_qb", t) for t in range(XT)]
                     + [("turn_kb", t) for t in range(XT)])
        rot_no = {name: n for n, name in enumerate(rot_units)}

        def rot_buf(name):
            return sc[:, rot_no[name] % 3, :]

        z_first0, z_first1 = half_no[("in0", 6, 0)], half_no[("in1", 3, 0)]
        sq_order = ([("norm0", t) for t in range(NT)] + [("sub", t) for t in range(NT)]
                    + [("norm1", t) for t in range(NT)]
                    + [("qk1", c, t) for c in range(3) for t in gemm_tiles("in1", c)]
                    + [("norm2", t) for t in range(XT)] + [("lat", t) for t in range(XT)]
                    + [("qa", t) for t in range(XT)] + [("ka", t) for t in range(XT)]
                    + [("gn", t) for t in range(XT)] + [("norm3", t) for t in range(XT)])
        sq_no = {name: n for n, name in enumerate(sq_order)}

        @block.tensor
        def _(pe):
            

            def begin(name):
                b, n = place[name]
                if n:
                    pe.wait_ge(free[b], n)
                return psum[:, b, :]

            def act_ready(stage, c, t, k):
                src = act_of[stage]
                if c:
                    return
                if src in act_base:
                    if t == 0:
                        pe.wait_ge(s_act, act_base[src] + k + 1)
                elif src in NORM_COLS:
                    if t == 0:
                        pe.wait_ge(*moved((src, k)))
                elif k % HALF_KT == 0:
                    pe.wait_ge(*moved((src, t, k // HALF_KT)))

            def gemm_unit(stage, c, t, parts=(0, 1)):
                name = (stage, c, t)
                o = begin(name) if parts[0] == 0 else psum[:, place[name][0], :]
                g0 = half_no[(stage, c, 0)]
                n = half_width(g0)
                for h in parts:
                    pe.wait_ge(s_wlo, g0 + h + 1)
                    hi, lo = w_view(w_hi, g0 + h), w_view(w_lo, g0 + h)
                    for kk in range(HALF_KT):
                        k = h * HALF_KT + kk
                        act_ready(stage, c, t, k)
                        x_hi, x_lo = act_hi[:, k, tile_cols(t)], act_lo[:, k, tile_cols(t)]
                        pe.matmul(o[:, 0:n], x_hi, hi[:, kk, :], start=(k == 0), stop=False)
                        pe.matmul(o[:, 0:n], x_hi, lo[:, kk, :], start=False, stop=False)
                        mm = pe.matmul(o[:, 0:n], x_lo, hi[:, kk, :], start=False, stop=(k == KT - 1))
                    if h == 0 and t == (gemm_tiles(stage, c)[-1] if stage != "gu" else XT - 1):
                        mm.then_inc(s_wused, 1)
                if parts[-1] == 1:
                    mm.then_inc(bank_full(name), 1)

            def ada_half(stage, c, h):
                name = (stage, c, 0)
                o = psum[:, place[name][0], :] if h else begin(name)
                g = half_no[(stage, c, h)]
                pe.wait_ge(s_wlo, g + 1)
                hi, lo = w_view(w_hi, g), w_view(w_lo, g)
                for kk in range(HALF_KT):
                    k = h * HALF_KT + kk
                    pe.matmul(o, cstat[:, k, :], hi[:, kk, :], start=(k == 0), stop=False)
                    mm = pe.matmul(o, cstat[:, k, :], lo[:, kk, :], start=False, stop=(k == KT - 1))
                if h == 0:
                    mm.then_inc(s_wused, 1)
                else:
                    mm.then_inc(bank_full(name), 1)

            def mod_columns(l):
                rows = mrow if l == 0 else mrow1
                for c in range(4):
                    pe.wait_ge(*moved((f"ada{l}", c, 0)))
                o = begin((f"mod{l}",))
                for blk in range(2 * KT):
                    mm = pe.matmul(o[:, 2 * blk:2 * blk + 2], rows[:, blk * P:(blk + 1) * P], sel[:, :, 0],
                                   start=True, stop=True)
                mm.then_inc(bank_full((f"mod{l}",)), 1)

            def gate_row(l, s, c):
                rows = mrow1[:, 2 * D:3 * D] if l else mrow0g
                pe.wait_ge(*moved(("ada1", 4 + c, 0) if l else ("ada0g", c, 0)))
                name = (f"gate{l}", s, c)
                o = begin(name)
                pe.matmul(o, sel[:, s, :], rows[:, c * COLS:(c + 1) * COLS],
                          start=True, stop=True).then_inc(bank_full(name), 1)

            def norm(stage):
                for t in range(norm_tiles[stage]):
                    pe.wait_ge(s_xn, xn_base[stage] + t + 1)
                for k in range(KT):
                    o = begin((stage, k))
                    for t in range(norm_tiles[stage]):
                        mm = pe.transpose(o[:, tile_cols(t)], xn[:, t, k * P:(k + 1) * P], ident[:])
                    mm.then_inc(bank_full((stage, k)), 1)

            def to_feature(stage, tiles, src):
                for t in (range(tiles) if isinstance(tiles, int) else tiles):
                    pe.wait_ge(s_tok, tok_base[stage] + t + 1)
                    for h in range(2):
                        o = begin((stage, t, h))
                        for i in range(HALF_KT):
                            k = h * HALF_KT + i
                            mm = pe.transpose(o[:, tile_cols(i)], src[:, t, k * P:(k + 1) * P], ident[:])
                        mm.then_inc(bank_full((stage, t, h)), 1)

            def turn(name, blocks=4):
                pe.wait_ge(s_rot, rot_no[name] + 1)
                o = begin(name)
                for i in range(blocks):
                    mm = pe.transpose(o[:, tile_cols(i)], rot_buf(name)[:, tile_cols(i)], ident[:])
                mm.then_inc(bank_full(name), 1)

            def turn_probs(name, src, blocks):
                o = begin(name)
                for i in range(blocks):
                    mm = pe.transpose(o[:, tile_cols(i)], src[:, tile_cols(i)], ident[:])
                mm.then_inc(bank_full(name), 1)

            pe.wait_ge(s_cin, 16 * N_CIN)
            pe.wait_ge(s_silu_v, 1)
            o = begin(("cols",))
            pe.transpose(o[:, 0:N_COLS], vecs[0:N_COLS, :], ident[0:N_COLS, 0:N_COLS]).then_inc(bank_full(("cols",)), 1)
            pe.wait_ge(s_cst, 1)
            for c in range(4):
                for h in range(2):
                    ada_half("ada0", c, h)
            pe.wait_ge(s_par, 16 * N_PAR)
            mod_columns(0)

            norm("norm0")
            units = [(c, t) for c in range(6) for t in range(NT)]
            for n, (c, t) in enumerate(units):
                gemm_unit("in0", c, t)
                if 2 <= n < 2 + 4 * NT:
                    turn(("turn0", *units[n - 2]))
            for c in range(4):
                for t in range(NT):
                    pe.wait_ge(*moved(("turn0", c, t)))

            def scores0(p):
                t, h = divmod(p, HEADS)
                keys = slice(0, NT * P) if t < XT else slice(XT * P, NT * P)
                n = keys.stop - keys.start
                for s in range(2):
                    rows = slice(64 * s, 64 * s + 64)
                    o = begin(("s0", p, s))
                    pe.matmul(o[:, 0:n], qT[rows, h, tile_cols(t)], kT[rows, h, keys], start=True, stop=True).then_inc(bank_full(("s0", p, s)), 1)

            def values0(p):
                t, h = divmod(p, HEADS)
                blocks = NT if t < XT else XT
                pe.wait_ge(*moved(("t0", p)))
                o = begin(("pv0", p))
                probs = sc[:, 6 + p % 2, :]
                for i in range(blocks):
                    mm = pe.matmul(o[:, 0:P], probs[:, tile_cols(i)], vbuf[:, NT - blocks + i, tile_cols(h)],
                                   start=(i == 0), stop=(i == blocks - 1))
                mm.then_inc(bank_full(("pv0", p)), 1)

            for c in (4, 5):
                for t in range(NT):
                    pe.wait_ge(*moved(("in0", c, t)))
            scores0(0)
            scores0(1)
            def beside0(p):
                stage, c, t, part = BESIDE_ATTENTION0[p]
                if stage == "in0":
                    gemm_unit(stage, c, t, parts=(part,))
                else:
                    ada_half(stage, c, part)

            beside0(0)
            for p in range(NT * HEADS):
                pe.wait_ge(s_comb, p + 1)
                turn_probs(("t0", p), sc[:, 4 + p % 2, :], NT if p < XT * HEADS else XT)
                if p:
                    beside0(p)
                if p + 2 < NT * HEADS:
                    scores0(p + 2)
                values0(p)

            mod_columns(1)
            gate_row(1, 0, 0)
            gate_row(1, 0, 1)
            to_feature("turn_o0", range(NT - 1), zbuf)
            for t in range(NT):
                if t == NT - 1:
                    to_feature("turn_o0", range(NT - 1, NT), zbuf)
                gemm_unit("out0", 0, t)
                if t == 0:
                    for c in range(2):
                        gate_row(0, 0, c)
                        gate_row(0, 1, c)
            for t in range(NT):
                gemm_unit("out0", 1, t)

            norm("norm1")
            units = [(c, t) for c in range(3) for t in gemm_tiles("in1", c)]
            for n in range(len(units) + 2):
                if n < len(units):
                    gemm_unit("in1", *units[n])
                if n >= 2:
                    turn(("turn1", *units[n - 2]), 4 if units[n - 2][0] < 2 else 2)
            for c, t in units:
                pe.wait_ge(*moved(("turn1", c, t)))

            def scores1(p):
                t, h = divmod(p, HEADS)
                o = begin(("s1", p))
                pe.matmul(o, qT[:, h, tile_cols(t)], kT[:, h // 4, :], start=True, stop=True).then_inc(bank_full(("s1", p)), 1)

            def values1(p):
                t, h = divmod(p, HEADS)
                pe.wait_ge(*moved(("t1", p)))
                o = begin(("pv1", p))
                probs = sc[:, 6 + p % 2, :]
                for i in range(NT):
                    mm = pe.matmul(o[:, 0:P], probs[:, tile_cols(i)], vbuf[:, i, tile_cols(h // 4)],
                                   start=(i == 0), stop=(i == NT - 1))
                mm.then_inc(bank_full(("pv1", p)), 1)

            z_units1 = [(c, t) for c in (3, 4) for t in range(XT)]
            scores1(0)
            scores1(1)
            gemm_unit("in1", *z_units1[0], parts=(0,))
            for p in range(XT * HEADS):
                pe.wait_ge(*moved(("s1", p)))
                turn_probs(("t1", p), sc[:, p % 2, :], NT)
                if p and p % 2 == 0:
                    gemm_unit("in1", *z_units1[p // 4], parts=((p // 2) % 2,))
                if p + 2 < XT * HEADS:
                    scores1(p + 2)
                values1(p)
            to_feature("turn_o1", XT, zbuf)
            for c in range(2):
                for t in range(XT):
                    gemm_unit("out1", c, t)

            norm("norm2")

            def in2(c):
                for t in range(XT):
                    gemm_unit("in2", c, t)

            in2(0)
            gemm_unit("in2", 1, 0)
            for t in range(XT):
                pe.wait_ge(*moved(("in2", 0, t)))
                o = begin(("turn_c", t))
                for i, src in enumerate((lat, iq, ik4)):
                    mm = pe.transpose(o[:, tile_cols(i)], src[:, t, :], ident[:])
                mm.then_inc(bank_full(("turn_c", t)), 1)
            gemm_unit("in2", 1, 1)
            for t in range(XT):
                pe.wait_ge(*moved(("turn_c", t)))
            for t in range(XT):
                for i in range(4):
                    rows = slice(32 * i, 32 * i + 32)
                    o = begin(("idx", t, i))
                    pe.matmul(o[:, 0:256], iqT[rows, tile_cols(t)], ikT[rows, :], start=True, stop=True).then_inc(bank_full(("idx", t, i)), 1)
            pe.wait_ge(s_late, 16 * N_LATE)
            for t in range(XT):
                o = begin(("latent", t))
                pe.matmul(o[:, 0:P], cT[:, tile_cols(t)], w_ukv[:].rearrange("p a d -> p (a d)"),
                              start=True, stop=True).then_inc(bank_full(("latent", t)), 1)
            gemm_unit("in2", 2, 0)
            for t in range(XT):
                turn(("turn_qa", t))
            gemm_unit("in2", 2, 1)
            pe.wait_ge(s_par2, 16 * 4)
            o = begin(("bias",))
            pe.matmul(o[0:HEADS, :], relb[:], onehot, start=True, stop=True).then_inc(bank_full(("bias",)), 1)
            gemm_unit("in2", 3, 0)
            for t in range(XT):
                turn(("turn_qb", t))
            gemm_unit("in2", 3, 1)
            gemm_unit("in2", 4, 0)
            for t in range(XT):
                turn(("turn_kb", t))
                pe.wait_ge(s_ka, t + 1)
                o = begin(("turn_ka", t))
                pe.transpose(o[:, 0:P], ka2[:, t, :], ident[:]).then_inc(bank_full(("turn_ka", t)), 1)
            gemm_unit("in2", 4, 1)
            in2(5)
            for t in range(XT):
                pe.wait_ge(*moved(("turn_qb", t)))
                pe.wait_ge(*moved(("turn_kb", t)))
                pe.wait_ge(*moved(("in2", 4, t)))

            def ret_scores(h):
                rows = slice(64 * (h % 2), 64 * (h % 2) + 64)
                o = begin(("ret_s", h))
                pe.matmul(o[:, 0:256], kbT[rows, h // 2, 0:P], qbT[rows, h // 2, 0:256], start=True, stop=True)
                pe.matmul(o[:, 256:384], kbT[rows, h // 2, P:256], qbT[rows, h // 2, P:256],
                              start=True, stop=True).then_inc(bank_full(("ret_s", h)), 1)

            def ret_values(h):
                pe.wait_ge(*moved(("ret_s", h)))
                m = sc[:, 4 + h % 2, :]
                d = slice(64 * h, 64 * h + 64)
                mm = pe.matmul(y_out[0][:, d], m[:, 0:P], vb[:, 0, d], start=True, stop=True)
                if h == HEADS - 1:
                    mm.then_inc(bank_full(("ret_y", 0)), 1)
                pe.matmul(y_out[1][:, d], m[:, P:256], vb[:, 0, d], start=True, stop=False)
                mm = pe.matmul(y_out[1][:, d], m[:, 256:384], vb[:, 1, d], start=False, stop=True)
                if h == HEADS - 1:
                    mm.then_inc(bank_full(("ret_y", 1)), 1)
                else:
                    mm.then_inc(s_yret, 1)

            def scores2(p):
                t, hp = divmod(p, 4)
                for e in range(2):
                    rows = slice(64 * e, 64 * e + 64)
                    o = begin(("s2", p, e))
                    pe.matmul(o[:, 0:256], qaT[rows, hp, tile_cols(t)], kaT[rows, :], start=True, stop=True).then_inc(bank_full(("s2", p, e)), 1)

            y_out = [begin(("ret_y", t)) for t in range(XT)]
            scores2(0)
            ret_scores(0)
            ret_scores(1)
            for p in range(8):
                if p + 1 < 8:
                    scores2(p + 1)
                pe.wait_ge(s_ex, p + 1)
                turn_probs(("t2", p), sc[:, p % 2, :], 4)
                for h in (2 * p, 2 * p + 1):
                    if h < HEADS:
                        ret_values(h)
                    if h + 2 < HEADS:
                        ret_scores(h + 2)
                pe.wait_ge(*moved(("t2", p)))
                o = begin(("pv2", p))
                probs = sc[:, 2 + p % 2, :]
                for e in range(2):
                    for i in range(2):
                        mm = pe.matmul(o[:, 64 * e:64 * e + 64], probs[:, tile_cols(2 * e + i)], va[:, i, :],
                                       start=(i == 0), stop=(i == 1))
                mm.then_inc(bank_full(("pv2", p)), 1)
            to_feature("turn_o2", XT, mix)
            for c in range(2):
                for t in range(XT):
                    gemm_unit("out2", c, t)

            norm("norm3")
            down_out = {(t, c): begin(("down", t, c)) for t in range(XT) for c in range(2)}

            def turn_hidden(j):
                for t in range(XT):
                    pe.wait_ge(*moved(("gu", j, t)))
                    o = begin(("turn_h", j, t))
                    for i in range(2):
                        mm = pe.transpose(o[:, tile_cols(i)], sc[:, 4 + 2 * (j % 2) + t, tile_cols(i)], ident[:])
                    mm.then_inc(bank_full(("turn_h", j, t)), 1)

            def down(j):
                g = half_no[("down", j, 0)]
                pe.wait_ge(s_wlo, g + 1)
                hi, lo = w_view(w_hi, g), w_view(w_lo, g)
                for t in range(XT):
                    pe.wait_ge(*moved(("turn_h", j, t)))
                    for i in range(2):
                        k = 2 * (j % 2) + i
                        x_hi, x_lo = act_hi[:, k, tile_cols(XT + t)], act_lo[:, k, tile_cols(XT + t)]
                        for c in range(2):
                            w = slice(c * COLS, (c + 1) * COLS)
                            o = down_out[(t, c)]
                            last = j == FFN_STEPS - 1 and i == 1
                            pe.matmul(o, x_hi, hi[:, i, w], start=(j == 0 and i == 0), stop=False)
                            pe.matmul(o, x_hi, lo[:, i, w], start=False, stop=False)
                            mm = pe.matmul(o, x_lo, hi[:, i, w], start=False, stop=last)
                            if last:
                                mm.then_inc(bank_full(("down", t, c)), 1)
                if not last:
                    mm.then_inc(s_wused, 1)

            for j in range(FFN_STEPS):
                gemm_unit("gu", j, 0)
                if j:
                    turn_hidden(j - 1)
                gemm_unit("gu", j, 1)
                if j:
                    down(j - 1)
            turn_hidden(FFN_STEPS - 1)
            down(FFN_STEPS - 1)

        @block.scalar
        def _(act):
            seq = Sequence(moved)
            done_halves = [0]

            def split_through(g):
                while done_halves[0] <= min(g, len(halves) - 1):
                    n = done_halves[0]
                    act.wait_ge(landed[n % RING], landed_at[n])
                    if n >= RING:
                        act.wait_ge(*released[n - RING])
                    seq.note(act.activation(w_hi[:, n % RING, 0:half_size(n)], raw[:, n % RING, 0:half_size(n)],
                                             ACTF.Copy).then_inc(s_whi, 1), s_whi)
                    done_halves[0] += 1

            def run_chunk(stage, c, unit, before_norm=False):
                g0 = half_no[(stage, c, 0)]
                tiles = gemm_tiles(stage, c)
                for t in tiles:
                    if t == tiles[-1] and not before_norm:
                        split_through(g0 + 3)
                    unit(c, t)
                if not before_norm:
                    split_through(g0 + 4)

            def square_sum(name, src, dst_junk, accum=None):
                act.wait_ge(*seq.last)
                if accum is None:
                    ins = act.activation(dst_junk, src, ACTF.Square)
                else:
                    ins = act.activation(dst_junk, src, ACTF.Square, accum_out=accum)
                assert seq.count.get(s_sq.name, 0) == sq_no[name], name
                seq.note(ins.then_inc(s_sq, 1), s_sq)

            def norm_modulated(stage, l):
                for k in range(KT + 2):
                    if k < KT:
                        act.wait_ge(*finished((stage, k)))
                        if k >= 4:
                            act.wait_ge(s_act, act_base[stage] + k - 3)
                        r = slice(0, XT * P)
                        seq.note(act.activation(sc[:, 4 + k % 4, r], psum[:, place[(stage, k)][0], r], ACTF.Identity,
                                                scale=mod[:, l, 0, k, 0:1], bias=mod[:, l, 1, k, 0:1]).then_inc(s_modx, 1), s_modx)
                    if k == 2 and before_act[stage]:
                        act.wait_ge(*finished(last_unit(before_act[stage])))
                    if k >= 2:
                        act.wait_ge(*moved((stage, k - 2)))
                        seq.note(act.activation(act_hi[:, k - 2, :], sc[:, 4 + (k - 2) % 4, :], ACTF.Copy).then_inc(s_h, 1), s_h)

            def norm(stage):
                act.wait_ge(*finished(last_unit(before_act[stage])))
                c0, r = NORM_COLS[stage], slice(0, XT * P)
                for k in range(KT):
                    act.wait_ge(*finished((stage, k)))
                    seq.note(act.activation(act_hi[:, k, r], psum[:, place[(stage, k)][0], r], ACTF.Identity,
                                            scale=cols[:, c0 + k:c0 + k + 1], bias=zero[:]).then_inc(s_h, 1), s_h)

            def to_feature(stage, tiles):
                act.wait_ge(*finished(last_unit(before_act[stage])))
                for t in (range(tiles) if isinstance(tiles, int) else tiles):
                    for h in range(2):
                        act.wait_ge(*finished((stage, t, h)))
                        ps = psum[:, place[(stage, t, h)][0], :].rearrange("p (k n) -> p k n", k=HALF_KT)
                        seq.note(act.activation(act_hi[:, h * HALF_KT:(h + 1) * HALF_KT, tile_cols(t)], ps,
                                                 ACTF.Copy).then_inc(s_h, 1), s_h)

            def move(dst, name, n=COLS, scale=1.0, wait_for=None):
                act.wait_ge(*finished(name))
                if wait_for:
                    act.wait_ge(*finished(wait_for))
                src = psum[:, place[name][0], 0:n]
                if len(dst.shape) == 3:
                    src = src.rearrange("p (k n) -> p k n", k=dst.shape[1])
                seq.freed(act.activation(dst, src, ACTF.Copy, scale=scale).then_inc(bank_free(name), 1), name)

            def tanh_half(dst, name, n=COLS):
                act.wait_ge(*finished(name))
                seq.note(act.activation(dst, psum[:, place[name][0], 0:n], ACTF.Tanh, scale=0.5).then_inc(s_tanh, 1), s_tanh)

            act.wait_ge(s_cin, 16 * N_CIN)
            seq.note(act.activation(silu_t[:, 1, :], silu_t[:, 0, :], ACTF.Tanh, scale=0.5).then_inc(s_silu, 1), s_silu)
            for t in range(XT):
                act.dma_start(xs[:, t, :], a["x"][0, t * P:(t + 1) * P, :]).then_inc(s_xin, 16)
                act.dma_start(xs[:, XT + t, :], a["ctx"][0, t * P:(t + 1) * P, :]).then_inc(s_xin, 16)
            split_through(2)
            act.wait_ge(s_xin, 16 * NT)
            for t in range(NT):
                square_sum(("norm0", t), xs[:, t, :], sc[:, 2 * (t % 2):2 * (t % 2) + 2, :].rearrange("p a n -> p (a n)"),
                           ss[:, t:t + 1])

            for c in range(4):
                run_chunk("ada0", c, lambda c, t: move(mrow[:, c * COLS:(c + 1) * COLS], ("ada0", c, 0)))
            act.wait_ge(s_lamin, 1)
            seq.note(act.activation(lam_s[:, 2:4], lam_s[:, 0:2], ACTF.Exp).then_inc(s_lamout, 1), s_lamout)
            act.wait_ge(s_mod, 1)
            norm_modulated("norm0", 0)

            turned = [("turn0", c, t) for c in range(4) for t in range(NT)]

            def move_turned(name):
                _, c, t = name
                dst = (qT if c < 2 else kT)[:, 4 * (c % 2):4 * (c % 2) + 4, tile_cols(t)]
                move(dst, name, scale=0.125 if c < 2 else 1.0)

            def unit0(c, t):
                n = c * NT + t
                if 2 <= n < 2 + len(turned):
                    move_turned(turned[n - 2])
                if c in (4, 5):
                    move(vbuf[:, t, (c - 4) * COLS:(c - 3) * COLS], ("in0", c, t))

            for c in range(6):
                run_chunk("in0", c, unit0)

            def exp0(p):
                t = p // HEADS
                n = NT * P if t < XT else XT * P
                act.wait_ge(s_mx, p + 1)
                if p >= 2:
                    act.wait_ge(s_comb, p - 1)
                for s in range(2):
                    b = place[("s0", p, s)][0]
                    seq.freed(act.activation(sc[:, 2 * (p % 2) + s, 0:n], psum[:, b, 0:n], ACTF.Exp,
                                                 bias=nmax[:, p % 2, s:s + 1], accum_out=rsum[:, p % 2, s:s + 1]).then_inc(bank_free(("s0", p, s)), 1), ("s0", p, s))

            def out0(p):
                t, h = divmod(p, HEADS)
                move(qT[:, h, tile_cols(t)], ("pv0", p), n=P, scale=rinv[:, p % 2, 0:1])

            def beside0(p):
                stage, c, t, part = BESIDE_ATTENTION0[p]
                if part == 0:
                    return
                if stage == "in0":
                    tanh_half(zbuf[:, t, (c - 6) * COLS:(c - 5) * COLS], (stage, c, t))
                elif stage == "ada0g":
                    move(mrow0g[:, c * COLS:(c + 1) * COLS], (stage, c, t))
                else:
                    move(mrow1[:, c * COLS:(c + 1) * COLS], (stage, c, t))

            def sub_squares(t):
                square_sum(("sub", t), qT[:, :, tile_cols(t)], squares0[:, t] if t < NT - 1 else
                           sc[:, 0:2, :].rearrange("p a (h d) -> p (a h) d", d=P))

            exp0(0)
            for p in range(NT * HEADS):
                if p:
                    out0(p - 1)
                if p + 1 < NT * HEADS:
                    exp0(p + 1)
                n = NT * P if p < XT * HEADS else XT * P
                move(sc[:, 6 + p % 2, 0:n], ("t0", p), n=n, wait_for=("pv0", p - 2) if p >= 2 else None)
                if p:
                    beside0(p - 1)
                if p in SPLITS_BESIDE0:
                    split_through(done_halves[0])
                if p in SUB_AT:
                    sub_squares(SUB_AT.index(p))
            out0(NT * HEADS - 1)
            beside0(NT * HEADS - 1)
            sub_squares(NT - 1)
            act.wait_ge(s_powin, pow_at[("sub", NT - 2)][0] + 1)
            to_feature("turn_o0", range(NT - 1))

            def out_unit(stage, c, t):
                name = (stage, c, t)
                act.wait_ge(*finished(name))
                ps = psum[:, place[name][0], :]
                if c == 0:
                    seq.note(act.activation(y_tok[:, t, 0:COLS], ps, ACTF.Copy).then_inc(s_a, 1), s_a)
                act.wait_ge(*seq.last)
                n0 = ss_post[(stage, t)]
                ins = act.activation(sc[:, 7, :], ps, ACTF.Square, accum_out=ss[:, n0 + c:n0 + c + 1])
                if c == 0:
                    seq.freed(ins.then_inc(bank_free(name), 1), name)
                else:
                    seq.note(ins.then_inc(s_psq, 1), s_psq)

            def unit_out0(c, t):
                out_unit("out0", c, t)
                if c == 0 and t == NT - 2:
                    to_feature("turn_o0", range(NT - 1, NT))

            def norm_square(stage, t, base):
                act.wait_ge(s_res, base + t + 1)
                square_sum((stage, t), xs[:, t, :],
                           sc[:, 2 * (t % 2):2 * (t % 2) + 2, :].rearrange("p a n -> p (a n)"),
                           ss[:, ss_norm[(stage, t)]:ss_norm[(stage, t)] + 1])

            run_chunk("out0", 0, unit_out0)

            def unit_last0(c, t):
                out_unit("out0", c, t)
                if t >= 2:
                    norm_square("norm1", t - 2, 0)

            run_chunk("out0", 1, unit_last0, before_norm=True)
            norm_square("norm1", NT - 2, 0)
            split_through(half_no[("in1", 0, 0)] + 1)
            norm_square("norm1", NT - 1, 0)
            act.wait_ge(s_mod, 2)
            norm_modulated("norm1", 1)
            split_through(half_no[("in1", 0, 0)] + 2)

            units1 = [(c, t) for c in range(3) for t in gemm_tiles("in1", c)]
            unit_no = {u: n for n, u in enumerate(units1)}

            def move_turned1(name):
                _, c, t = name
                if c < 2:
                    move(qT[:, 4 * c:4 * c + 4, tile_cols(t)], name, scale=float(P) ** -0.5)
                else:
                    move(kT[:, 0:2, tile_cols(t)], name, n=256)

            def unit1(c, t):
                n = unit_no[(c, t)]
                if n >= 2:
                    move_turned1(("turn1", *units1[n - 2]))
                name = ("in1", c, t)
                act.wait_ge(*finished(name))
                ps = psum[:, place[name][0], :]
                if n >= 2:
                    act.wait_ge(s_powin, pow_at[("qk1", *units1[n - 2])][0] + 1)
                if c == 2:
                    seq.note(act.activation(vbuf[:, t, 0:256], ps[:, 256:512], ACTF.Copy).then_inc(s_a, 1), s_a)
                w = 4 if c < 2 else 2
                square_sum(("qk1", c, t), ps[:, 0:w * P], sc[:, 5 + n % 2, 0:w * P])

            for c in range(3):
                run_chunk("in1", c, unit1)
            for u in units1[-2:]:
                move_turned1(("turn1", *u))

            def exp1(p):
                act.wait_ge(s_mx, NT * HEADS + p + 1)
                if p >= 2:
                    act.wait_ge(*finished(("t1", p - 2)))
                b = place[("s1", p)][0]
                seq.freed(act.activation(sc[:, p % 2, :], psum[:, b, :], ACTF.Exp, bias=nmax[:, p % 2, 0:1],
                                             accum_out=rsum[:, p % 2, 0:1]).then_inc(bank_free(("s1", p)), 1), ("s1", p))

            exp1(0)
            z_units1 = [(c, t) for c in (3, 4) for t in range(XT)]
            for p in range(XT * HEADS):
                if p + 1 < XT * HEADS:
                    if p >= 1:
                        act.wait_ge(s_rinv, p)
                    exp1(p + 1)
                move(sc[:, 6 + p % 2, :], ("t1", p), wait_for=("pv1", p - 2) if p >= 2 else None)
                if p % 4 == 3:
                    c, t = z_units1[p // 4]
                    tanh_half(zbuf[:, t, (c - 3) * COLS:(c - 2) * COLS], ("in1", c, t))
                if p == 6:
                    split_through(z_first1 + 3)
                if p == 8:
                    split_through(z_first1 + 4)
            split_through(half_no[("out1", 0, 0)] + 1)
            to_feature("turn_o1", XT)
            for c in range(2):
                run_chunk("out1", c, lambda c, t: out_unit("out1", c, t), before_norm=(c == 1))
            norm_square("norm2", 0, NT)
            split_through(half_no[("in2", 0, 0)] + 1)
            norm_square("norm2", 1, NT)
            norm("norm2")
            split_through(half_no[("in2", 0, 0)] + 2)

            def unit2(c, t):
                name = ("in2", c, t)
                ps = psum[:, place[name][0], :]
                if c == 0:
                    act.wait_ge(*finished(name))
                    seq.note(act.activation(iq[:, t, :], ps[:, 128:256], ACTF.Copy).then_inc(s_a, 1), s_a)
                    seq.note(act.activation(ik4[:, t, :].rearrange("p (r d) -> p r d", r=4),
                                             ps[:, 256:288].unsqueeze(1).broadcast_to((P, 4, 32)), ACTF.Copy).then_inc(s_a, 1), s_a)
                    seq.note(act.activation(iw[:, t, :], ps[:, 288:292], ACTF.Copy, scale=0.5).then_inc(s_a, 1), s_a)
                    square_sum(("lat", t), ps[:, 0:P], vecs[:], ss[:, ss_lat + t:ss_lat + t + 1])
                elif c == 1:
                    act.wait_ge(*finished(name))
                    square_sum(("qa", t), ps, sc[:, 5 + t, :])
                    if t == 0:
                        for u in range(XT):
                            nm = ("turn_c", u)
                            act.wait_ge(*finished(nm))
                            tp = psum[:, place[nm][0], :]
                            seq.note(act.activation(cT[:, tile_cols(u)], tp[:, 0:P], ACTF.Copy,
                                                     scale=cols[:, C_KV:C_KV + 1]).then_inc(s_a, 1), s_a)
                            seq.note(act.activation(iqT[:, tile_cols(u)], tp[:, P:2 * P], ACTF.Copy).then_inc(s_a, 1), s_a)
                            seq.freed(act.activation(ikT[:, tile_cols(u)], tp[:, 2 * P:3 * P], ACTF.Copy).then_inc(bank_free(nm), 1), nm)
                    else:
                        for u in range(XT):
                            for i in range(4):
                                nm = ("idx", u, i)
                                act.wait_ge(*finished(nm))
                                seq.freed(act.activation(relus[:, u, i, :], psum[:, place[nm][0], 0:256], ACTF.Relu,
                                                         scale=32.0 ** -0.5).then_inc(bank_free(nm), 1), nm)
                elif c == 2:
                    nm = ("latent", t)
                    act.wait_ge(*finished(nm))
                    square_sum(("ka", t), psum[:, place[nm][0], 0:64], vecs[:, 0:64], ss[:, ss_ka + t:ss_ka + t + 1])
                    if t == 1:
                        for u in range(XT):
                            move(qaT[:, :, tile_cols(u)], ("turn_qa", u), scale=0.125)
                elif c == 3:
                    if t == 1:
                        for u in range(XT):
                            move(qbT[:, :, tile_cols(u)], ("turn_qb", u))
                elif c == 4:
                    move(vb[:, t, :], name)
                    if t == 0:
                        for u in range(XT):
                            move(kbT[:, :, tile_cols(u)], ("turn_kb", u), scale=0.125)
                            move(kaT[:, tile_cols(u)], ("turn_ka", u), n=P)
                else:
                    tanh_half(gb[:, t, :], name)

            for c in range(6):
                run_chunk("in2", c, unit2)
            for p in range(8):
                act.wait_ge(s_mx, (NT + XT) * HEADS + p + 1)
                for e in range(2):
                    v = sc[:, p % 2, 256 * e:256 * e + 256]
                    seq.note(act.activation(v, v, ACTF.Exp, bias=nmax[:, p % 2, e:e + 1],
                                             accum_out=rsum[:, p % 2, e:e + 1]).then_inc(s_ex if e else s_a, 1), s_ex if e else s_a)
                move(sc[:, 2 + p % 2, :], ("t2", p), wait_for=("pv2", p - 2) if p >= 2 else None)
                if p == 4:
                    for t in range(XT):
                        act.wait_ge(s_yc, t + 1)
                        square_sum(("gn", t), sc[:, 4 + t, :], sc[:, 6 + t, :])
            to_feature("turn_o2", XT)
            def unit_out2(c, t):
                if c == 1:
                    act.wait_ge(*moved(("out2", 0, t)))
                    act.wait_ge(*moved(("out2", 1, t)))
                    square_sum(("norm3", t), xs[:, t, :],
                               sc[:, 2 * (t % 2):2 * (t % 2) + 2, :].rearrange("p a n -> p (a n)"),
                               ss[:, ss_norm[("norm3", t)]:ss_norm[("norm3", t)] + 1])

            run_chunk("out2", 0, unit_out2)
            unit_out2(1, 0)
            split_through(half_no[("gu", 0, 1)])
            unit_out2(1, 1)
            norm("norm3")
            split_through(half_no[("gu", 0, 1)] + 1)
            n_tanh = [0]

            def gate_tanh(j, t):
                act.wait_ge(*finished(("gu", j, t)))
                if j:
                    act.wait_ge(*moved(("gu", j - 1, t)))
                seq.note(act.activation(sc[:, t, 0:256], psum[:, 4 + t, 0:256], ACTF.Tanh, scale=0.5).then_inc(s_tanh, 1), s_tanh)

            def hidden_hi(j):
                for t in range(XT):
                    act.wait_ge(*finished(("turn_h", j, t)))
                    if j >= 2:
                        act.wait_ge(*released[half_no[("down", j - 2, 0)]])
                    ps = psum[:, 6 + t, 0:256].rearrange("p (k n) -> p k n", k=2)
                    k = 2 * (j % 2)
                    seq.note(act.activation(act_hi[:, k:k + 2, tile_cols(XT + t)], ps, ACTF.Copy).then_inc(s_h, 1), s_h)

            for j in range(FFN_STEPS):
                gate_tanh(j, 0)
                if j:
                    hidden_hi(j - 1)
                split_through(half_no.get(("gu", j + 1, 0), 0))
                gate_tanh(j, 1)
                split_through(half_no.get(("gu", j + 1, 1), 0))
                split_through(half_no[("down", j, 0)])
            hidden_hi(FFN_STEPS - 1)

        @block.gpsimd
        def _(pool):
            seq = Sequence(moved)
            seq.note(pool.memset(half_neg[:], -0.5).then_inc(s_g, 1), s_g)
            pool.memset(zero[:], 0.0).then_inc(s_half, 1)
            for dst, src in ((sel[:], a["k_sel"]), (rope_a[:], a["k_rope_a"]),
                             (lamb[:], a["a_lambda"][0].partition_broadcast(P))):
                pool.dma_start(dst, src).then_inc(s_par, 16)
            pool.wait_ge(s_half, 1)
            n_pows = [0]

            def powers_through(key):
                while n_pows[0] <= pow_at[key][0]:
                    n, w = pows[n_pows[0]]
                    pool.wait_ge(s_powin, n_pows[0] + 1)
                    seq.note(pool.tensor_tensor(rstd[:, n:n + w], ms[:, n:n + w], half_neg[:, 0:w], ALU.pow).then_inc(s_powout, 1), s_powout)
                    n_pows[0] += 1

            powers_through(("norm0", NT - 1))
            pool.wait_ge(s_mod, 1)
            for dst, src in ((gate0[:, 1, :], a["post_g"][0].partition_broadcast(P)),
                             (subln[:], a["a_subln_g"][0].partition_broadcast(P)),
                             (rope_b[:], a["k_rope_b"]), (rope_c[:], a["k_rope_c"]),
                             (qk_g[:], a["b_qk_g"][0].partition_broadcast(P)),
                             (qkn2[:, 0, :], a["q_norm_w_2"][0].partition_broadcast(P)),
                             (qkn2[:, 1, :], a["k_norm_w_2"][0].partition_broadcast(P)),
                             (w_ukv[:, 0, :], a["w_uk_2"][0]), (w_ukv[:, 1, :], a["w_uv_2"][0]),
                             (relb[:], a["rel_bias_2"])):
                pool.dma_start(dst, src).then_inc(s_late, 16)
            pool.wait_ge(s_sub, 1)
            for t in range(NT):
                pool.wait_ge(*moved(("in0", 6, t)))
                pool.wait_ge(*moved(("in0", 7, t)))
                z = zbuf[:, t, :].rearrange("p (h d) -> p h d", d=P)
                seq.note(pool.tensor_tensor(z, z, subln[:].unsqueeze(1).broadcast_to((P, HEADS, P)), ALU.mult).then_inc(s_zg, 1), s_zg)
            for t in range(NT):
                powers_through(("sub", t))
                n = pow_at[("sub", t)][1]
                o = qT[:, :, tile_cols(t)]
                pool.wait_ge(*seq.last)
                seq.note(pool.tensor_tensor(o, o, rstd[:, n:n + HEADS].unsqueeze(2).broadcast_to((P, HEADS, P)), ALU.mult).then_inc(s_og, 1), s_og)
                if t < NT - 1:
                    z = zbuf[:, t, :].rearrange("p (h d) -> p h d", d=P)
                    pool.wait_ge(*seq.last)
                    seq.note(pool.tensor_tensor(z, o, z, ALU.mult).then_inc(s_tok, 1), s_tok)
            powers_through(("ka", XT - 1))
            pool.wait_ge(s_toepr, 32)
            for t in range(XT):
                pool.wait_ge(s_mark, t + 1)
                seq.note(pool.tensor_tensor(biasm[:, t], biasm[:, t], taken[:, t, :].unsqueeze(1).broadcast_to((P, HEADS, 256)),
                                            ALU.add).then_inc(s_masked, 1), s_masked)
            powers_through(("norm3", XT - 1))

        @block.vector
        def _(dve):
            seq = Sequence(moved)
            done_halves = [0]

            def split_through(g):
                while done_halves[0] <= min(g, len(halves) - 1):
                    n = done_halves[0]
                    r = slice(0, half_size(n))
                    dve.wait_ge(s_whi, n + 1)
                    seq.note(dve.tensor_tensor(w_lo[:, n % RING, r], raw[:, n % RING, r],
                                                w_hi[:, n % RING, r].bitcast(F32), ALU.subtract).then_inc(s_wlo, 1), s_wlo)
                    done_halves[0] += 1

            def run_chunk(stage, c, unit, before_norm=False):
                g0 = half_no[(stage, c, 0)]
                tiles = gemm_tiles(stage, c)
                for t in tiles:
                    if t == tiles[-1] and not before_norm:
                        split_through(g0 + 3)
                    unit(c, t)
                if not before_norm:
                    split_through(g0 + 4)

            def free_bank(name):
                dve.wait_ge(*seq.last)
                seq.freed(dve.tensor_copy(ss[0:1, 255:256], psum[0:1, place[name][0], 0:1]).then_inc(bank_free(name), 1), name)

            def mean_power(key, sums, width, scale, eps=EPS):
                i, n, w = pow_at[key]
                assert i == seq.count.get(s_powin.name, 0) and w == width, key
                seq.note(dve.tensor_scalar(ms[:, n:n + w], sums, scale, eps, ALU.mult, ALU.add).then_inc(s_powin, 1), s_powin)

            def rs(key):
                i, n, w = pow_at[key]
                dve.wait_ge(s_powout, i + 1)
                return rstd[:, n:n + w]

            def squares(name):
                dve.wait_ge(s_sq, sq_no[name] + 1)

            def norm_in(stage):
                tiles = norm_tiles[stage]
                for t in range(tiles):
                    squares((stage, t))
                    n0 = ss_norm[(stage, t)]
                    mean_power((stage, t), ss[:, n0:n0 + 1], 1, 1.0 / D)
                for t in range(tiles):
                    assert seq.count.get(s_xn.name, 0) == xn_base[stage] + t
                    seq.note(dve.tensor_scalar(xn[:, t, :], xs[:, t, :], rs((stage, t)), None, ALU.mult).then_inc(s_xn, 1), s_xn)

            def norm_lo_modulated(stage, l):
                for k in range(KT + 2):
                    if k < KT:
                        dve.wait_ge(s_modx, act_base[stage] + k + 1)
                        r = slice(XT * P, NT * P)
                        seq.freed(dve.tensor_scalar(sc[:, 4 + k % 4, r], psum[:, place[(stage, k)][0], r], mod[:, l, 0, k, 1:2],
                                                    mod[:, l, 1, k, 1:2], ALU.mult, ALU.add).then_inc(bank_free((stage, k)), 1), (stage, k))
                    if k >= 2:
                        dve.wait_ge(s_h, h_base[stage] + k - 1)
                        seq.note(dve.tensor_tensor(act_lo[:, k - 2, :], sc[:, 4 + (k - 2) % 4, :], act_hi[:, k - 2, :].bitcast(F32),
                                                    ALU.subtract).then_inc(s_act, 1), s_act)

            def norm_lo(stage):
                c0, r = NORM_COLS[stage], slice(0, XT * P)
                for k in range(KT):
                    dve.wait_ge(s_h, h_base[stage] + k + 1)
                    seq.freed(dve.scalar_tensor_tensor(out=act_lo[:, k, r], in0=psum[:, place[(stage, k)][0], r],
                                                       scalar=cols[:, c0 + k:c0 + k + 1], in1=act_hi[:, k, r].bitcast(F32),
                                                       op0=ALU.mult, op1=ALU.subtract).then_inc(bank_free((stage, k)), 1), (stage, k))

            def to_feature(stage, tiles):
                dve.wait_ge(*finished(last_unit(before_act[stage])))
                for t in (range(tiles) if isinstance(tiles, int) else tiles):
                    for h in range(2):
                        name = (stage, t, h)
                        dve.wait_ge(s_h, h_base[stage] + 2 * t + h + 1)
                        ps = psum[:, place[name][0], :].rearrange("p (k n) -> p k n", k=HALF_KT)
                        r = slice(h * HALF_KT, (h + 1) * HALF_KT)
                        seq.freed(dve.tensor_tensor(act_lo[:, r, tile_cols(t)], ps,
                                                        act_hi[:, r, tile_cols(t)].bitcast(F32), ALU.subtract).then_inc(bank_free(name), 1), name)

            def rope(src, table, heads, half, dst, src_name=None, on_done=None):
                def v(ap):
                    return ap[:, 0:heads * 2 * half].rearrange("p (h s d) -> p h s d", h=heads, s=2)
                cos, sin = table
                full_cos = cos.unsqueeze(1).unsqueeze(1).broadcast_to((P, heads, 2, half))
                one_sin = sin.unsqueeze(1).broadcast_to((P, heads, half))
                x, ta, tb, o = v(src), v(sc[:, 3, :]), v(sc[:, 4, :]), v(dst)
                dve.wait_ge(*seq.last)
                seq.note(dve.tensor_tensor(ta, x, full_cos, ALU.mult).then_inc(s_v, 1), s_v)
                seq.note(dve.tensor_tensor(tb[:, :, 0, :], x[:, :, 1, :], one_sin, ALU.mult).then_inc(s_v, 1), s_v)
                ins = dve.tensor_tensor(tb[:, :, 1, :], x[:, :, 0, :], one_sin, ALU.mult)
                if src_name:
                    seq.freed(ins.then_inc(bank_free(src_name), 1), src_name)
                else:
                    seq.note(ins.then_inc(s_v, 1), s_v)
                dve.wait_ge(*seq.last)
                seq.note(dve.tensor_tensor(o[:, :, 0, :], ta[:, :, 0, :], tb[:, :, 0, :], ALU.subtract).then_inc(s_v, 1), s_v)
                seq.note(dve.tensor_tensor(o[:, :, 1, :], ta[:, :, 1, :], tb[:, :, 1, :], ALU.add).then_inc(s_rot, 1), s_rot)

            def rot_free(name):
                n = rot_no[name]
                assert seq.count.get(s_rot.name, 0) == n, name
                if n >= 3:
                    dve.wait_ge(*finished(rot_units[n - 3]))

            dve.wait_ge(s_silu, 1)
            seq.note(dve.scalar_tensor_tensor(out=silu_t[:, 1, :], in0=silu_t[:, 1, :], scalar=1.0,
                                               in1=silu_t[:, 0, :], op0=ALU.add, op1=ALU.mult).then_inc(s_v, 1), s_v)
            dve.wait_ge(*seq.last)
            seq.note(dve.tensor_scalar(vecs[0:16, :], silu_t[:, 1, :], 0.5, None, ALU.mult).then_inc(s_silu_v, 1), s_silu_v)
            dve.wait_ge(*finished(("cols",)))
            seq.freed(dve.tensor_copy(cols[:, 0:N_COLS], psum[:, place[("cols",)][0], 0:N_COLS]).then_inc(bank_free(("cols",)), 1), ("cols",))
            dve.wait_ge(*seq.last)
            seq.note(dve.tensor_copy(c_hi[:], cols[:, 0:16]).then_inc(s_v, 1), s_v)
            dve.wait_ge(*seq.last)
            seq.note(dve.tensor_tensor(c_lo[:], cols[:, 0:16], c_hi[:].bitcast(F32), ALU.subtract).then_inc(s_v, 1), s_v)
            dve.wait_ge(*seq.last)
            for g in range(4):
                src = (c_hi[:].bitcast(F32) if g < 2 else c_lo[:])[:, 8 * (g % 2):8 * (g % 2) + 8]
                seq.note(dve.tensor_copy(cstat[:, :, 32 * g:32 * g + 32], src.unsqueeze(2).broadcast_to((P, KT, 32))).then_inc(s_cst if g == 3 else s_v, 1), s_cst if g == 3 else s_v)
            split_through(2)
            norm_in("norm0")
            dve.wait_ge(s_par, 16 * N_PAR)
            pairs = lamb[:].rearrange("p (a b) d -> p a b d", a=2)
            prod = sc[:, 7, 0:128].rearrange("p (a d) -> p a d", a=2)
            seq.note(dve.tensor_tensor(prod, pairs[:, :, 0, :], pairs[:, :, 1, :], ALU.mult).then_inc(s_v, 1), s_v)
            dve.wait_ge(*seq.last)
            seq.note(dve.tensor_reduce(lam_s[:, 0:2], prod, AX_X, ALU.add).then_inc(s_lamin, 1), s_lamin)

            def mod_sums(l):
                nm = (f"mod{l}",)
                dve.wait_ge(*finished(nm))
                ps = psum[:, place[nm][0], 0:32].rearrange("p (w k s) -> p w k s", w=2, k=KT)
                b = cols[:, C_ADAB + 24 * l:C_ADAB + 24 * l + 16].rearrange("p (w k) -> p w k", w=2)
                for w in range(2):
                    ins = dve.tensor_tensor(mod[:, l, 1 - w], ps[:, w], b[:, w].unsqueeze(2).broadcast_to((P, KT, 2)), ALU.add)
                    if w:
                        seq.freed(ins.then_inc(bank_free(nm), 1), nm)
                    else:
                        seq.note(ins.then_inc(s_v, 1), s_v)
                dve.wait_ge(*seq.last)
                g = cols[:, C_PRE + 8 * l:C_PRE + 8 * l + 8].unsqueeze(2).broadcast_to((P, KT, 2))
                seq.note(dve.scalar_tensor_tensor(out=mod[:, l, 0], in0=mod[:, l, 0], scalar=1.0, in1=g,
                                                   op0=ALU.add, op1=ALU.mult).then_inc(s_mod, 1), s_mod)

            for c in range(4):
                run_chunk("ada0", c, lambda c, t: None)
            mod_sums(0)
            dve.wait_ge(s_lamout, 1)
            neg_lambda = lam_s[:, 4:5]
            seq.note(dve.tensor_scalar(neg_lambda, lam_s[:, 3:4], LAMBDA_INIT, lam_s[:, 2:3], ALU.subtract,
                                        ALU.subtract).then_inc(s_v, 1), s_v)
            norm_lo_modulated("norm0", 0)

            def unit0(c, t):
                name = ("in0", c, t)
                if c < 4:
                    dve.wait_ge(*finished(name))
                    ps = psum[:, place[name][0], :]
                    rot_free(("turn0", c, t))
                    if t < XT:
                        rope(ps, (rope_a[:, 0, t, :], rope_a[:, 1, t, :]), 8, 32, rot_buf(("turn0", c, t)), name)
                    else:
                        seq.note(dve.tensor_copy(rot_buf(("turn0", c, t)), ps).then_inc(s_rot, 1), s_rot)
                        free_bank(name)

            for c in range(6):
                run_chunk("in0", c, unit0)

            def max0(p):
                n = NT * P if p < XT * HEADS else XT * P
                dve.wait_ge(*finished(("s0", p, 0)))
                dve.wait_ge(*finished(("s0", p, 1)))
                b = place[("s0", p, 0)][0]
                seq.note(dve.tensor_reduce(nmax[:, p % 2, :], psum[:, b:b + 2, 0:n], AX_X, ALU.max, negate=True).then_inc(s_mx, 1), s_mx)

            def comb0(p):
                n = NT * P if p < XT * HEADS else XT * P
                dve.wait_ge(*moved(("s0", p, 0)))
                dve.wait_ge(*moved(("s0", p, 1)))
                r = rinv[:, p % 2, :]
                if p >= 2:
                    dve.wait_ge(*moved(("pv0", p - 2)))
                seq.note(dve.reciprocal(r[:, 0:2], rsum[:, p % 2, :]).then_inc(s_v, 1), s_v)
                dve.wait_ge(*seq.last)
                seq.note(dve.scalar_tensor_tensor(out=r[:, 2:3], in0=r[:, 1:2], scalar=neg_lambda,
                                                   in1=rsum[:, p % 2, 0:1], op0=ALU.mult, op1=ALU.mult).then_inc(s_v, 1), s_v)
                dve.wait_ge(*seq.last)
                if p >= 2:
                    dve.wait_ge(*finished(("t0", p - 2)))
                seq.note(dve.scalar_tensor_tensor(out=sc[:, 4 + p % 2, 0:n], in0=sc[:, 2 * (p % 2) + 1, 0:n],
                                                   scalar=r[:, 2:3], in1=sc[:, 2 * (p % 2), 0:n],
                                                   op0=ALU.mult, op1=ALU.add).then_inc(s_comb, 1), s_comb)

            def gate_z(dst, name):
                dve.wait_ge(s_tanh, n_tanh[0] + 1)
                n_tanh[0] += 1
                seq.freed(dve.scalar_tensor_tensor(out=dst, in0=dst, scalar=1.0, in1=psum[:, place[name][0], :],
                                                       op0=ALU.add, op1=ALU.mult).then_inc(bank_free(name), 1), name)

            n_tanh = [0]
            def sub_mean(t):
                squares(("sub", t))
                n0 = 32 + 8 * t
                src = squares0[:, t] if t < NT - 1 else sc[:, 0:2, :].rearrange("p a (h d) -> p (a h) d", d=P)
                seq.note(dve.tensor_reduce(ss[:, n0:n0 + 8], src, AX_X, ALU.add).then_inc(s_v, 1), s_v)
                dve.wait_ge(*seq.last)
                mean_power(("sub", t), ss[:, n0:n0 + 8], 8, 1.0 / P)

            dve.wait_ge(s_late, 16 * N_LATE)
            seq.note(dve.tensor_scalar(subln[:], subln[:], 0.5 * (1.0 - LAMBDA_INIT), None, ALU.mult).then_inc(s_sub, 1), s_sub)

            max0(0)
            for p in range(NT * HEADS):
                comb0(p)
                if p + 1 < NT * HEADS:
                    max0(p + 1)
                if p >= 2:
                    stage, c, t, part = BESIDE_ATTENTION0[p - 2]
                    if stage == "in0" and part == 1:
                        gate_z(zbuf[:, t, (c - 6) * COLS:(c - 5) * COLS], (stage, c, t))
                if p - 1 in SPLITS_BESIDE0:
                    split_through(done_halves[0])
                if p - 1 in SUB_AT:
                    sub_mean(SUB_AT.index(p - 1))
            split_through(done_halves[0])
            sub_mean(NT - 1)
            mod_sums(1)
            dve.wait_ge(*finished(("gate1", 0, 1)))
            to_feature("turn_o0", range(NT - 1))
            dve.wait_ge(s_og, NT)
            z = zbuf[:, NT - 1, :].rearrange("p (h d) -> p h d", d=P)
            seq.count[s_tok.name] = NT - 1
            seq.note(dve.tensor_tensor(z, qT[:, :, tile_cols(NT - 1)], z, ALU.mult).then_inc(s_tok, 1), s_tok)
            dve.wait_ge(s_par1, 48)
            for c in range(2):
                nm = ("gate1", 0, c)
                r = slice(c * COLS, (c + 1) * COLS)
                seq.freed(dve.tensor_tensor(gate1[:, r], psum[:, place[nm][0], :], k_flat[:, r], ALU.add).then_inc(bank_free(nm), 1), nm)
                dve.wait_ge(*seq.last)
                seq.note(dve.tensor_tensor(gate1[:, r], gate1[:, r], k_flat[:, D + c * COLS:D + (c + 1) * COLS], ALU.mult).then_inc(s_v, 1), s_v)

            def gates0():
                for c in range(2):
                    r = slice(c * COLS, (c + 1) * COLS)
                    dve.wait_ge(*finished(("gate0", 0, c)))
                    dve.wait_ge(*finished(("gate0", 1, c)))
                    for s in range(2):
                        nm = ("gate0", s, c)
                        seq.freed(dve.tensor_tensor(sc[:, 2 * c + s, :], psum[:, place[nm][0], :], k_flat[:, 2 * D + c * COLS:2 * D + (c + 1) * COLS],
                                                    ALU.add).then_inc(bank_free(nm), 1), nm)
                    for s in range(2):
                        dve.wait_ge(*seq.last)
                        seq.note(dve.tensor_tensor(gate0[:, s, r], sc[:, 2 * c + s, :], gate0[:, 1, r], ALU.mult).then_inc(s_v, 1), s_v)

            gates0()

            def post_mean(l, t):
                stage = f"out{l}"
                gate = gate1 if l else gate0[:, t // XT, :]
                dve.wait_ge(*moved((stage, 0, t)))
                seq.note(dve.tensor_tensor(y_tok[:, t, 0:COLS], y_tok[:, t, 0:COLS], gate[:, 0:COLS], ALU.mult).then_inc(s_v, 1), s_v)
                name = (stage, 1, t)
                dve.wait_ge(s_psq, l * NT + t + 1)
                n0 = ss_post[(stage, t)]
                seq.note(dve.tensor_tensor(ss[:, n0:n0 + 1], ss[:, n0:n0 + 1], ss[:, n0 + 1:n0 + 2], ALU.add).then_inc(s_v, 1), s_v)
                dve.wait_ge(*seq.last)
                mean_power((f"post{l}", t), ss[:, n0:n0 + 1], 1, 1.0 / D)
                seq.freed(dve.tensor_tensor(y_tok[:, t, COLS:D], psum[:, place[name][0], :], gate[:, COLS:D],
                                            ALU.mult).then_inc(bank_free(name), 1), name)

            def residual(l, t):
                dve.wait_ge(*seq.last)
                seq.note(dve.scalar_tensor_tensor(out=xs[:, t, :], in0=y_tok[:, t, :], scalar=rs((f"post{l}", t)),
                                                   in1=xs[:, t, :], op0=ALU.mult, op1=ALU.add).then_inc(s_res, 1), s_res)

            def norm_mean(stage, t):
                squares((stage, t))
                n0 = ss_norm[(stage, t)]
                mean_power((stage, t), ss[:, n0:n0 + 1], 1, 1.0 / D)

            def normed(stage, t):
                seq.note(dve.tensor_scalar(xn[:, t, :], xs[:, t, :], rs((stage, t)), None, ALU.mult).then_inc(s_xn, 1), s_xn)

            def residual_steps(l, tiles, t):
                stage = f"norm{l + 1}"
                if 1 <= t <= tiles:
                    residual(l, t - 1)
                if t >= 2:
                    norm_mean(stage, t - 2)
                if t < tiles:
                    post_mean(l, t)
                if t >= 2:
                    normed(stage, t - 2)

            def unit_out0(c, t):
                if c == 0 and t == NT - 2:
                    to_feature("turn_o0", range(NT - 1, NT))
                if c == 1:
                    residual_steps(0, NT, t)

            run_chunk("out0", 0, unit_out0)
            run_chunk("out0", 1, unit_out0, before_norm=True)
            residual_steps(0, NT, NT)
            residual_steps(0, NT, NT + 1)
            split_through(half_no[("in1", 0, 0)] + 1)
            norm_lo_modulated("norm1", 1)
            split_through(half_no[("in1", 0, 0)] + 2)

            units1 = [(c, t) for c in range(3) for t in gemm_tiles("in1", c)]
            unit_no = {u: n for n, u in enumerate(units1)}

            def unit1(c, t):
                n, w = unit_no[(c, t)], 4 if c < 2 else 2
                name = ("in1", c, t)
                key = ("qk1", c, t)
                squares(key)
                n0 = 80 + 4 * n
                dve.wait_ge(*seq.last)
                seq.note(dve.tensor_reduce(ss[:, n0:n0 + w], sc[:, 5 + n % 2, 0:w * P].rearrange("p (h d) -> p h d", d=P),
                                            AX_X, ALU.add).then_inc(s_v, 1), s_v)
                dve.wait_ge(*seq.last)
                mean_power(key, ss[:, n0:n0 + w], w, 1.0 / P)
                nm = ("turn1", c, t)
                rot_free(nm)
                r, buf = rs(key), sc[:, 7, :] if t < XT else rot_buf(nm)
                for h in range(w):
                    ins = dve.scalar_tensor_tensor(out=buf[:, tile_cols(h)], in0=psum[:, place[name][0], tile_cols(h)],
                                                   scalar=r[:, h:h + 1], in1=qk_g[:, 0 if c < 2 else 1, :],
                                                   op0=ALU.mult, op1=ALU.mult)
                    if h == w - 1:
                        seq.freed(ins.then_inc(bank_free(name), 1), name)
                    else:
                        seq.note(ins.then_inc(s_v, 1), s_v)
                if t < XT:
                    rope(sc[:, 7, :], (rope_b[:, 0, t, :], rope_b[:, 1, t, :]), w, 64, rot_buf(nm))
                else:
                    seq.note(dve.memset(ss[0:1, 255:256], 0.0).then_inc(s_rot, 1), s_rot)

            for c in range(3):
                run_chunk("in1", c, unit1)

            def max1(p):
                dve.wait_ge(*finished(("s1", p)))
                b = place[("s1", p)][0]
                if p >= 2:
                    dve.wait_ge(*moved(("s1", p - 2)))
                seq.note(dve.tensor_reduce(nmax[:, p % 2, 0:1], psum[:, b, :], AX_X, ALU.max, negate=True).then_inc(s_mx, 1), s_mx)

            def out1(p):
                t, h = divmod(p, HEADS)
                dve.wait_ge(*finished(("pv1", p)))
                seq.freed(dve.tensor_scalar(qT[:, h, tile_cols(t)], psum[:, 7, 0:P], rinv[:, p % 2, 0:1], None,
                                                ALU.mult).then_inc(bank_free(("pv1", p)), 1), ("pv1", p))

            z_units1 = [(c, t) for c in (3, 4) for t in range(XT)]
            dve.wait_ge(*seq.last)
            max1(0)
            for p in range(XT * HEADS):
                if p + 1 < XT * HEADS:
                    max1(p + 1)
                dve.wait_ge(*moved(("s1", p)))
                dve.wait_ge(*seq.last)
                seq.note(dve.reciprocal(rinv[:, p % 2, 0:1], rsum[:, p % 2, 0:1]).then_inc(s_rinv, 1), s_rinv)
                if p:
                    out1(p - 1)
                if p % 4 == 3:
                    c, t = z_units1[p // 4]
                    gate_z(zbuf[:, t, (c - 3) * COLS:(c - 2) * COLS], ("in1", c, t))
                if p == 7:
                    split_through(z_first1 + 3)
                if p == 9:
                    split_through(z_first1 + 4)
            out1(XT * HEADS - 1)
            dve.wait_ge(*seq.last)
            for t in range(XT):
                z = zbuf[:, t, :].rearrange("p (h d) -> p h d", d=P)
                seq.note(dve.scalar_tensor_tensor(out=z, in0=qT[:, :, tile_cols(t)], scalar=0.5, in1=z,
                                                   op0=ALU.mult, op1=ALU.mult).then_inc(s_tok, 1), s_tok)
            split_through(half_no[("out1", 0, 0)] + 1)
            to_feature("turn_o1", XT)
            run_chunk("out1", 0, lambda c, t: None)
            run_chunk("out1", 1, lambda c, t: residual_steps(1, XT, t), before_norm=True)
            residual_steps(1, XT, XT)
            residual_steps(1, XT, XT + 1)
            split_through(half_no[("in2", 0, 0)] + 1)
            norm_lo("norm2")
            split_through(half_no[("in2", 0, 0)] + 2)

            def unit2(c, t):
                name = ("in2", c, t)
                ps = psum[:, place[name][0], :]
                if c == 0:
                    squares(("lat", t))
                    mean_power(("lat", t), ss[:, ss_lat + t:ss_lat + t + 1], 1, 1.0 / P)
                    seq.freed(dve.tensor_scalar(lat[:, t, :], ps[:, 0:P], rs(("lat", t)), None, ALU.mult).then_inc(bank_free(name), 1), name)
                elif c == 1:
                    squares(("qa", t))
                    n0 = 120 + 8 * t
                    seq.note(dve.tensor_reduce(ss[:, n0:n0 + 8], sc[:, 5 + t, :].rearrange("p (h d) -> p h d", d=64),
                                                AX_X, ALU.add).then_inc(s_v, 1), s_v)
                    dve.wait_ge(*seq.last)
                    mean_power(("qa", t), ss[:, n0:n0 + 8], 8, 1.0 / 64)
                    buf = sc[:, 7, :].rearrange("p (h d) -> p h d", d=64)
                    v = ps.rearrange("p (h d) -> p h d", d=64)
                    dve.wait_ge(*seq.last)
                    seq.freed(dve.tensor_tensor(buf, v, rs(("qa", t)).unsqueeze(2).broadcast_to((P, 8, 64)), ALU.mult).then_inc(bank_free(name), 1), name)
                    dve.wait_ge(*seq.last)
                    nm = ("turn_qa", t)
                    rot_free(nm)
                    seq.note(dve.tensor_tensor(rot_buf(nm).rearrange("p (h d) -> p h d", d=64), buf,
                                                qkn2[:, 0, :].unsqueeze(1).broadcast_to((P, 8, 64)), ALU.mult).then_inc(s_rot, 1), s_rot)
                elif c in (2, 3):
                    if c == 2:
                        keys2(t)
                    dve.wait_ge(*finished(name))
                    nm = ("turn_qb" if c == 2 else "turn_kb", t)
                    rot_free(nm)
                    rope(ps, (rope_c[:, 0, t, :], rope_c[:, 1, t, :]), 8, 32, rot_buf(nm), name)
                    if c == 2 and t == 0:
                        index_scores(0)
                    elif c == 2:
                        top(0, 0, 2)
                    elif t == 0:
                        dve.wait_ge(*finished(("bias",)))
                        seq.note(dve.tensor_copy(toep, psum[0:HEADS, place[("bias",)][0], :]).then_inc(s_toep, 1), s_toep)
                        free_bank(("bias",))
                        top(0, 2, 4)
                    else:
                        top(0, 4, 6)
                elif c == 4:
                    if t == 0:
                        top(0, 6, 8)
                        mark(0)
                        index_scores(1)
                    else:
                        top(1, 0, 3)
                else:
                    gate_z(gb[:, t, :], name)
                    if t == 0:
                        top(1, 3, 5)
                    else:
                        top(1, 5, 8)
                        mark(1)

            def keys2(t):
                squares(("ka", t))
                nm = ("latent", t)
                lp = psum[:, place[nm][0], :]
                mean_power(("ka", t), ss[:, ss_ka + t:ss_ka + t + 1], 1, 1.0 / 64)
                dve.wait_ge(*finished(("turn_c", XT - 1)))
                seq.note(dve.tensor_copy(va[:, t, :], lp[:, 64:128]).then_inc(s_v, 1), s_v)
                r = rs(("ka", t))
                seq.note(dve.scalar_tensor_tensor(out=ka2[:, t, 0:64], in0=lp[:, 0:64], scalar=r, in1=qkn2[:, 1, :],
                                                   op0=ALU.mult, op1=ALU.mult).then_inc(s_v, 1), s_v)
                seq.note(dve.scalar_tensor_tensor(out=ka2[:, t, 64:128], in0=lp[:, 0:64], scalar=r, in1=qkn2[:, 1, :],
                                                   op0=ALU.mult, op1=ALU.mult).then_inc(s_ka, 1), s_ka)
                free_bank(nm)

            def index_scores(t):
                acc = score[:, t, :]
                for i in range(4):
                    dve.wait_ge(*moved(("idx", t, i)))
                    r = relus[:, t, i, :]
                    if i:
                        dve.wait_ge(*seq.last)
                        seq.note(dve.scalar_tensor_tensor(out=acc, in0=r, scalar=iw[:, t, i:i + 1], in1=acc,
                                                           op0=ALU.mult, op1=ALU.add).then_inc(s_v, 1), s_v)
                    else:
                        seq.note(dve.tensor_scalar(acc, r, iw[:, t, 0:1], None, ALU.mult).then_inc(s_v, 1), s_v)
                dve.wait_ge(*seq.last)
                for half in range(2):
                    limit = t * P + 64 * (half + 1)
                    if limit < 256:
                        seq.note(dve.memset(score[64 * half:64 * half + 64, t, limit:256], INADMISSIBLE).then_inc(s_v, 1), s_v)

            def top(t, first, last):
                acc = score[:, t, :]
                for _ in range(first, last):
                    dve.wait_ge(*seq.last)
                    seq.note(dve.max(best, acc).then_inc(s_v, 1), s_v)
                    dve.wait_ge(*seq.last)
                    seq.note(dve.match_replace(acc, best, acc, LOWEST).then_inc(s_v, 1), s_v)

            def mark(t):
                dve.wait_ge(*seq.last)
                seq.note(dve.tensor_scalar(taken[:, t, :], score[:, t, ::-1], -3.2e38, INADMISSIBLE,
                                            ALU.is_gt, ALU.mult).then_inc(s_mark, 1), s_mark)

            for c in range(6):
                run_chunk("in2", c, unit2)

            def decayed(h):
                nm = ("ret_s", h)
                dve.wait_ge(*finished(nm))
                if h >= 2:
                    dve.wait_ge(s_yret, h - 1)
                ps = psum[:, place[nm][0], :]
                m = sc[:, 4 + h % 2, :]
                seq.note(dve.tensor_tensor(m[:, 0:256], ps[:, 0:256], decay[:, h, :], ALU.mult).then_inc(s_v, 1), s_v)
                seq.freed(dve.tensor_tensor(m[:, 256:384], ps[:, 256:384], decay[:, h, 0:P], ALU.mult).then_inc(bank_free(nm), 1), nm)

            def centred(t):
                nm = ("ret_y", t)
                dve.wait_ge(*finished(("ret_y", 1)))
                y = psum[:, place[nm][0], :].rearrange("p (h d) -> p h d", d=64)
                yc = sc[:, 4 + t, :].rearrange("p (h d) -> p h d", d=64)
                n0 = 140 + 16 * t
                seq.note(dve.tensor_reduce(ss[:, n0:n0 + 8], y, AX_X, ALU.add).then_inc(s_v, 1), s_v)
                dve.wait_ge(*seq.last)
                seq.note(dve.tensor_scalar(ss[:, n0:n0 + 8], ss[:, n0:n0 + 8], 1.0 / 64, None, ALU.mult).then_inc(s_v, 1), s_v)
                dve.wait_ge(*seq.last)
                seq.note(dve.tensor_tensor(yc, y, ss[:, n0:n0 + 8].unsqueeze(2).broadcast_to((P, 8, 64)), ALU.subtract).then_inc(s_yc, 1), s_yc)
                free_bank(nm)

            dve.wait_ge(s_par2, 16 * 4)

            def max2(p):
                t, hp = divmod(p, 4)
                buf = sc[:, p % 2, :]
                if p >= 2:
                    dve.wait_ge(*finished(("t2", p - 2)))
                if hp == 0:
                    dve.wait_ge(s_masked, t + 1)
                v = buf.rearrange("p (e k) -> p e k", e=2)
                for e in range(2):
                    nm = ("s2", p, e)
                    dve.wait_ge(*finished(nm))
                    seq.freed(dve.tensor_tensor(buf[:, 256 * e:256 * e + 256], psum[:, place[nm][0], 0:256],
                                                biasm[:, t, 2 * hp + e, ::-1], ALU.add).then_inc(bank_free(nm), 1), nm)
                dve.wait_ge(*seq.last)
                seq.note(dve.tensor_reduce(nmax[:, p % 2, :], v, AX_X, ALU.max, negate=True).then_inc(s_mx, 1), s_mx)

            def out2(p):
                t, hp = divmod(p, 4)
                dve.wait_ge(s_ex, p + 1)
                seq.note(dve.reciprocal(rinv[:, p % 2, 0:2], rsum[:, p % 2, :]).then_inc(s_v, 1), s_v)
                dve.wait_ge(*seq.last)
                dve.wait_ge(*finished(("pv2", p)))
                ps = psum[:, 7, 0:P].rearrange("p (e d) -> p e d", e=2)
                dst = mix[:, t, hp * P:(hp + 1) * P].rearrange("p (e d) -> p e d", e=2)
                ins = dve.tensor_tensor(dst, ps, rinv[:, p % 2, 0:2].unsqueeze(2).broadcast_to((P, 2, 64)), ALU.mult)
                if p == 7:
                    seq.note(ins.then_inc(s_tok, 1), s_tok)
                    free_bank(("pv2", p))
                else:
                    seq.freed(ins.then_inc(bank_free(("pv2", p)), 1), ("pv2", p))

            def group_mean(t):
                squares(("gn", t))
                n0 = 140 + 16 * t + 8
                seq.note(dve.tensor_reduce(ss[:, n0:n0 + 8], sc[:, 6 + t, :].rearrange("p (h d) -> p h d", d=64), AX_X, ALU.add).then_inc(s_v, 1), s_v)
                dve.wait_ge(*seq.last)
                mean_power(("gn", t), ss[:, n0:n0 + 8], 8, 1.0 / 64, GN_EPS)

            def group_norm(t):
                yc = sc[:, 4 + t, :].rearrange("p (h d) -> p h d", d=64)
                flat = sc[:, 4 + t, :]
                seq.note(dve.tensor_tensor(yc, yc, rs(("gn", t)).unsqueeze(2).broadcast_to((P, 8, 64)), ALU.mult).then_inc(s_v, 1), s_v)
                dve.wait_ge(*seq.last)
                seq.note(dve.tensor_tensor(flat, flat, gn_wb[:, 0, :], ALU.mult).then_inc(s_v, 1), s_v)
                dve.wait_ge(*seq.last)
                seq.note(dve.tensor_tensor(flat, flat, gn_wb[:, 1, :], ALU.add).then_inc(s_v, 1), s_v)
                dve.wait_ge(*seq.last)
                done = s_v if t else s_tok
                seq.note(dve.scalar_tensor_tensor(out=mix[:, t, 512:1024], in0=flat, scalar=0.5, in1=gb[:, t, :],
                                                   op0=ALU.mult, op1=ALU.mult).then_inc(done, 1), done)

            max2(0)
            for p in range(8):
                if p + 1 < 8:
                    max2(p + 1)
                for h in (2 * p, 2 * p + 1):
                    if h < HEADS:
                        decayed(h)
                if p == 5:
                    group_mean(0)
                    group_mean(1)
                elif p > 5:
                    group_norm(p - 6)
                out2(p)
                if p == 3:
                    centred(0)
                    centred(1)
            to_feature("turn_o2", XT)

            def add_out(c, t):
                nm = ("out2", c, t)
                dve.wait_ge(*finished(nm))
                v = xs[:, t, c * COLS:(c + 1) * COLS]
                seq.freed(dve.tensor_tensor(v, v, psum[:, place[nm][0], :], ALU.add).then_inc(bank_free(nm), 1), nm)

            run_chunk("out2", 0, add_out)
            add_out(1, 0)
            norm_mean("norm3", 0)
            add_out(1, 1)
            normed("norm3", 0)
            norm_mean("norm3", 1)
            normed("norm3", 1)
            split_through(half_no[("gu", 0, 1)])
            norm_lo("norm3")
            split_through(half_no[("gu", 0, 1)] + 1)

            def gate_up(j, t):
                nm = ("gu", j, t)
                dve.wait_ge(s_tanh, n_tanh[0] + 1)
                n_tanh[0] += 1
                th, hid = sc[:, t, 0:256], sc[:, 4 + 2 * (j % 2) + t, 0:256]
                seq.note(dve.scalar_tensor_tensor(out=sc[:, 2 + t, 0:256], in0=th, scalar=1.0, in1=psum[:, 4 + t, 0:256],
                                                   op0=ALU.add, op1=ALU.mult).then_inc(s_v, 1), s_v)
                dve.wait_ge(*seq.last)
                if j >= 2:
                    dve.wait_ge(*finished(("turn_h", j - 2, t)))
                seq.freed(dve.scalar_tensor_tensor(out=hid, in0=sc[:, 2 + t, 0:256], scalar=0.5,
                                                       in1=psum[:, 4 + t, 256:512], op0=ALU.mult, op1=ALU.mult).then_inc(bank_free(nm), 1), nm)

            def hidden_lo(j):
                for t in range(XT):
                    dve.wait_ge(s_h, h_base["hidden"] + 2 * j + t + 1)
                    ps = psum[:, 6 + t, 0:256].rearrange("p (k n) -> p k n", k=2)
                    k = 2 * (j % 2)
                    hi = act_hi[:, k:k + 2, tile_cols(XT + t)].bitcast(F32)
                    seq.freed(dve.tensor_tensor(act_lo[:, k:k + 2, tile_cols(XT + t)], ps, hi, ALU.subtract).then_inc(bank_free(("turn_h", j, t)), 1), ("turn_h", j, t))

            for j in range(FFN_STEPS):
                gate_up(j, 0)
                if j:
                    hidden_lo(j - 1)
                split_through(half_no.get(("gu", j + 1, 0), 0))
                gate_up(j, 1)
                split_through(half_no.get(("gu", j + 1, 1), 0))
                split_through(half_no[("down", j, 0)])
            hidden_lo(FFN_STEPS - 1)
            for t in range(XT):
                for c in range(2):
                    nm = ("down", t, c)
                    dve.wait_ge(*finished(nm))
                    v = xs[:, t, c * COLS:(c + 1) * COLS]
                    seq.note(dve.tensor_tensor(v, v, psum[:, place[nm][0], :], ALU.add).then_inc(s_outr, 1), s_outr)


def _constants():
    import numpy as np

    f = np.float32
    k = {"k_ident": np.eye(P, dtype=f)}
    sel = np.zeros((P, 2, P), f)
    for s in range(2):
        sel[32 * s, s, :] = 1.0
        sel[64 + 32 * s, s, :] = 1.0
    k["k_sel"] = sel
    tok = np.arange(XT * P)
    rows, cols = tok // 64, tok % 64

    def axial(head_dim):
        ax = head_dim // 2
        fr = (f(10000.0) ** (-np.arange(0, ax, 2, dtype=f) / f(ax))).astype(f)
        ang = np.concatenate([rows.astype(f)[:, None] * fr, cols.astype(f)[:, None] * fr], axis=-1).astype(f)
        return ang

    half = 32
    inv = (f(10000.0) ** (-np.arange(half, dtype=f) / f(half))).astype(f)
    for name, ang in (("k_rope_a", axial(64)), ("k_rope_b", axial(128)), ("k_rope_c", tok.astype(f)[:, None] * inv)):
        t = np.stack([np.cos(ang), np.sin(ang)]).astype(f)
        k[name] = np.ascontiguousarray(t.reshape(2, XT, P, -1).transpose(2, 0, 1, 3))
    j = np.arange(P)[:, None, None].astype(np.float64)
    i = np.arange(2 * P)[None, None, :].astype(np.float64)
    g = 1.0 - 2.0 ** (-5.0 - np.arange(HEADS))[None, :, None]
    k["k_decay"] = np.where(i >= j, g ** np.maximum(i - j, 0.0), 0.0).astype(f)
    rel = 255 - np.arange(COLS)
    n = np.abs(rel)
    large = 8 + (np.log(np.maximum(n, 1).astype(f) / f(8)) / f(math.log(16.0)) * f(8)).astype(np.int32)
    bucket = np.where(rel > 0, 16, 0) + np.where(n < 8, n, np.minimum(large, 15))
    onehot = np.zeros((32, COLS), f)
    onehot[bucket, np.arange(COLS)] = 1.0
    k["k_onehot"] = onehot
    return k


_INS = ["x", "c", "ctx", "c_ctx", "ada_w", "ada_b", "pre_g", "post_g", "w_out", "a_w_in", "a_lambda", "a_subln_g",
        "b_w_in", "b_qk_g", "norm1_w_2", "w_in_2", "q_norm_w_2", "k_norm_w_2", "kv_norm_w_2", "w_uk_2", "w_uv_2",
        "rel_bias_2", "ret_gn_w_2", "ret_gn_b_2", "w_out_2", "norm2_w_2", "w_gate_2", "w_up_2", "w_down_2"]


def kernel(**inputs):
    import numpy as _np
    import concourse.bacc as _bacc
    from concourse.bass_utils import run_bass_kernel_spmd as _run

    nc = _bacc.Bacc("TRN2", target_bir_lowering=False, num_devices=1, dynamic_dma_scratch_size=1024)
    arrays, args = {}, {}
    for name in _INS:
        arrays[f"in_{name}"] = _np.ascontiguousarray(inputs[name])
    for name, v in _constants().items():
        arrays[f"in_{name}"] = v
    for key, v in arrays.items():
        args[key[3:]] = nc.dram_tensor(key, v.shape, mybir.dt.from_np(v.dtype), kind="ExternalInput").ap()
    out = nc.dram_tensor("out_0", (1, XT * P, D), F32, kind="ExternalOutput").ap()
    block_kernel(nc, args, out)
    r = _run(nc, [arrays], core_ids=[0])
    return r.results[0]["out_0"]
```
